# Optimizing a Trainium2 kernel written in Bass

```python
import math
import jax
import jax.numpy as jnp
from jax import lax
import numpy as np

D_MODEL = 1024
BATCH = 1
SEQ = 1024
DEPTH = 1
DEC_BATCH = 8
DEC_SEQ = 8
PAST_LEN = 1024
PAGE_SIZE = 128

MIX_W = D_MODEL
ATTN_W = MIX_W // 2
POOL_W = MIX_W - ATTN_W
HEAD_DIM = 64
N_HEADS = ATTN_W // HEAD_DIM
N_KV_HEADS = 2
HEADS_PER_KV = N_HEADS // N_KV_HEADS
SCALE = HEAD_DIM ** -0.5
ROT_DIM = HEAD_DIM // 4
ROPE_THETA = 500000.0
CMP_LEN = 32
CMP_STRIDE = 16
CMP_HID = HEAD_DIM
SEL_BLOCK = 64
SEL_TOPN = 16
WINDOW = 512
Q_BLOCK = 128
FORCE_BONUS = 1000.0
POOL_WINDOWS = (2, 4, 8, 16)
N_POOL_GROUPS = len(POOL_WINDOWS)
POOL_CH = POOL_W // N_POOL_GROUPS
POOL_HIST = max(POOL_WINDOWS) - 1
N_MEM = 256
MEM_HEADS = 4
MEM_HEAD_DIM = 128
MEM_W = MEM_HEADS * MEM_HEAD_DIM
D_FF = 4 * D_MODEL
EPS = 1e-6
KV_W = 2 * N_KV_HEADS * HEAD_DIM
IN_SPLITS = (ATTN_W, ATTN_W + KV_W, ATTN_W + 2 * KV_W, ATTN_W + 3 * KV_W, ATTN_W + 3 * KV_W + 3 * N_HEADS)
N_IN = ATTN_W + 3 * KV_W + 3 * N_HEADS + POOL_W

kernel_name = 'nsa_pool_hybrid_decode_step'

def rms_norm(x, g):
    xf = x.astype(jnp.float32)
    y = xf * lax.rsqrt(jnp.mean(xf * xf, axis=-1, keepdims=True) + EPS)
    return (y * g.astype(jnp.float32)).astype(x.dtype)

def rope(x, pos):
    half = ROT_DIM // 2
    inv = ROPE_THETA ** (-jnp.arange(half, dtype=jnp.float32) / half)
    ang = pos.astype(jnp.float32)[:, None] * inv[None, :]
    cos = jnp.cos(ang)[None, :, None, :]
    sin = jnp.sin(ang)[None, :, None, :]
    xf = x.astype(jnp.float32)
    x1, x2, rest = xf[..., :half], xf[..., half:ROT_DIM], xf[..., ROT_DIM:]
    return jnp.concatenate([x1 * cos - x2 * sin, x2 * cos + x1 * sin, rest], axis=-1).astype(x.dtype)

def masked_softmax(s, mask):
    s = jnp.where(mask, s.astype(jnp.float32), -1e30)
    m = jnp.max(s, axis=-1, keepdims=True)
    e = jnp.where(mask, jnp.exp(s - m), 0.0)
    return e / jnp.maximum(jnp.sum(e, axis=-1, keepdims=True), 1e-30)

def project(xn, w_in, pos):
    B, T, _ = xn.shape
    q, kc, ks, kw, gl, pool_in = jnp.split(xn @ w_in, IN_SPLITS, axis=-1)
    q = q.reshape(B, T, N_HEADS, HEAD_DIM)

    def kv(a, rotate):
        a = a.reshape(B, T, 2, N_KV_HEADS, HEAD_DIM)
        if not rotate:
            return a
        return jnp.stack([rope(a[:, :, 0], pos), a[:, :, 1]], axis=2)

    gates = jax.nn.sigmoid(gl.reshape(B, T, N_HEADS, 3).astype(jnp.float32)).astype(xn.dtype)
    return q, rope(q, pos), kv(kc, False), kv(ks, True), kv(kw, True), gates, pool_in

def compress(kv, pe, w1, w2):
    B, L = kv.shape[:2]
    R = CMP_LEN // CMP_STRIDE
    nch = L // CMP_STRIDE
    n_cmp = nch - R + 1
    ch = kv[:, :nch * CMP_STRIDE].reshape(B, nch, CMP_STRIDE, 2, N_KV_HEADS, HEAD_DIM)
    w1b = w1.reshape(2, CMP_LEN, HEAD_DIM, CMP_HID)
    w1r = w1.reshape(2, R, CMP_STRIDE, HEAD_DIM, CMP_HID)
    h = jnp.einsum('cld,cldh->ch', pe, w1b)[None, None, :, None, :]
    for r in range(R):
        u = jnp.einsum('bnscgd,csdh->bncgh', ch, w1r[:, r])
        h = h + u[:, r:r + n_cmp]
    out = jnp.einsum('bncgh,chd->bncgd', jax.nn.gelu(h), w2)
    return out[:, :, 0], out[:, :, 1]

def cat_blocks(parts):
    a = parts[0]
    L = sum(pt.shape[1] for pt in parts)
    n_sel = -(-L // SEL_BLOCK)
    pad = jnp.zeros((a.shape[0], n_sel * SEL_BLOCK - L) + a.shape[2:], a.dtype)
    full = jnp.concatenate(list(parts) + [pad], axis=1)
    return full.reshape((a.shape[0], n_sel, SEL_BLOCK) + a.shape[2:])

def nsa_attention(q, qr, gates, pos_base, cmp_full, sel_blk, win_ext, win_pos0, p):
    B, T = q.shape[:2]
    dt = q.dtype
    ck, cv = compress(cmp_full, p['pe_cmp'], p['w_cmp1'], p['w_cmp2'])
    n_cmp = ck.shape[1]
    n_sel = sel_blk.shape[1]
    k_top = min(SEL_TOPN, n_sel)
    ci = jnp.arange(n_cmp)[:, None] * CMP_STRIDE
    sj = jnp.arange(n_sel)[None, :] * SEL_BLOCK
    overlap = jnp.maximum(jnp.minimum(ci + CMP_LEN, sj + SEL_BLOCK) - jnp.maximum(ci, sj), 0).astype(jnp.float32) / CMP_LEN
    cmp_end = jnp.arange(n_cmp) * CMP_STRIDE + CMP_LEN - 1
    blk_ids = jnp.arange(n_sel)
    qb = math.gcd(T, Q_BLOCK)
    b_idx = jnp.arange(B)[:, None, None, None]
    g_idx = jnp.arange(N_KV_HEADS)[None, None, :, None]
    m_sel = k_top * SEL_BLOCK

    def grp(a):
        return a.reshape((B, qb, N_KV_HEADS, HEADS_PER_KV) + a.shape[3:])

    def block(q0):
        pos = pos_base + q0 + jnp.arange(qb)
        qc = grp(lax.dynamic_slice_in_dim(q, q0, qb, 1))
        qs = grp(lax.dynamic_slice_in_dim(qr, q0, qb, 1))
        g = grp(lax.dynamic_slice_in_dim(gates, q0, qb, 1))
        s = jnp.einsum('bqghd,bngd->bqghn', qc, ck) * SCALE
        p_c = masked_softmax(s, (cmp_end[None, :] <= pos[:, None])[None, :, None, None, :])
        o_c = jnp.einsum('bqghn,bngd->bqghd', p_c.astype(dt), cv)
        imp = jnp.einsum('bqgn,nj->bqgj', p_c.sum(axis=3), overlap)
        cur = (pos // SEL_BLOCK)[:, None]
        valid = (blk_ids[None, :] * SEL_BLOCK <= pos[:, None])[None, :, None, :]
        forced = ((blk_ids[None, :] == 0) | (blk_ids[None, :] == cur) | (blk_ids[None, :] == cur - 1))[None, :, None, :]
        score = jnp.where(valid, imp + jnp.where(forced, FORCE_BONUS, 0.0), -1e9)
        _, idx = lax.top_k(score, k_top)
        kv_s = sel_blk[b_idx, idx, :, :, g_idx]
        kpos = (idx[..., None] * SEL_BLOCK + jnp.arange(SEL_BLOCK)).reshape(B, qb, N_KV_HEADS, 1, m_sel)
        s = jnp.einsum('bqghd,bqgkld->bqghkl', qs, kv_s[..., 0, :]) * SCALE
        p_s = masked_softmax(s.reshape(B, qb, N_KV_HEADS, HEADS_PER_KV, m_sel), kpos <= pos[None, :, None, None, None])
        o_s = jnp.einsum('bqghm,bqgmd->bqghd', p_s.astype(dt), kv_s[..., 1, :].reshape(B, qb, N_KV_HEADS, m_sel, HEAD_DIM))
        kw = lax.dynamic_slice_in_dim(win_ext, q0, WINDOW + qb, 1)
        kp = win_pos0 + q0 + jnp.arange(WINDOW + qb)
        wm = (kp[None, :] <= pos[:, None]) & (kp[None, :] >= pos[:, None] - WINDOW) & (kp[None, :] >= 0)
        s = jnp.einsum('bqghd,bkgd->bqghk', qs, kw[:, :, 0]) * SCALE
        p_w = masked_softmax(s, wm[None, :, None, None, :])
        o_w = jnp.einsum('bqghk,bkgd->bqghd', p_w.astype(dt), kw[:, :, 1])
        o = g[..., 0:1] * o_c + g[..., 1:2] * o_s + g[..., 2:3] * o_w
        return o.reshape(B, qb, N_HEADS, HEAD_DIM)

    out = lax.map(block, jnp.arange(T // qb) * qb)
    return jnp.moveaxis(out, 0, 1).reshape(B, T, ATTN_W)

def pool_mix(ext, pos_base, w_pool):
    B, Lx, _ = ext.shape
    T = Lx - POOL_HIST
    xf = ext.astype(jnp.float32)
    cs = jnp.concatenate([jnp.zeros((B, 1, POOL_W), jnp.float32), jnp.cumsum(xf, axis=1)], axis=1)
    hi = cs[:, POOL_HIST + 1:]
    pos = pos_base + jnp.arange(T)
    means = []
    for gi, w in enumerate(POOL_WINDOWS):
        c = slice(gi * POOL_CH, (gi + 1) * POOL_CH)
        lo = cs[:, POOL_HIST + 1 - w:POOL_HIST + 1 - w + T, c]
        cnt = jnp.minimum(pos + 1, w).astype(jnp.float32)[None, :, None]
        means.append((hi[:, :, c] - lo) / cnt)
    d = (jnp.concatenate(means, axis=-1) - xf[:, POOL_HIST:]).astype(ext.dtype)
    d = d.reshape(B, T, N_POOL_GROUPS, POOL_CH)
    return jnp.einsum('btgc,gcd->btgd', d, w_pool).reshape(B, T, POOL_W)

def cross_attend(xn, mem_kv, w_mq, w_mo):
    B, T, _ = xn.shape
    q = (xn @ w_mq).reshape(B, T, MEM_HEADS, MEM_HEAD_DIM)
    s = jnp.einsum('bthd,bmhd->bhtm', q, mem_kv[:, :, 0]).astype(jnp.float32) * (MEM_HEAD_DIM ** -0.5)
    pr = jax.nn.softmax(s, axis=-1).astype(xn.dtype)
    o = jnp.einsum('bhtm,bmhd->bthd', pr, mem_kv[:, :, 1]).reshape(B, T, MEM_W)
    return o @ w_mo

def layer_tail(x, q, qr, gates, cmp_full, sel_blk, win_ext, win_pos0, pool_ext, mem_kv, pos_base, p):
    a = nsa_attention(q, qr, gates, pos_base, cmp_full, sel_blk, win_ext, win_pos0, p)
    m = pool_mix(pool_ext, pos_base, p['w_pool'])
    mix = jnp.concatenate([rms_norm(a, p['g_attn_out']), rms_norm(m, p['pool_scale'])], axis=-1)
    x = x + mix @ p['w_out']
    x = x + cross_attend(rms_norm(x, p['g_norm2']), mem_kv, p['w_mq'], p['w_mo'])
    h = jax.nn.relu(rms_norm(x, p['g_norm3']) @ p['w_up'])
    return x + (h * h) @ p['w_down']

def prompt_layer(x, mem, p):
    B, S, _ = x.shape
    pos = jnp.arange(S)
    q, qr, cmp_kv, sel_kv, win_kv, gates, pool_in = project(rms_norm(x, p['g_norm1']), p['w_in'], pos)
    win_ext = jnp.concatenate([jnp.zeros((B, WINDOW) + win_kv.shape[2:], win_kv.dtype), win_kv], axis=1)
    pool_ext = jnp.concatenate([jnp.zeros((B, POOL_HIST, POOL_W), pool_in.dtype), pool_in], axis=1)
    mem_kv = (rms_norm(mem, p['g_mem']) @ p['w_mkv']).reshape(B, N_MEM, 2, MEM_HEADS, MEM_HEAD_DIM)
    y = layer_tail(x, q, qr, gates, cmp_kv, cat_blocks([sel_kv]), win_ext, -WINDOW, pool_ext, mem_kv, 0, p)
    state = (cmp_kv, sel_kv, win_kv[:, -min(WINDOW, S):], pool_ext[:, -POOL_HIST:], mem_kv)
    return y, state

def sample_layer(x, cache_cmp, cache_sel, cache_win, st_pool, mem_kv, page_table, p):
    DB, T, _ = x.shape
    past = page_table.shape[1] * PAGE_SIZE
    pos = past + jnp.arange(T)
    q, qr, cmp_kv, sel_kv, win_kv, gates, pool_in = project(rms_norm(x, p['g_norm1']), p['w_in'], pos)

    def gather(pool):
        return pool[page_table].reshape((DB, past) + pool.shape[2:])

    cmp_full = jnp.concatenate([gather(cache_cmp), cmp_kv], axis=1)
    sel_blk = cat_blocks([gather(cache_sel), sel_kv])
    wb = cache_win.shape[1]
    win_ext = jnp.concatenate([jnp.zeros((DB, WINDOW - wb) + win_kv.shape[2:], win_kv.dtype), cache_win, win_kv], axis=1)
    pool_ext = jnp.concatenate([st_pool, pool_in], axis=1)
    y = layer_tail(x, q, qr, gates, cmp_full, sel_blk, win_ext, past - WINDOW, pool_ext, mem_kv, past, p)
    state = (cmp_kv, sel_kv, win_ext[:, -min(WINDOW, wb + T):], pool_ext[:, -POOL_HIST:])
    return y, state

def setup_inputs(seed: int = 0) -> dict:
    key = jax.random.key(seed)
    k = jax.random.split(key, 32)
    n_pages = PAST_LEN // PAGE_SIZE
    n_used = DEC_BATCH * n_pages
    n_phys = n_used + (n_used + 3) // 4
    wb = min(WINDOW, PAST_LEN)

    def nrm(kk, shape, scale=1.0):
        return jax.random.normal(kk, shape, jnp.float32) * scale

    def gain(kk, shape):
        return 1.0 + 0.05 * jax.random.normal(kk, shape, jnp.float32)

    kv_page = (DEPTH, n_phys, PAGE_SIZE, 2, N_KV_HEADS, HEAD_DIM)
    page_table = jax.random.permutation(k[7], n_phys)[:n_used].reshape(DEC_BATCH, n_pages).astype(jnp.int32)
    return {
        'x_prompt': nrm(k[0], (BATCH, SEQ, D_MODEL)),
        'x_sample': nrm(k[1], (DEC_BATCH, DEC_SEQ, D_MODEL)),
        'cache_cmp_kv': nrm(k[2], kv_page),
        'cache_sel_kv': nrm(k[3], kv_page),
        'cache_win_kv': nrm(k[4], (DEPTH, DEC_BATCH, wb, 2, N_KV_HEADS, HEAD_DIM)),
        'state_pool': nrm(k[5], (DEPTH, DEC_BATCH, POOL_HIST, POOL_W)),
        'cache_mem_kv': nrm(k[6], (DEPTH, DEC_BATCH, N_MEM, 2, MEM_HEADS, MEM_HEAD_DIM)),
        'page_table': page_table,
        'mem_prompt': nrm(k[8], (BATCH, N_MEM, D_MODEL)),
        'w_in': nrm(k[9], (DEPTH, D_MODEL, N_IN), D_MODEL ** -0.5),
        'pe_cmp': nrm(k[10], (DEPTH, 2, CMP_LEN, HEAD_DIM), 0.1),
        'w_cmp1': nrm(k[11], (DEPTH, 2, CMP_LEN * HEAD_DIM, CMP_HID), (CMP_LEN * HEAD_DIM) ** -0.5),
        'w_cmp2': nrm(k[12], (DEPTH, 2, CMP_HID, HEAD_DIM), CMP_HID ** -0.5),
        'w_pool': nrm(k[13], (DEPTH, N_POOL_GROUPS, POOL_CH, POOL_CH), POOL_CH ** -0.5),
        'g_attn_out': gain(k[14], (DEPTH, ATTN_W)),
        'pool_scale': gain(k[15], (DEPTH, POOL_W)),
        'w_out': nrm(k[16], (DEPTH, MIX_W, D_MODEL), MIX_W ** -0.5),
        'g_norm1': gain(k[17], (DEPTH, D_MODEL)),
        'g_norm2': gain(k[18], (DEPTH, D_MODEL)),
        'g_mem': gain(k[19], (DEPTH, D_MODEL)),
        'w_mq': nrm(k[20], (DEPTH, D_MODEL, MEM_W), D_MODEL ** -0.5),
        'w_mkv': nrm(k[21], (DEPTH, D_MODEL, 2 * MEM_W), D_MODEL ** -0.5),
        'w_mo': nrm(k[22], (DEPTH, MEM_W, D_MODEL), MEM_W ** -0.5),
        'g_norm3': gain(k[23], (DEPTH, D_MODEL)),
        'w_up': nrm(k[24], (DEPTH, D_MODEL, D_FF), D_MODEL ** -0.5),
        'w_down': nrm(k[25], (DEPTH, D_FF, D_MODEL), D_FF ** -0.5),
        'g_final': gain(k[26], (D_MODEL,)),
    }

def reference(x_prompt, x_sample, cache_cmp_kv, cache_sel_kv, cache_win_kv, state_pool, cache_mem_kv, page_table, mem_prompt, w_in, pe_cmp, w_cmp1, w_cmp2, w_pool, g_attn_out, pool_scale, w_out, g_norm1, g_norm2, g_mem, w_mq, w_mkv, w_mo, g_norm3, w_up, w_down, g_final):
    yp, ys = x_prompt, x_sample
    st_p, st_s = [], []
    for l in range(DEPTH):
        p = {'w_in': w_in[l], 'pe_cmp': pe_cmp[l], 'w_cmp1': w_cmp1[l], 'w_cmp2': w_cmp2[l],
             'w_pool': w_pool[l], 'g_attn_out': g_attn_out[l], 'pool_scale': pool_scale[l],
             'w_out': w_out[l], 'g_norm1': g_norm1[l], 'g_norm2': g_norm2[l], 'g_mem': g_mem[l],
             'w_mq': w_mq[l], 'w_mkv': w_mkv[l], 'w_mo': w_mo[l], 'g_norm3': g_norm3[l],
             'w_up': w_up[l], 'w_down': w_down[l]}
        yp, sp = prompt_layer(yp, mem_prompt, p)
        ys, ss = sample_layer(ys, cache_cmp_kv[l], cache_sel_kv[l], cache_win_kv[l], state_pool[l], cache_mem_kv[l], page_table, p)
        st_p.append(sp)
        st_s.append(ss)
    return (rms_norm(yp, g_final), rms_norm(ys, g_final),
            jnp.stack([s[0] for s in st_p]), jnp.stack([s[1] for s in st_p]), jnp.stack([s[2] for s in st_p]),
            jnp.stack([s[3] for s in st_p]), jnp.stack([s[4] for s in st_p]),
            jnp.stack([s[0] for s in st_s]), jnp.stack([s[1] for s in st_s]), jnp.stack([s[2] for s in st_s]),
            jnp.stack([s[3] for s in st_s]))


_drawn_inputs = setup_inputs


def setup_inputs(seed=0):
    import zlib

    import numpy as np

    out = dict(_drawn_inputs(seed))
    spreads = {}
    factors = {'g_norm2': 8.0}
    for name, (base, spread) in spreads.items():
        noise = np.random.default_rng([zlib.crc32(name.encode()), seed]).standard_normal(out[name].shape)
        drawn = base * np.exp(spread * noise) if base else spread * noise
        out[name] = jnp.asarray(drawn.astype(out[name].dtype))
    for name, factor in factors.items():
        out[name] = (out[name] * factor).astype(out[name].dtype)
    return out
```

```python
from contextlib import ExitStack

import numpy as np
import concourse.bass as bass
from concourse import mybir

F32 = mybir.dt.float32
F32R = mybir.dt.float32r
I32 = mybir.dt.int32
ALU = mybir.AluOpType
ACT = mybir.ActivationFunctionType
AX = mybir.AxisListType

P = 128
DM = 1024
SEQ = 1024
DB, DT = 8, 8
PAST = 1024
PAGE = 128
AW = 512
NH, NG, HPG, HD = 8, 2, 4, 64
KVW = 2 * NG * HD
C_Q, C_KC, C_KS, C_KW, C_GL, C_PI, C_END = 0, 512, 768, 1024, 1280, 1304, 1816
SCALE = HD ** -0.5
ROT = HD // 4
HALF = ROT // 2
WIN = 512
STRIDE, CLEN = 16, 32
NCH = SEQ // STRIDE
NCMP = NCH - 1
SELB = 64
NMEM, MH, MD = 256, 4, 128
DFF = 4096
PW = 512
HIST = 15
EPS = 1e-6
NT = SEQ // P + 1
KC = DM // P
NEG = -1e30
TOK = SEQ + DB * DT


def rows_of(i):
    return P if i < NT - 1 else DB * DT


class Phase:

    def __init__(self, nc, ctx, tag):
        self.nc, self.ctx, self.tag, self.sems = nc, ctx, tag, []
        ctx.callback(self.release)

    def sb(self, name, shape, dt=F32, side=None):
        return self.ctx.enter_context(self.nc.sbuf_tensor(f"{self.tag}_{name}", shape, dt, side=side))

    def ps(self, name, shape):
        return self.ctx.enter_context(self.nc.psum_tensor(f"{self.tag}_{name}", shape, F32))

    def sem(self, name):
        s = self.nc.alloc_semaphore(f"{self.tag}_{name}")
        self.sems.append(s)
        return s

    def release(self):
        if self.sems:
            self.nc.clear_and_free_semaphores(self.sems)
            self.nc.all_engine_barrier()


class Chain:

    def __init__(self, eng, sem):
        self.eng, self.sem, self.n = eng, sem, 0

    def __call__(self, ins):
        self.n += 1
        ins.then_inc(self.sem, 1)
        self.eng.wait_ge(self.sem, self.n)


def project(nc, tag, tiles, x_of, gain, weight, width, y, store, s_st, t, rope=None):
    n_grp = -(-width // 512)
    step = -(-width // n_grp // 4) * 4
    groups = [(a, min(a + step, width)) for a in range(0, width, step)]
    RAW = 4
    with ExitStack() as ctx:
        ph = Phase(nc, ctx, tag)
        w_raw = ph.sb("w_raw", [P, RAW, width])
        w_hi = ph.sb("w_hi", [P, KC, width], F32R)
        w_lo = ph.sb("w_lo", [P, KC, width], F32R)
        x_t = ph.sb("x_t", [P, 2, DM])
        junk = ph.sb("junk", [P, DM])
        xT_hi = ph.sb("xT_hi", [P, 2, KC, P], F32R)
        xT_lo = ph.sb("xT_lo", [P, 2, KC, P], F32R)
        gT = ph.sb("gT", [P, KC])
        stat = ph.sb("stat", [P, 4, NT])
        ident = ph.sb("ident", [P, P])
        acc = [[ph.ps(f"acc{b}{g}", [P, 512]) for g in range(len(groups))] for b in range(2)]
        psT = [ph.ps(f"psT{h}", [P, 4, P]) for h in range(2)]
        if rope:
            q_rot, cs = rope
            t4 = ph.sb("t4", [P, 4, NH, HALF])
        s_w = [ph.sem(f"weight_slot{k}_loaded") for k in range(RAW)]
        s_g = ph.sem("gain_loaded")
        s_x = [ph.sem("x_loaded_even"), ph.sem("x_loaded_odd")]
        s_c = ph.sem("constants_loaded")
        s_cs = ph.sem("rope_table_loaded")
        s_hi = ph.sem("weight_hi_made")
        s_lo = ph.sem("weight_lo_made")
        s_sum = ph.sem("squares_summed")
        s_ms = ph.sem("mean_square_made")
        s_sd = ph.sem("root_taken")
        s_xn = ph.sem("x_scaled")
        s_tr = ph.sem("x_transposed")
        s_th = ph.sem("xT_hi_made")
        s_tl = ph.sem("xT_lo_made")
        s_mm = ph.sem("group_multiplied")
        s_yv = ph.sem("y_copied_by_vector")
        s_ya = ph.sem("y_copied_by_scalar")
        s_rope = ph.sem("keys_rotated")
        s_dve = ph.sem("vector_chain")
        ng = len(groups)
        n_v, n_a = -(-ng // 2), ng // 2
        n = len(tiles)
        with nc.Block() as block:

            @block.sync
            def _(sp):
                for c in range(KC):
                    if c >= RAW:
                        sp.wait_ge(s_lo, c - RAW + 1)
                    sp.dma_start(w_raw[:, c % RAW, :], weight[c * P:(c + 1) * P, :]).then_inc(s_w[c % RAW], 16)
                started = 0
                for j, i in enumerate(tiles):
                    sp.wait_ge(s_yv, n_v * (j + 1))
                    if n_a:
                        sp.wait_ge(s_ya, n_a * (j + 1))
                    if rope:
                        sp.wait_ge(s_rope, j + 1)
                    started += store(sp, s_st, i)
                if started:
                    sp.wait_ge(s_st, 16 * started)

            @block.gpsimd
            def _(pool):
                def load_x(j):
                    i = tiles[j]
                    pool.dma_start(x_t[0:rows_of(i), j % 2, :], x_of(i)).then_inc(s_x[j % 2], 16)

                load_x(0)
                pool.dma_start(gT[:, :], gain.rearrange("(c p) -> p c", p=P),
                               allow_slow_non_contiguous=True).then_inc(s_g, 16)
                pool.dma_start(ident[:, :], t["k_ident"]).then_inc(s_c, 16)
                if rope:
                    pool.dma_start(cs[:, :, :], t["k_rope"]).then_inc(s_cs, 16)
                for j in range(1, n):
                    if j >= 2:
                        pool.wait_ge(s_tr, 2 * (j - 1))
                    load_x(j)

            @block.scalar
            def _(act):
                def square_sum(j):
                    r = rows_of(tiles[j])
                    act.wait_ge(s_x[j % 2], 16 * (j // 2 + 1))
                    if j:
                        act.wait_ge(s_sum, j)
                    nc.scalar.activation(junk[0:r, :], x_t[0:r, j % 2, :], ACT.Square,
                                         accum_out=stat[0:r, 0, j:j + 1]).then_inc(s_sum, 1)
                    act.wait_ge(s_ms, j + 1)
                    nc.scalar.activation(stat[0:r, 2, j:j + 1], stat[0:r, 1, j:j + 1], ACT.Sqrt).then_inc(s_sd, 1)

                def hi(j):
                    r = rows_of(tiles[j])
                    for h in range(2):
                        act.wait_ge(s_tr, 2 * j + h + 1)
                        if j >= 2:
                            act.wait_ge(s_mm, ng * (j - 1))
                        nc.scalar.copy(xT_hi[:, j % 2, 4 * h:4 * h + 4, 0:r], psT[h][:, :, 0:r]).then_inc(s_th, 1)

                square_sum(0)
                if n > 1:
                    square_sum(1)
                hi(0)
                act.wait_ge(s_g, 16)
                for c in range(KC):
                    act.wait_ge(s_w[c % RAW], 16 * (c // RAW + 1))
                    nc.scalar.mul(w_hi[:, c, :], w_raw[:, c % RAW, :], gT[:, c:c + 1]).then_inc(s_hi, 1)
                for j, i in enumerate(tiles):
                    r = rows_of(i)
                    if j + 1 < n:
                        hi(j + 1)
                    if j + 2 < n:
                        square_sum(j + 2)
                    for g, (a, b) in enumerate(groups):
                        if g % 2 == 1:
                            act.wait_ge(s_mm, ng * j + g + 1)
                            nc.scalar.copy(y[0:r, i, a:b], acc[j % 2][g][0:r, 0:b - a]).then_inc(s_ya, 1)

            @block.vector
            def _(dve):
                chain = Chain(dve, s_dve)

                def scale_x(j):
                    r = rows_of(tiles[j])
                    dve.wait_ge(s_sum, j + 1)
                    nc.vector.tensor_scalar(stat[0:r, 1, j:j + 1], stat[0:r, 0, j:j + 1], 1.0 / DM, EPS,
                                            ALU.mult, ALU.add).then_inc(s_ms, 1)
                    dve.wait_ge(s_sd, j + 1)
                    chain(nc.vector.reciprocal(stat[0:r, 3, j:j + 1], stat[0:r, 2, j:j + 1]))
                    nc.vector.tensor_scalar(x_t[0:r, j % 2, :], x_t[0:r, j % 2, :], stat[0:r, 3, j:j + 1], None,
                                            ALU.mult).then_inc(s_xn, 1)

                def rotate(chain, j, i, r):
                    q = y[0:r, i, C_Q:C_Q + AW].rearrange("p (h d) -> p h d", d=HD)
                    k = y[0:r, i, C_KS:C_KS + 2 * KVW].rearrange("p (b u g d) -> p b u g d", b=2, u=2, g=NG)[:, :, 0]
                    for part in range(2):
                        if part == 0:
                            x1, x2 = q[:, :, 0:HALF], q[:, :, HALF:ROT]
                            o1, o2 = q_rot[0:r, i, :, 0:HALF], q_rot[0:r, i, :, HALF:ROT]
                            shape, tt = [r, NH, HALF], [t4[0:r, m, :, :] for m in range(4)]
                            cos, sin = (cs[0:r, i, m * HALF:(m + 1) * HALF].unsqueeze(1).broadcast_to(shape)
                                        for m in range(2))
                        else:
                            x1, x2 = k[:, :, :, 0:HALF], k[:, :, :, HALF:ROT]
                            o1, o2 = x1, x2
                            shape = [r, 2, NG, HALF]
                            tt = [t4[0:r, m, 0:4, :].rearrange("p (b g) e -> p b g e", b=2) for m in range(4)]
                            cos, sin = (cs[0:r, i, m * HALF:(m + 1) * HALF].unsqueeze(1).unsqueeze(1).broadcast_to(shape)
                                        for m in range(2))
                        nc.vector.tensor_tensor(tt[0], x1, cos, ALU.mult)
                        nc.vector.tensor_tensor(tt[1], x2, sin, ALU.mult)
                        nc.vector.tensor_tensor(tt[2], x2, cos, ALU.mult)
                        chain(nc.vector.tensor_tensor(tt[3], x1, sin, ALU.mult))
                        nc.vector.tensor_tensor(o1, tt[0], tt[1], ALU.subtract)
                        last = nc.vector.tensor_tensor(o2, tt[2], tt[3], ALU.add)
                        if part == 0:
                            chain(last)
                        else:
                            last.then_inc(s_rope, 1)
                    if j + 1 < n:
                        chain.eng.wait_ge(s_rope, j + 1)

                def lo(j):
                    r = rows_of(tiles[j])
                    for h in range(2):
                        dve.wait_ge(s_th, 2 * j + h + 1)
                        nc.vector.tensor_tensor(xT_lo[:, j % 2, 4 * h:4 * h + 4, 0:r], psT[h][:, :, 0:r],
                                                xT_hi[:, j % 2, 4 * h:4 * h + 4, 0:r].bitcast(F32),
                                                ALU.subtract).then_inc(s_tl, 1)

                scale_x(0)
                if n > 1:
                    scale_x(1)
                lo(0)
                dve.wait_ge(s_g, 16)
                for c in range(KC):
                    dve.wait_ge(s_hi, c + 1)
                    nc.vector.scalar_tensor_tensor(w_lo[:, c, :], w_raw[:, c % RAW, :], gT[:, c:c + 1],
                                                   w_hi[:, c, :].bitcast(F32), ALU.mult, ALU.subtract).then_inc(s_lo, 1)
                for j, i in enumerate(tiles):
                    r = rows_of(i)
                    if j + 1 < n:
                        lo(j + 1)
                    if j + 2 < n:
                        scale_x(j + 2)
                    for g, (a, b) in enumerate(groups):
                        if g % 2 == 0:
                            dve.wait_ge(s_mm, ng * j + g + 1)
                            nc.vector.tensor_copy(y[0:r, i, a:b], acc[j % 2][g][0:r, 0:b - a]).then_inc(s_yv, 1)
                    if rope:
                        dve.wait_ge(s_cs, 16)
                        dve.wait_ge(s_yv, n_v * (j + 1))
                        dve.wait_ge(s_ya, n_a * (j + 1))
                        rotate(chain, j, i, r)

            @block.tensor
            def _(pe):
                pe.wait_ge(s_c, 16)

                def transposes(j):
                    r = rows_of(tiles[j])
                    pe.wait_ge(s_xn, j + 1)
                    for c in range(KC):
                        if j and c % 4 == 0:
                            pe.wait_ge(s_tl, 2 * (j - 1) + c // 4 + 1)
                        m = nc.tensor.transpose(psT[c // 4][:, c % 4, 0:r], x_t[0:r, j % 2, c * P:(c + 1) * P],
                                                ident[0:r, 0:r])
                        if c % 4 == 3:
                            m.then_inc(s_tr, 1)

                transposes(0)
                for j, i in enumerate(tiles):
                    r = rows_of(i)
                    pe.wait_ge(s_tl, 2 * (j + 1))
                    if j + 1 < n:
                        transposes(j + 1)
                    if j >= 2:
                        pe.wait_ge(s_yv, n_v * (j - 1))
                        if n_a:
                            pe.wait_ge(s_ya, n_a * (j - 1))
                    for g, (a, b) in enumerate(groups):
                        for c in range(KC):
                            if j == 0 and g == 0:
                                pe.wait_ge(s_lo, c + 1)
                            for n_pass, (xs, ws) in enumerate(((xT_hi, w_hi), (xT_hi, w_lo), (xT_lo, w_hi))):
                                m = nc.tensor.matmul(acc[j % 2][g][0:r, 0:b - a], xs[:, j % 2, c, 0:r], ws[:, c, a:b],
                                                     start=(c == 0 and n_pass == 0),
                                                     stop=(c == KC - 1 and n_pass == 2))
                        m.then_inc(s_mm, 1)


def pool_mix(nc, t, yp, mT):
    seq_len = HIST + DT
    p_len = HIST + SEQ
    length = p_len + DB * seq_len
    with ExitStack() as ctx:
        ph = Phase(nc, ctx, "mix")
        ext = ph.sb("ext", [P, 4, length])
        sums = ph.sb("sums", [P, 2, length])
        diff = ph.sb("diff", [P, 4, TOK])
        state = ph.sb("state", [DB * HIST, PW])
        w = ph.sb("w", [P, 4, P])
        edge = ph.sb("edge", [P, 4, HIST])
        ident = ph.sb("ident", [P, P])
        psT = [ph.ps(f"psT{k}", [P, 4, P]) for k in range(2)]
        psM = [ph.ps(f"psM{k}", [P, 512]) for k in range(2)]
        s_c = ph.sem("constants_loaded")
        s_tr = ph.sem("tile_transposed")
        s_ext = ph.sem("ext_written")
        s_zero = ph.sem("zeros_written")
        s_d = ph.sem("difference_made")
        s_mm = ph.sem("mixed")
        s_m = ph.sem("mT_written")
        s_dve = ph.sem("vector_chain")
        samples = ext[:, :, p_len:length].rearrange("p g (b s) -> p g b s", b=DB)
        cols = [(0, 512), (512, 1024), (1024, TOK)]
        with nc.Block() as block:

            @block.sync
            def _(sp):
                sp.dma_start(ident[:, :], t["k_ident"]).then_inc(s_c, 16)
                sp.dma_start(state[:, :], t["state_pool"][0].rearrange("b s c -> (b s) c")).then_inc(s_c, 16)
                sp.dma_start(w[:, :, :], t["w_pool"][0].rearrange("g c d -> c g d")).then_inc(s_c, 16)
                sp.dma_start(edge[:, :, :], t["k_edge"]).then_inc(s_c, 16)

            @block.tensor
            def _(pe):
                pe.wait_ge(s_c, 64)
                for k in range(NT + 1):
                    if k >= 2:
                        pe.wait_ge(s_ext, k - 1)
                    r = rows_of(k) if k < NT else DB * HIST
                    for g in range(4):
                        src = yp[0:r, k, g * P:(g + 1) * P] if k < NT else state[:, g * P:(g + 1) * P]
                        m = nc.tensor.transpose(psT[k % 2][:, g, 0:r], src, ident[0:r, 0:r])
                    m.then_inc(s_tr, 1)
                for g in range(4):
                    pe.wait_ge(s_d, g + 1)
                    for k, (a, b) in enumerate(cols):
                        u = 3 * g + k
                        if u >= 2:
                            pe.wait_ge(s_m, u - 1)
                        nc.tensor.matmul(psM[u % 2][:, 0:b - a], w[:, g, :], diff[:, g, a:b],
                                         start=True, stop=True).then_inc(s_mm, 1)

            @block.scalar
            def _(act):
                for k in range(NT + 1):
                    act.wait_ge(s_tr, k + 1)
                    if k < NT - 1:
                        dst, src = ext[:, :, HIST + k * P:HIST + (k + 1) * P], psT[k % 2][:, :, :]
                        nc.scalar.copy(dst, src).then_inc(s_ext, 1)
                        continue
                    n = DT if k == NT - 1 else HIST
                    for g in range(4):
                        dst = samples[:, g, :, HIST:seq_len] if k == NT - 1 else samples[:, g, :, 0:HIST]
                        m = nc.scalar.copy(dst, psT[k % 2][:, g, 0:DB * n].rearrange("p (b s) -> p b s", b=DB))
                    m.then_inc(s_ext, 1)
                for u in range(12):
                    g, (a, b) = u // 3, cols[u % 3]
                    act.wait_ge(s_mm, u + 1)
                    nc.scalar.copy(mT[:, g, a:b], psM[u % 2][:, 0:b - a]).then_inc(s_m, 1)

            @block.vector
            def _(dve):
                chain = Chain(dve, s_dve)
                chain(nc.vector.memset(ext[:, :, 0:HIST], 0.0))
                dve.wait_ge(s_ext, NT + 1)
                dve.wait_ge(s_c, 64)
                for g in range(4):
                    wide = 2 << g
                    cur, m, at = ext[:, g, :], 1, 1
                    while m < wide:
                        new = sums[:, at % 2, :]
                        chain(nc.vector.tensor_tensor(new[:, 2 * m - 1:length], cur[:, 2 * m - 1:length],
                                                      cur[:, m - 1:length - m], ALU.add))
                        cur, m, at = new, 2 * m, at + 1
                    chain(nc.vector.tensor_tensor(cur[:, HIST:2 * HIST], cur[:, HIST:2 * HIST], edge[:, g, :], ALU.mult))
                    nc.vector.scalar_tensor_tensor(diff[:, g, 0:SEQ], cur[:, HIST:p_len], 1.0 / wide,
                                                   ext[:, g, HIST:p_len], ALU.mult, ALU.subtract)
                    tail = cur[:, p_len:length].rearrange("p (b s) -> p b s", b=DB)[:, :, HIST:seq_len]
                    nc.vector.scalar_tensor_tensor(diff[:, g, SEQ:TOK].rearrange("p (b s) -> p b s", b=DB), tail,
                                                   1.0 / wide, samples[:, g, :, HIST:seq_len], ALU.mult,
                                                   ALU.subtract).then_inc(s_d, 1)
                    dve.wait_ge(s_d, g + 1)


def compress(nc, t, o, ck_s, cv_s, ck_hi, ck_lo, cv_p):
    n_seq = DB + 1
    pairs = PAGE // 2
    n_j = STRIDE // 2
    RAW = 3
    with ExitStack() as ctx:
        ph = Phase(nc, ctx, "cmp")
        raw = ph.sb("raw", [P, RAW, 4, 2, 2 * NG, HD])
        paired = ph.sb("paired", [P, 2, 4, 2 * NG, 2, HD])
        rT = ph.sb("rT", [P, 2, 2 * NG, 4 * P])
        w1 = ph.sb("w1", [P, 2, n_j, 2, HD])
        w2 = ph.sb("w2", [HD, 2, 2 * HD])
        pe_t = ph.sb("pe_t", [P, 2, 2 * n_j])
        pe_b = ph.sb("pe_b", [HD, 2])
        ident = ph.sb("ident", [P, P])
        table = ph.sb("table", [1, DB * DB], I32)
        late = ph.sb("late", [HD, 2, NG, NCMP])
        z = ph.sb("z", [HD, 2, n_seq, NG, NCH])
        z3 = ph.sb("z3", [HD, 2, n_seq, NG, NCH])
        psT = [ph.ps(f"psT{k}", [P, 4, P]) for k in range(2)]
        psU = [ph.ps(f"psU{k}", [P, 2, NG, NCH]) for k in range(2)]
        psE = ph.ps("psE", [HD, 2])
        psV = [ph.ps(f"psV{k}", [HD, 4, 2 * HD]) for k in range(2)]
        psP = ph.ps("psP", [P, 2, 2, HD])
        s_c = ph.sem("weights_loaded")
        s_id = ph.sem("identity_loaded")
        s_tab = ph.sem("page_table_loaded")
        s_raw = [ph.sem(f"raw_slot{k}_loaded") for k in range(RAW)]
        s_pair = ph.sem("columns_paired")
        s_tr = ph.sem("tile_transposed")
        s_rT = ph.sem("tile_copied")
        s_pe = ph.sem("pe_term_made")
        s_peb = ph.sem("pe_term_copied")
        s_pl = ph.sem("pe_loaded")
        s_u = ph.sem("windows_multiplied")
        s_late = ph.sem("late_half_moved")
        s_z = ph.sem("hidden_made")
        s_sq = ph.sem("hidden_squared")
        s_cu = ph.sem("cubic_made")
        s_ex = ph.sem("exp_made")
        s_ge = ph.sem("gelu_made")
        s_out = ph.sem("outputs_multiplied")
        s_fin = ph.sem("hi_parts_copied")
        s_dve = ph.sem("vector_chain")
        cache = t["cache_cmp_kv"][0].rearrange("n (p r) u g d -> n p (r u g d)", r=2)
        own = o["p_cmp_kv"][0, 0].rearrange("(k p r) u g d -> p k (r u g d)", p=P, r=2)
        with nc.Block() as block:

            @block.sync
            def _(sp):
                sp.dma_start(table[:, :], t["page_table"].rearrange("(a b) n -> a (b n)", a=1)).then_inc(s_tab, 16)
                sp.wait_ge(s_tab, 16)
                for q in range(n_seq):
                    if q >= RAW:
                        sp.wait_ge(s_pair, 4 * (q - RAW + 1))
                    if q == DB:
                        dst = raw[:, q % RAW].rearrange("p k r c d -> p k (r c d)")
                        sp.dma_start(dst, own).then_inc(s_raw[q % RAW], 16)
                        continue
                    for n in range(PAST // PAGE):
                        page = sp.value_load(table[0:1, q * DB + n:q * DB + n + 1], min_val=0,
                                             max_val=cache.shape[0] - 1)
                        dst = raw[pairs * (n % 2):pairs * (n % 2) + pairs, q % RAW, n // 2].rearrange("p r c d -> p (r c d)")
                        sp.dma_start(dst, cache[bass.DynSlice(page, 1)].rearrange("a p f -> (a p) f")
                                     ).then_inc(s_raw[q % RAW], 16)

            @block.gpsimd
            def _(pool):
                pool.dma_start(ident[:, :], t["k_ident"]).then_inc(s_id, 16)
                for c in range(2):
                    pool.dma_start(pe_t[:, c, :], t["pe_cmp"][0, c].rearrange("l d -> (l d)").rearrange("(j p) -> p j", p=P),
                                   allow_slow_non_contiguous=True).then_inc(s_pl, 16)

            @block.tensor
            def _(pe):
                pe.wait_ge(s_id, 16)
                pe.wait_ge(s_c, 16 * 8)

                def transposes(q):
                    for k in range(4):
                        pe.wait_ge(s_pair, 4 * q + k + 1)
                        u = 4 * q + k
                        if u >= 2:
                            pe.wait_ge(s_rT, u - 1)
                        for cg in range(2 * NG):
                            m = nc.tensor.transpose(psT[u % 2][:, cg, :], paired[:, q % 2, k, cg].rearrange("p r d -> p (r d)"),
                                                    ident[:, :])
                        m.then_inc(s_tr, 1)

                transposes(0)
                for q in range(n_seq):
                    if q + 1 < n_seq:
                        transposes(q + 1)
                    if q == 1:
                        pe.wait_ge(s_pl, 32)
                        for c in range(2):
                            for k in range(2 * n_j):
                                m = nc.tensor.matmul(psE[:, c:c + 1], w1[:, c, k % n_j, k // n_j, :], pe_t[:, c, k:k + 1],
                                                     start=(k == 0), stop=(k == 2 * n_j - 1))
                        m.then_inc(s_pe, 1)
                    pe.wait_ge(s_rT, 4 * (q + 1))
                    if q >= 2:
                        pe.wait_ge(s_z, q - 1)
                    for c in range(2):
                        for j in range(n_j):
                            mov = rT[:, q % 2, NG * c:NG * c + NG, :].rearrange("p g (n j) -> p j g n", j=n_j)[:, j]
                            m = nc.tensor.matmul(psU[q % 2][:, c, :, :], w1[:, c, j, :, :].rearrange("p r h -> p (r h)"),
                                                 mov, start=(j == 0), stop=(j == n_j - 1))
                    m.then_inc(s_u, 1)
                pe.wait_ge(s_ge, n_seq)
                for g in range(NG):
                    nc.tensor.matmul(psT[0][g * HD:(g + 1) * HD, :, :].rearrange("p a b -> p (a b)"), w2[:, 0, 0:HD],
                                     z3[:, 0, 0:DB, g, :], start=True, stop=True)
                for b in range(DB):
                    for g in range(NG):
                        nc.tensor.matmul(psV[b // 4][:, b % 4, g * HD:(g + 1) * HD], z3[:, 1, b, g, :], w2[:, 1, 0:HD],
                                         start=True, stop=True)
                for g in range(NG):
                    nc.tensor.matmul(psP[:, 0, g, :], w2[:, 0, :], z3[:, 0, DB, g, :], start=True, stop=True)
                for g in range(NG):
                    m = nc.tensor.matmul(psP[0:HD, 1, g, :], z3[:, 1, DB, g, :], w2[:, 1, 0:HD], start=True, stop=True)
                m.then_inc(s_out, 1)

            @block.scalar
            def _(act):
                for c in range(2):
                    for r in range(2):
                        src = t["w_cmp1"][0, c].rearrange("(r j p) h -> r p j h", r=2, p=P)[r]
                        act.dma_start(w1[:, c, :, r, :], src).then_inc(s_c, 16)
                    for k in range(2):
                        act.dma_start(w2[:, c, k * HD:(k + 1) * HD], t["w_cmp2"][0, c]).then_inc(s_c, 16)

                def late_half(act, q):
                    act.wait_ge(s_u, q + 1)
                    if q:
                        act.wait_ge(s_z, q)
                    for c in range(2):
                        m = nc.scalar.copy(late[:, c, :, :], psU[q % 2][HD:P, c, :, 1:NCH])
                    m.then_inc(s_late, 1)

                for q in range(n_seq + 3):
                    if q < n_seq:
                        for k in range(4):
                            u = 4 * q + k
                            act.wait_ge(s_tr, u + 1)
                            if q >= 2:
                                act.wait_ge(s_u, q - 1)
                            nc.scalar.copy(rT[:, q % 2, :, k * P:(k + 1) * P], psT[u % 2][:, :, :]).then_inc(s_rT, 1)
                    if 0 <= q - 1 < n_seq:
                        late_half(act, q - 1)
                    if 0 <= q - 2 < n_seq:
                        act.wait_ge(s_z, q - 1)
                        nc.scalar.activation(z3[:, :, q - 2], z[:, :, q - 2], ACT.Square).then_inc(s_sq, 1)
                    if 0 <= q - 3 < n_seq:
                        act.wait_ge(s_cu, q - 2)
                        nc.scalar.activation(z3[:, :, q - 3], z3[:, :, q - 3], ACT.Exp,
                                             scale=-2.0 * 0.7978845608028654).then_inc(s_ex, 1)
                act.wait_ge(s_out, 1)
                nc.scalar.copy(ck_hi[:, :, :], psP[:, 0, :, :])
                nc.scalar.copy(cv_p[0:NCMP, :, 0:HD], psP[0:NCMP, 1, :, :])
                nc.scalar.copy(cv_s[:, 0:4, :], psV[0][:, :, :])
                nc.scalar.copy(cv_s[:, 4:8, :], psV[1][:, :, :]).then_inc(s_fin, 1)

            @block.vector
            def _(dve):
                chain = Chain(dve, s_dve)
                nc.vector.memset(z[:, :, :, :, NCMP:NCH], 0.0)

                def pair(q):
                    dve.wait_ge(s_raw[q % RAW], 16 * (8 * (q // RAW + 1) if q < DB else 8 * (q // RAW) + 1))
                    if q >= 2:
                        dve.wait_ge(s_tr, 4 * (q - 1))
                    for k in range(4):
                        nc.vector.tensor_copy(paired[:, q % 2, k], raw[:, q % RAW, k].rearrange("p r c d -> p c r d")
                                              ).then_inc(s_pair, 1)

                pair(0)
                for q in range(n_seq + 3):
                    if q + 1 < n_seq:
                        pair(q + 1)
                    if q == 1:
                        dve.wait_ge(s_pe, 1)
                        nc.vector.tensor_copy(pe_b[:, :], psE[:, :]).then_inc(s_peb, 1)
                        dve.wait_ge(s_peb, 1)
                    if 0 <= q - 1 < n_seq:
                        dve.wait_ge(s_late, q)
                        for c in range(2):
                            m = nc.vector.scalar_tensor_tensor(z[:, c, q - 1, :, 0:NCMP], psU[(q - 1) % 2][0:HD, c, :, 0:NCMP],
                                                               pe_b[:, c:c + 1], late[:, c, :, :], ALU.add, ALU.add)
                        m.then_inc(s_z, 1)
                    if 0 <= q - 2 < n_seq:
                        w = z3[:, :, q - 2]
                        dve.wait_ge(s_sq, q - 1)
                        chain(nc.vector.tensor_scalar(w, w, 0.044715, 1.0, ALU.mult, ALU.add))
                        nc.vector.tensor_tensor(w, w, z[:, :, q - 2], ALU.mult).then_inc(s_cu, 1)
                    if 0 <= q - 3 < n_seq:
                        w = z3[:, :, q - 3]
                        dve.wait_ge(s_ex, q - 2)
                        chain(nc.vector.tensor_scalar(w, w, 1.0, None, ALU.add))
                        chain(nc.vector.reciprocal(w, w))
                        nc.vector.tensor_tensor(w, w, z[:, :, q - 3], ALU.mult).then_inc(s_ge, 1)
                dve.wait_ge(s_fin, 1)
                nc.vector.tensor_copy(ck_s[:, :, :], psT[0][:, :, :].rearrange("p a b -> p (a b)").rearrange("p (b n) -> p b n", b=DB))
                nc.vector.tensor_tensor(ck_lo[:, :, :], psP[:, 0, :, :], ck_hi[:, :, :].bitcast(F32), ALU.subtract)
                chain(nc.vector.tensor_tensor(cv_p[0:NCMP, :, HD:P], psP[0:NCMP, 1, :, :],
                                              cv_p[0:NCMP, :, 0:HD].bitcast(F32), ALU.subtract))


N_SEL = PAST + DT
N_WIN = WIN + DT
S_WIN0 = N_SEL
S_CMP0 = N_SEL + N_WIN
S_COLS = S_CMP0 + NCH
N_MID = PAST // SELB - 2


def sample_attention(nc, t, o, yq, q_rot, ck_s, cv_s, aT):
    R = NH * DT
    KV = 3
    with ExitStack() as ctx:
        ph = Phase(nc, ctx, "smp")
        ident = ph.sb("ident", [P, P])
        same = ph.sb("same", [R, R])
        mask = ph.sb("mask", [R, S_COLS])
        block_no = ph.sb("block_no", [R, N_MID])
        table = ph.sb("table", [1, DB * DB], I32)
        gate_tok = ph.sb("gate_tok", [R, 3 * NH])
        gate = ph.sb("gate", [R, DB, 3])
        q_pair = ph.sb("q_pair", [R, 2, HPG, NG, HD])
        q_bd = ph.sb("q_bd", [P, 2, DB, R])
        sel = ph.sb("sel", [P, KV, PAST // P, KVW])
        win = ph.sb("win", [P, KV, WIN // P, KVW])
        new = ph.sb("new", [DT, KV, 2, KVW])
        kT = ph.sb("kT", [P, 2, N_SEL + N_WIN])
        sc = ph.sb("sc", [R, 2, S_COLS])
        stat = ph.sb("stat", [R, 2, 16])
        mid = ph.sb("mid", [R, 2, NCH])
        imp = ph.sb("imp", [R, 2, 4, N_MID])
        pT = ph.sb("pT", [P, 2, 15, R])
        a_rows = ph.sb("a_rows", [R, DB, HD])
        scratch = nc.dram_tensor("gate_scratch", (R, 3 * NH), F32, kind="Internal").ap()
        psS = ph.ps("psS", [R, 4, 512])
        psT = [ph.ps(f"psT{k}", [P, 512]) for k in range(2)]
        psO = ph.ps("psO", [R, P])
        psI = ph.ps("psI", [P, 512])
        s_c = ph.sem("constants_loaded")
        s_tab = ph.sem("page_table_loaded")
        s_kv = [ph.sem(f"keys_slot{k}_loaded") for k in range(KV)]
        s_ge = ph.sem("gate_exp")
        s_gt = ph.sem("gate_made")
        s_gw = ph.sem("gate_stored")
        s_gr = ph.sem("gate_read")
        s_qp = ph.sem("q_paired")
        s_qt = ph.sem("q_transposed")
        s_qz = ph.sem("q_zeroed")
        s_qb = ph.sem("q_blocks_written")
        s_kt = ph.sem("keys_transposed")
        s_kc = ph.sem("keys_copied")
        s_s = ph.sem("scores_made")
        s_sm = ph.sem("scores_masked")
        s_mc = ph.sem("cmp_max")
        s_ec = ph.sem("cmp_exp")
        s_pc = ph.sem("cmp_probs")
        s_i = ph.sem("importance_summed")
        s_ic = ph.sem("importance_copied")
        s_m = ph.sem("maxima")
        s_e = ph.sem("exps")
        s_p = ph.sem("probs_scaled")
        s_pt = ph.sem("probs_transposed")
        s_pq = ph.sem("pT_copied")
        s_o = ph.sem("output_multiplied")
        s_a = ph.sem("output_copied")
        s_at = ph.sem("outputs_transposed")
        s_af = ph.sem("aT_written")
        s_dve = ph.sem("vector_chain")
        i_s = NT - 1
        cache = t["cache_sel_kv"][0].rearrange("n p u g d -> n p (u g d)")
        cwin = t["cache_win_kv"][0].rearrange("b (k p) u g d -> b p k (u g d)", p=P)
        new_sel = o["s_sel_kv"][0].rearrange("b n u g d -> b n (u g d)")
        new_win = o["s_win_kv"][0].rearrange("b n u g d -> b n (u g d)")
        blocks = ([(k * P, P, lambda b, k=k: sel[:, b % KV, k, P:KVW]) for k in range(8)]
                  + [(PAST, DT, lambda b: new[:, b % KV, 0, P:KVW]), (S_WIN0 + WIN, DT, lambda b: new[:, b % KV, 1, P:KVW])]
                  + [(S_WIN0 + k * P, P, lambda b, k=k: win[:, b % KV, k, P:KVW]) for k in range(4)]
                  + [(S_CMP0, HD, lambda b: cv_s[:, b, :])])
        key_src = ([(k * P, P, lambda b, k=k: sel[:, b % KV, k, 0:P]) for k in range(8)]
                   + [(PAST, DT, lambda b: new[:, b % KV, 0, 0:P])]
                   + [(S_WIN0 + k * P, P, lambda b, k=k: win[:, b % KV, k, 0:P]) for k in range(4)]
                   + [(S_WIN0 + WIN, DT, lambda b: new[:, b % KV, 1, 0:P])])
        key_sets = [key_src[0:4], key_src[4:8], key_src[8:12], key_src[12:14]]
        n_loads = PAST // PAGE + 3
        with nc.Block() as block:

            @block.sync
            def _(sp):
                sp.dma_start(table[:, :], t["page_table"].rearrange("(a b) n -> a (b n)", a=1)).then_inc(s_tab, 16)
                sp.wait_ge(s_tab, 16)
                for b in range(DB):
                    if b >= KV:
                        sp.wait_ge(s_o, b - KV + 1)
                    for n in range(PAST // PAGE):
                        page = sp.value_load(table[0:1, b * DB + n:b * DB + n + 1], min_val=0,
                                             max_val=cache.shape[0] - 1)
                        sp.dma_start(sel[:, b % KV, n, :], cache[bass.DynSlice(page, 1)].rearrange("a p f -> (a p) f")
                                     ).then_inc(s_kv[b % KV], 16)
                    sp.dma_start(win[:, b % KV], cwin[b]).then_inc(s_kv[b % KV], 16)
                    sp.dma_start(new[:, b % KV, 0, :], new_sel[b]).then_inc(s_kv[b % KV], 16)
                    sp.dma_start(new[:, b % KV, 1, :], new_win[b, WIN - DT:WIN]).then_inc(s_kv[b % KV], 16)

            @block.gpsimd
            def _(pool):
                pool.dma_start(ident[:, :], t["k_ident"]).then_inc(s_c, 16)
                pool.dma_start(same[:, :], t["k_same"]).then_inc(s_c, 16)
                pool.dma_start(mask[:, :], t["k_smask"]).then_inc(s_c, 16)
                pool.dma_start(block_no[:, :], t["k_block_no"]).then_inc(s_c, 16)
                nc.gpsimd.memset(q_bd[:, :, :, :], 0.0).then_inc(s_qz, 1)
                q = yq[0:R, i_s, C_Q:C_Q + AW].rearrange("p (g h d) -> p h g d", g=NG, h=HPG)
                nc.gpsimd.tensor_copy(q_pair[:, 0], q).then_inc(s_qp, 1)
                nc.gpsimd.tensor_copy(q_pair[:, 1], q).then_inc(s_qp, 1)
                pool.wait_ge(s_qp, 2)
                nc.gpsimd.tensor_copy(q_pair[:, 1, :, :, 0:ROT],
                                      q_rot[0:R, i_s].rearrange("p (g h) e -> p h g e", g=NG)).then_inc(s_qp, 1)
                pool.wait_ge(s_gt, 1)
                pool.dma_start(scratch, gate_tok[:, :]).then_inc(s_gw, 16)
                pool.wait_ge(s_gw, 16)
                for h in range(NH):
                    pool.dma_start(gate[h * DT:(h + 1) * DT, :, :],
                                   scratch.rearrange("(b t) (h j) -> h t b j", b=DB, h=NH)[h],
                                   allow_slow_non_contiguous=True).then_inc(s_gr, 16)

            @block.tensor
            def _(pe):
                pe.wait_ge(s_c, 64)
                pe.wait_ge(s_qp, 3)
                for v in range(2):
                    for h in range(HPG):
                        m = nc.tensor.transpose(psT[v][:, h * R:(h + 1) * R],
                                                q_pair[:, v, h].rearrange("p g d -> p (g d)"), ident[0:R, 0:R])
                    m.then_inc(s_qt, 1)
                pe.wait_ge(s_qb, 4)

                def keys(b):
                    pe.wait_ge(s_kv[b % KV], 16 * n_loads * (b // KV + 1))
                    for k, members in enumerate(key_sets):
                        u = 4 * b + k
                        if u >= 2:
                            pe.wait_ge(s_kc, u - 1)
                        if b >= 2 and k < 2:
                            pe.wait_ge(s_pq, 2 * (b - 1))
                        for m_i, (c0, n, src) in enumerate(members):
                            m = nc.tensor.transpose(psT[k % 2][:, m_i * P:m_i * P + n], src(b), ident[0:n, 0:n])
                        m.then_inc(s_kt, 1)

                def scores(b):
                    pe.wait_ge(s_kc, 4 * (b + 1))
                    if b:
                        pe.wait_ge(s_sm, b)
                    c = 0
                    while c < S_COLS:
                        end = min(S_COLS, (c // 512 + 1) * 512, *[x for x in (S_WIN0, S_CMP0) if x > c] or [S_COLS])
                        if c >= S_CMP0:
                            q, k = q_bd[:, 0, b, :], ck_s[:, b, c - S_CMP0:end - S_CMP0]
                        else:
                            q, k = q_bd[:, 1, b, :], kT[:, b % 2, c:end]
                        m = nc.tensor.matmul(psS[:, c // 512, c % 512:c % 512 + end - c], q, k, start=True, stop=True)
                        c = end
                    m.then_inc(s_s, 1)

                def importance(b):
                    pe.wait_ge(s_pc, b + 1)
                    if b:
                        pe.wait_ge(s_ic, b)
                    nc.tensor.matmul(psI[0:R, 0:NCH], same[:, :], sc[:, b % 2, S_CMP0:S_COLS],
                                     start=True, stop=True).then_inc(s_i, 1)

                def prob_transposes(b):
                    pe.wait_ge(s_p, b + 1)
                    for v in range(2):
                        for m_i, (c0, n, _) in enumerate(blocks[8 * v:8 * v + 8]):
                            m = nc.tensor.transpose(psT[v][0:n, m_i * R:(m_i + 1) * R], sc[:, b % 2, c0:c0 + n],
                                                    ident[0:R, 0:R])
                        m.then_inc(s_pt, 1)

                def values(b):
                    if b:
                        pe.wait_ge(s_a, 2 * b)
                    for m_i, (c0, n, val) in enumerate(blocks):
                        if m_i % 8 == 0:
                            pe.wait_ge(s_pq, 2 * b + m_i // 8 + 1)
                        m = nc.tensor.matmul(psO[:, :], pT[0:n, b % 2, m_i, :], val(b), start=(m_i == 0),
                                             stop=(m_i == len(blocks) - 1))
                    m.then_inc(s_o, 1)

                keys(0)
                scores(0)
                keys(1)
                importance(0)
                for b in range(DB):
                    if b + 1 < DB:
                        scores(b + 1)
                    prob_transposes(b)
                    if b + 1 < DB:
                        importance(b + 1)
                    if b + 2 < DB:
                        keys(b + 2)
                    values(b)
                pe.wait_ge(s_a, 2 * DB)
                for b in range(DB):
                    m = nc.tensor.transpose(psI[0:HD, b * R:(b + 1) * R], a_rows[:, b, :], ident[0:R, 0:R])
                m.then_inc(s_at, 1)

            @block.scalar
            def _(act):
                nc.scalar.activation(gate_tok[:, :], yq[0:R, i_s, C_GL:C_PI], ACT.Exp, scale=-1.0).then_inc(s_ge, 1)

                def copy_keys(b):
                    for k, members in enumerate(key_sets):
                        act.wait_ge(s_kt, 4 * b + k + 1)
                        c0 = members[0][0]
                        n = sum(x[1] for x in members)
                        if b >= 2 and k == 0:
                            act.wait_ge(s_s, b - 1)
                        if k < 2:
                            m = nc.scalar.copy(kT[:, b % 2, c0:c0 + n], psT[k % 2][:, 0:n])
                        elif k == 2:
                            nc.scalar.copy(kT[:, b % 2, c0:c0 + DT], psT[0][:, 0:DT])
                            m = nc.scalar.copy(kT[:, b % 2, S_WIN0:S_WIN0 + 3 * P], psT[0][:, P:4 * P])
                        else:
                            m = nc.scalar.copy(kT[:, b % 2, c0:c0 + n], psT[1][:, 0:n])
                        m.then_inc(s_kc, 1)

                def cmp_exp(b):
                    st = stat[:, b % 2]
                    act.wait_ge(s_mc, b + 1)
                    nc.scalar.activation(sc[:, b % 2, S_CMP0:S_COLS], sc[:, b % 2, S_CMP0:S_COLS], ACT.Exp,
                                         bias=st[:, 3:4], scale=SCALE, accum_out=st[:, 4:5]).then_inc(s_ec, 1)

                copy_keys(0)
                copy_keys(1)
                cmp_exp(0)
                for b in range(DB):
                    st = stat[:, b % 2]
                    act.wait_ge(s_m, b + 1)
                    for v, (c0, c1) in enumerate(((0, N_SEL), (S_WIN0, S_CMP0))):
                        nc.scalar.activation(sc[:, b % 2, c0:c1], sc[:, b % 2, c0:c1], ACT.Exp, bias=st[:, 8 + v:9 + v],
                                             scale=SCALE, accum_out=st[:, 10 + v:11 + v]).then_inc(s_e, 1)
                    if b + 1 < DB:
                        cmp_exp(b + 1)
                    act.wait_ge(s_pt, 2 * b + 1)
                    if b >= 2:
                        act.wait_ge(s_o, b - 1)
                    nc.scalar.copy(pT[:, b % 2, 0:8, :], psT[0][:, :].rearrange("p (m r) -> p m r", r=R)).then_inc(s_pq, 1)
                    act.wait_ge(s_pt, 2 * b + 2)
                    nc.scalar.copy(pT[0:DT, b % 2, 8:10, :], psT[1][0:DT, 0:2 * R].rearrange("p (m r) -> p m r", r=R))
                    nc.scalar.copy(pT[:, b % 2, 10:14, :], psT[1][:, 2 * R:6 * R].rearrange("p (m r) -> p m r", r=R))
                    nc.scalar.copy(pT[0:HD, b % 2, 14, :], psT[1][0:HD, 6 * R:7 * R]).then_inc(s_pq, 1)
                    if b + 2 < DB:
                        copy_keys(b + 2)
                act.wait_ge(s_at, 1)
                src = psI[0:HD, :].rearrange("d (b m e s) -> d b m e s", b=DB, m=4, e=2)
                dst = aT[:, :, SEQ:TOK].rearrange("d m (b s) -> d b m s", b=DB)
                nc.scalar.copy(dst[0:HD], src[:, :, :, 0])
                nc.scalar.copy(dst[HD:P], src[:, :, :, 1]).then_inc(s_af, 1)
                act.wait_ge(s_af, 1)

            @block.vector
            def _(dve):
                chain = Chain(dve, s_dve)
                dve.wait_ge(s_ge, 1)
                chain(nc.vector.tensor_scalar(gate_tok[:, :], gate_tok[:, :], 1.0, None, ALU.add))
                nc.vector.reciprocal(gate_tok[:, :], gate_tok[:, :]).then_inc(s_gt, 1)
                dve.wait_ge(s_qz, 1)
                for v in range(2):
                    dve.wait_ge(s_qt, v + 1)
                    src = psT[v][:, 0:HPG * R].rearrange("p (h b s) -> p b h s", h=HPG, b=DB)
                    for g in range(NG):
                        dst = q_bd[g * HD:(g + 1) * HD, v, :, g * 32:(g + 1) * 32].rearrange("p b (h s) -> p b h s", h=HPG)
                        nc.vector.tensor_copy(dst, src[g * HD:(g + 1) * HD]).then_inc(s_qb, 1)
                dve.wait_ge(s_c, 64)

                def cmp_max(b):
                    st, S = stat[:, b % 2], sc[:, b % 2]
                    dve.wait_ge(s_s, b + 1)
                    if b >= 2:
                        dve.wait_ge(s_pt, 2 * (b - 1))
                    flat = psS[:, :, :].rearrange("p a b -> p (a b)")
                    nc.vector.tensor_tensor(S, flat[:, 0:S_COLS], mask[:, :], ALU.add).then_inc(s_sm, 1)
                    dve.wait_ge(s_sm, b + 1)
                    chain(nc.vector.reduce_max(st[:, 2:3], S[:, S_CMP0:S_COLS], AX.X, negate=True))
                    nc.vector.tensor_scalar(st[:, 3:4], st[:, 2:3], SCALE, None, ALU.mult).then_inc(s_mc, 1)

                def cmp_probs(b):
                    st, S = stat[:, b % 2], sc[:, b % 2]
                    dve.wait_ge(s_ec, b + 1)
                    chain(nc.vector.reciprocal(st[:, 5:6], st[:, 4:5]))
                    nc.vector.tensor_scalar(S[:, S_CMP0:S_COLS], S[:, S_CMP0:S_COLS], st[:, 5:6], None,
                                            ALU.mult).then_inc(s_pc, 1)

                def selection(b):
                    st, S = stat[:, b % 2], sc[:, b % 2]
                    nc.vector.reduce_max(st[:, 13:14], S[:, S_WIN0:S_CMP0], AX.X, negate=True)
                    dve.wait_ge(s_i, b + 1)
                    w = mid[:, b % 2]
                    nc.vector.tensor_copy(w, psI[0:R, 0:NCH]).then_inc(s_ic, 1)
                    dve.wait_ge(s_ic, b + 1)
                    quad = w.rearrange("p (j e) -> p j e", e=4)
                    whole, halves, total, drop = (imp[:, b % 2, x] for x in range(4))
                    nc.vector.reduce_sum(whole, quad[:, 1:1 + N_MID, 0:3], AX.X)
                    chain(nc.vector.tensor_tensor(halves, quad[:, 1:1 + N_MID, 3], quad[:, 0:N_MID, 3], ALU.add))
                    chain(nc.vector.scalar_tensor_tensor(total, halves, SELB / 4 / CLEN, whole, ALU.mult, ALU.add))
                    chain(nc.vector.tensor_reduce(st[:, 6:7], total, AX.X, ALU.min))
                    chain(nc.vector.scalar_tensor_tensor(drop, total, st[:, 6:7], block_no[:, :], ALU.is_equal, ALU.mult))
                    chain(nc.vector.reduce_max(st[:, 7:8], drop, AX.X))
                    chain(nc.vector.tensor_scalar(drop, block_no[:, :], st[:, 7:8], NEG, ALU.is_equal, ALU.mult))
                    body = S[:, SELB:SELB * (1 + N_MID)].rearrange("p (j e) -> p j e", e=SELB)
                    chain(nc.vector.tensor_tensor(body, body, drop.unsqueeze(2).broadcast_to([R, N_MID, SELB]), ALU.add))
                    chain(nc.vector.reduce_max(st[:, 12:13], S[:, 0:N_SEL], AX.X, negate=True))
                    nc.vector.tensor_scalar(st[:, 8:10], st[:, 12:14], SCALE, None, ALU.mult).then_inc(s_m, 1)

                def scale_probs(b):
                    st, S = stat[:, b % 2], sc[:, b % 2]
                    dve.wait_ge(s_e, 2 * (b + 1))
                    if b == 0:
                        dve.wait_ge(s_gr, 16 * NH)
                    chain(nc.vector.reciprocal(st[:, 14:16], st[:, 10:12]))
                    chain(nc.vector.tensor_tensor(st[:, 14:16], st[:, 14:16], gate[:, b, 1:3], ALU.mult))
                    nc.vector.tensor_scalar(S[:, 0:N_SEL], S[:, 0:N_SEL], st[:, 14:15], None, ALU.mult)
                    nc.vector.tensor_scalar(S[:, S_CMP0:S_COLS], S[:, S_CMP0:S_COLS], gate[:, b, 0:1], None, ALU.mult)
                    nc.vector.tensor_scalar(S[:, S_WIN0:S_CMP0], S[:, S_WIN0:S_CMP0], st[:, 15:16], None,
                                            ALU.mult).then_inc(s_p, 1)

                def keep_outputs(b):
                    dve.wait_ge(s_o, b + 1)
                    for g in range(NG):
                        nc.vector.tensor_copy(a_rows[g * 32:(g + 1) * 32, b, :],
                                              psO[g * 32:(g + 1) * 32, g * HD:(g + 1) * HD]).then_inc(s_a, 1)

                cmp_max(0)
                cmp_probs(0)
                for b in range(DB):
                    selection(b)
                    if b + 1 < DB:
                        cmp_max(b + 1)
                    scale_probs(b)
                    if b + 1 < DB:
                        cmp_probs(b + 1)
                    if b:
                        keep_outputs(b - 1)
                keep_outputs(DB - 1)


WB = WIN // P + 1
P_WIN0 = SEQ
P_CMP0 = SEQ + WB * P
P_COLS = P_CMP0 + NCH


def prompt_attention(nc, t, yq, q_rot, ck_hi, ck_lo, cv_p, aT):
    LAG = 2
    n_tiles = NT - 1
    units = [(i, g) for i in range(n_tiles) for g in range(NG)]

    def key_blocks(u):
        i, _ = units[u]
        first = max(0, i - WB + 1)
        return ([(kb * P, 0, kb) for kb in range(i + 1)]
                + [(P_WIN0 + (kb - first) * P, 1, kb) for kb in range(first, i + 1)] + [(P_CMP0, 2, 0)])

    base = [0]
    for u in range(len(units)):
        base.append(base[-1] + len(key_blocks(u)))

    def steps():
        for s in range(3):
            yield "prep", (0, s)
        for u in range(len(units) + 1):
            blocks = list(range(len(key_blocks(u - 1)))) if u else []
            prep = []
            if u < len(units):
                i, g = units[u]
                prep = [(i, 3), (i, 4)] if g == 0 else [(i + 1, s) for s in range(3) if i + 1 < n_tiles]
            shares = [blocks[k * len(blocks) // 16:(k + 1) * len(blocks) // 16] for k in range(16)]
            for hh in range(HPG):
                live = u < len(units)
                if live:
                    yield "sel scores", (u, hh)
                if hh == 0 and u >= 2:
                    yield "drain", (u - 2, 0)
                kinds = (("sel max", "win scores"), ("sel exp", "win max"), ("win exp",), ("scale",))
                for k in range(4):
                    for b in shares[4 * hh + k]:
                        yield "block", (u - 1, b)
                    for kind in kinds[k] if live else ():
                        yield kind, (u, hh)
                    if prep and k == 1:
                        yield "prep", prep.pop(0)
        yield "drain", (len(units) - 1, 0)

    def cols_of(i):
        return (i + 1) * P, (min(i, WB - 1) + 1) * P

    with ExitStack() as ctx:
        ph = Phase(nc, ctx, "att")
        ident = ph.sb("ident", [P, P])
        identR = ph.sb("identR", [P, P], F32R)
        n_mask = 2 * P + n_tiles * NCH
        masksR = ph.sb("masksR", [P, n_mask], F32R)
        causal, oldest = masksR[:, 0:P], masksR[:, P:2 * P]
        gate = ph.sb("gate", [P, n_tiles, NH, 3])
        q_dup = ph.sb("q_dup", [P, 2, NH, 2, HD])
        k_dup = ph.sb("k_dup", [P, 2, NG, 2, HD])
        qS = ph.sb("qS", [P, 2, NH, P], F32R)
        k_hi = ph.sb("k_hi", [P, 2, NG, SEQ], F32R)
        k_lo = ph.sb("k_lo", [P, 2, NG, SEQ], F32R)
        v_st = ph.sb("v_st", [P, 2, n_tiles, NG, P], F32R)
        prob = ph.sb("prob", [P, 2 * HPG, P_COLS])
        stat = ph.sb("stat", [P, 2 * HPG, 16])
        pT_hi = ph.sb("pT_hi", [P, LAG + 1, 4 * P], F32R)
        pT_lo = ph.sb("pT_lo", [P, LAG + 1, 4 * P], F32R)
        other = ph.sb("other", [P, 2, P])
        psA = ph.ps("psA", [P, 2, 512])
        psB = ph.ps("psB", [P, 2, 512])
        psQ = ph.ps("psQ", [P, 4, P])
        psT = [ph.ps(f"psT{k}", [P, 4, P]) for k in range(2)]
        psO = ph.ps("psO", [P, 4, P])
        flatA = psA[:, :, :].rearrange("p a b -> p (a b)")
        flatB = psB[:, :, :].rearrange("p a b -> p (a b)")
        B_CMP = WB * P
        s_c = ph.sem("constants_loaded")
        s_mr = ph.sem("masks_rounded")
        s_ge = ph.sem("gate_exp")
        s_g = ph.sem("gate_made")
        s_qd = ph.sem("queries_doubled")
        s_kd = ph.sem("keys_doubled")
        s_qt = ph.sem("prep_transposed")
        s_qh = ph.sem("prep_hi_made")
        s_ql = ph.sem("prep_lo_made")
        s_vh = ph.sem("value_hi_made")
        s_sa = ph.sem("sel_scores_made")
        s_sb = ph.sem("win_cmp_scores_made")
        s_ma = ph.sem("sel_max_made")
        s_mb = ph.sem("win_cmp_max_made")
        s_ea = ph.sem("sel_exp_made")
        s_eb = ph.sem("win_cmp_exp_made")
        s_f = ph.sem("factors_made")
        s_pv = ph.sem("probs_scaled_by_vector")
        s_pp = ph.sem("probs_scaled_by_pool")
        s_pt = ph.sem("probs_transposed")
        s_th = ph.sem("pT_hi_made")
        s_tl = ph.sem("pT_lo_made")
        s_o = ph.sem("unit_output_made")
        s_oc = ph.sem("other_halves_copied")
        s_od = ph.sem("output_drained")
        s_dve = ph.sem("vector_chain")

        def prep_no(arg):
            return 5 * arg[0] + arg[1]

        with nc.Block() as block:

            @block.sync
            def _(sp):
                sp.dma_start(ident[:, :], t["k_ident"]).then_inc(s_c, 16)
                sp.dma_start(prob[:, 0, 0:n_mask], t["k_pmask"]).then_inc(s_c, 16)

            @block.gpsimd
            def _(pool):
                def double_keys(i):
                    if i:
                        pool.wait_ge(s_qt, 5 * (i - 1) + 1)
                    k = yq[:, i, C_KS:C_KS + 2 * KVW].rearrange("p (b u g d) -> p b u g d", b=2, u=2, g=NG)[:, :, 0]
                    for b in range(2):
                        m = nc.gpsimd.tensor_copy(k_dup[:, b], k[:, b].unsqueeze(2).broadcast_to([P, NG, 2, HD]))
                    m.then_inc(s_kd, 1)

                def double_queries(i):
                    if i:
                        pool.wait_ge(s_qt, 5 * i)
                    q = yq[:, i, C_Q:C_Q + AW].rearrange("p (h d) -> p h d", d=HD).unsqueeze(2)
                    r = q_rot[:, i].unsqueeze(2).broadcast_to([P, NH, 2, ROT])
                    nc.gpsimd.tensor_copy(q_dup[:, 0], q.broadcast_to([P, NH, 2, HD]))
                    nc.gpsimd.tensor_copy(q_dup[:, 1, :, :, ROT:HD], q[:, :, :, ROT:HD].broadcast_to([P, NH, 2, HD - ROT]))
                    nc.gpsimd.tensor_copy(q_dup[:, 1, :, :, 0:ROT], r).then_inc(s_qd, 1)

                double_keys(0)
                double_queries(0)
                for kind, arg in steps():
                    if kind == "prep" and arg[1] == 1 and arg[0] + 1 < n_tiles:
                        double_keys(arg[0] + 1)
                    if kind == "prep" and arg[1] == 4 and arg[0] + 1 < n_tiles:
                        double_queries(arg[0] + 1)
                    if kind == "scale":
                        (u, hh), (i, g) = arg, units[arg[0]]
                        n = HPG * u + hh
                        slot = n % (2 * HPG)
                        pool.wait_ge(s_f, n + 1)
                        c1 = P_WIN0 + cols_of(i)[1]
                        nc.gpsimd.tensor_scalar(prob[:, slot, P_WIN0:c1], prob[:, slot, P_WIN0:c1],
                                                stat[:, slot, 14:15], 1.0, ALU.mult, ALU.mult)
                        nc.gpsimd.tensor_scalar(prob[:, slot, P_CMP0:P_COLS], prob[:, slot, P_CMP0:P_COLS],
                                                stat[:, slot, 12:13], 1.0, ALU.mult, ALU.mult).then_inc(s_pp, 1)

            @block.tensor
            def _(pe):
                def product(u, arg):
                    i, g = units[u]
                    c0, branch, kb = key_blocks(u)[arg]
                    n = base[u] + arg
                    last = arg == len(key_blocks(u)) - 1
                    rows = NCMP if branch == 2 else P
                    val = cv_p[0:NCMP, g, :] if branch == 2 else v_st[:, branch, kb, g, :]
                    pe.wait_ge(s_th, n + 1)
                    if arg == 0 and u:
                        pe.wait_ge(s_od, u)
                    out = psO[:, :, :].rearrange("p a b -> p (a b)")
                    nc.tensor.matmul(out, val, pT_hi[0:rows, n % (LAG + 1), :], start=(arg == 0), stop=False)
                    pe.wait_ge(s_tl, n + 1)
                    m = nc.tensor.matmul(out, val, pT_lo[0:rows, n % (LAG + 1), :], start=False, stop=last)
                    if last:
                        m.then_inc(s_o, 1)

                pe.wait_ge(s_c, 32)
                pe.wait_ge(s_mr, 2)
                for kind, arg in steps():
                    if kind == "prep":
                        i, s = arg
                        p = prep_no(arg)
                        if p:
                            pe.wait_ge(s_ql, p)
                        pe.wait_ge(s_kd if s == 0 else s_qd, i + 1)
                        for x in range(4):
                            src = k_dup[:, x // 2, x % 2] if s == 0 else q_dup[:, (s - 1) % 2, 4 * ((s - 1) // 2) + x]
                            m = nc.tensor.transpose(psQ[:, x, :], src.rearrange("p a b -> p (a b)"), ident[:, :])
                        m.then_inc(s_qt, 1)
                    elif kind == "sel scores":
                        (u, hh), (i, g) = arg, units[arg[0]]
                        n = HPG * u + hh
                        h = HPG * g + hh
                        nsel, _ = cols_of(i)
                        pe.wait_ge(s_ql, 5 * i + (3 if g == 0 else 5))
                        if n:
                            pe.wait_ge(s_ea, n)
                        q = qS[:, 1, h, :]
                        for c in range(0, nsel, 512):
                            e = min(c + 512, nsel)
                            nc.tensor.matmul(flatA[:, c:e], q, k_hi[:, 0, g, c:e], start=True, stop=False)
                            m = nc.tensor.matmul(flatA[:, c:e], q, k_lo[:, 0, g, c:e], start=False, stop=(e < nsel))
                        m = nc.tensor.matmul(flatA[:, nsel - P:nsel], identR[:, :], causal, start=False, stop=True)
                        m.then_inc(s_sa, 1)
                    elif kind == "win scores":
                        (u, hh), (i, g) = arg, units[arg[0]]
                        n = HPG * u + hh
                        h = HPG * g + hh
                        _, nwin = cols_of(i)
                        q = qS[:, 1, h, :]
                        if n:
                            pe.wait_ge(s_eb, n)
                        k0 = (i + 1) * P - nwin
                        for c in range(0, nwin, 512):
                            e = min(c + 512, nwin)
                            nc.tensor.matmul(flatB[:, c:e], q, k_hi[:, 1, g, k0 + c:k0 + e], start=True, stop=False)
                            nc.tensor.matmul(flatB[:, c:e], q, k_lo[:, 1, g, k0 + c:k0 + e], start=False, stop=False)
                            if c == 0 and nwin == WB * P:
                                nc.tensor.matmul(flatB[:, 0:P], identR[:, :], oldest, start=False, stop=True)
                        nc.tensor.matmul(flatB[:, nwin - P:nwin], identR[:, :], causal, start=False, stop=True)
                        out = flatB[:, B_CMP:B_CMP + NCH]
                        qc = qS[:, 0, h, :]
                        nc.tensor.matmul(out, qc, ck_hi[:, g, :], start=True, stop=False)
                        nc.tensor.matmul(out, qc, ck_lo[:, g, :], start=False, stop=False)
                        nc.tensor.matmul(out, identR[:, :], masksR[:, 2 * P + i * NCH:2 * P + (i + 1) * NCH],
                                         start=False, stop=True).then_inc(s_sb, 1)
                    elif kind == "block":
                        u, b = arg
                        n = base[u] + b
                        c0, branch, _ = key_blocks(u)[b]
                        w = NCH if branch == 2 else P
                        if b == 0:
                            pe.wait_ge(s_pv, HPG * (u + 1))
                            pe.wait_ge(s_pp, HPG * (u + 1))
                        if n >= 2:
                            pe.wait_ge(s_tl, n - 1)
                        for hh in range(HPG):
                            m = nc.tensor.transpose(psT[n % 2][0:w, hh, :], prob[:, HPG * (u % 2) + hh, c0:c0 + w],
                                                    ident[:, :])
                        m.then_inc(s_pt, 1)
                        if b >= LAG:
                            product(u, b - LAG)
                    elif kind == "drain":
                        n_b = len(key_blocks(arg[0]))
                        for b in range(max(0, n_b - LAG), n_b):
                            product(arg[0], b)

            @block.scalar
            def _(act):
                act.wait_ge(s_c, 32)
                nc.scalar.copy(identR[:, :], ident[:, :]).then_inc(s_mr, 1)
                nc.scalar.copy(masksR[:, :], prob[:, 0, 0:n_mask]).then_inc(s_mr, 1)
                act.wait_ge(s_mr, 2)
                nc.scalar.activation(gate[:, :, :, :].rearrange("p i h j -> p i (h j)"), yq[:, 0:n_tiles, C_GL:C_PI],
                                     ACT.Exp, scale=-1.0).then_inc(s_ge, 1)
                for kind, arg in steps():
                    if kind == "prep":
                        i, s = arg
                        p = prep_no(arg)
                        act.wait_ge(s_qt, p + 1)
                        if s == 0:
                            dst = k_hi[:, :, :, i * P:(i + 1) * P]
                            nc.scalar.copy(dst, psQ[:, :, :].rearrange("p (b g) t -> p b g t", b=2)).then_inc(s_qh, 1)
                            v = yq[:, i, C_KS:C_KS + 2 * KVW].rearrange("p (b u g d) -> p b u g d", b=2, u=2, g=NG)[:, :, 1]
                            nc.scalar.copy(v_st[:, :, i, :, 0:HD], v).then_inc(s_vh, 1)
                        else:
                            dst = qS[:, (s - 1) % 2, 4 * ((s - 1) // 2):4 * ((s - 1) // 2) + 4, :]
                            nc.scalar.mul(dst, psQ[:, :, :], SCALE).then_inc(s_qh, 1)
                    elif kind == "sel exp":
                        (u, hh), (i, g) = arg, units[arg[0]]
                        n = HPG * u + hh
                        slot = n % (2 * HPG)
                        nsel, _ = cols_of(i)
                        act.wait_ge(s_ma, n + 1)
                        nc.scalar.activation(prob[:, slot, 0:nsel], flatA[:, 0:nsel], ACT.Exp, bias=stat[:, slot, 1:2],
                                             accum_out=stat[:, slot, 5:6]).then_inc(s_ea, 1)
                    elif kind == "win exp":
                        (u, hh), (i, g) = arg, units[arg[0]]
                        n = HPG * u + hh
                        slot = n % (2 * HPG)
                        _, nwin = cols_of(i)
                        act.wait_ge(s_mb, n + 1)
                        nc.scalar.activation(prob[:, slot, P_WIN0:P_WIN0 + nwin], flatB[:, 0:nwin], ACT.Exp,
                                             bias=stat[:, slot, 2:3], accum_out=stat[:, slot, 6:7])
                        nc.scalar.activation(prob[:, slot, P_CMP0:P_COLS], flatB[:, B_CMP:B_CMP + NCH], ACT.Exp,
                                             bias=stat[:, slot, 0:1], accum_out=stat[:, slot, 4:5]).then_inc(s_eb, 1)
                    elif kind == "block":
                        u, b = arg
                        n = base[u] + b
                        w = NCH if key_blocks(u)[b][1] == 2 else P
                        act.wait_ge(s_pt, n + 1)
                        nc.scalar.copy(pT_hi[0:w, n % (LAG + 1), :], psT[n % 2][0:w].rearrange("p a b -> p (a b)")).then_inc(s_th, 1)
                    elif kind == "drain":
                        u = arg[0]
                        act.wait_ge(s_o, u + 1)
                        if u:
                            act.wait_ge(s_od, u)
                        halves = psO[:, :, :].rearrange("p (m e) t -> p e m t", e=2)
                        nc.scalar.copy(other[0:HD], halves[HD:P, 0])
                        nc.scalar.copy(other[HD:P], halves[0:HD, 1]).then_inc(s_oc, 1)

            @block.vector
            def _(dve):
                chain = Chain(dve, s_dve)
                flat_gate = gate[:, :, :, :].rearrange("p i h j -> p (i h j)")
                dve.wait_ge(s_ge, 1)
                chain(nc.vector.tensor_scalar(flat_gate, flat_gate, 1.0, None, ALU.add))
                nc.vector.reciprocal(flat_gate, flat_gate).then_inc(s_g, 1)
                dve.wait_ge(s_g, 1)
                for kind, arg in steps():
                    if kind == "prep":
                        i, s = arg
                        p = prep_no(arg)
                        dve.wait_ge(s_qh, p + 1)
                        if s == 0:
                            dve.wait_ge(s_vh, i + 1)
                            v = yq[:, i, C_KS:C_KS + 2 * KVW].rearrange("p (b u g d) -> p b u g d", b=2, u=2, g=NG)[:, :, 1]
                            nc.vector.tensor_tensor(v_st[:, :, i, :, HD:P], v, v_st[:, :, i, :, 0:HD].bitcast(F32),
                                                    ALU.subtract)
                            nc.vector.tensor_tensor(k_lo[:, :, :, i * P:(i + 1) * P],
                                                    psQ[:, :, :].rearrange("p (b g) t -> p b g t", b=2),
                                                    k_hi[:, :, :, i * P:(i + 1) * P].bitcast(F32),
                                                    ALU.subtract).then_inc(s_ql, 1)
                        else:
                            q = qS[HD:P, (s - 1) % 2, 4 * ((s - 1) // 2):4 * ((s - 1) // 2) + 4, :]
                            nc.vector.scalar_tensor_tensor(q, psQ[HD:P, :, :], SCALE, q.bitcast(F32), ALU.mult,
                                                           ALU.subtract).then_inc(s_ql, 1)
                    elif kind == "sel max":
                        (u, hh), (i, g) = arg, units[arg[0]]
                        n = HPG * u + hh
                        st = stat[:, n % (2 * HPG), :]
                        nsel, _ = cols_of(i)
                        dve.wait_ge(s_sa, n + 1)
                        nc.vector.reduce_max(st[:, 1:2], flatA[:, 0:nsel], AX.X, negate=True).then_inc(s_ma, 1)
                    elif kind == "win max":
                        (u, hh), (i, g) = arg, units[arg[0]]
                        n = HPG * u + hh
                        st = stat[:, n % (2 * HPG), :]
                        _, nwin = cols_of(i)
                        dve.wait_ge(s_sb, n + 1)
                        m = nc.vector.reduce_max(st[:, 2:3], flatB[:, 0:nwin], AX.X, negate=True)
                        m = nc.vector.reduce_max(st[:, 0:1], flatB[:, B_CMP:B_CMP + NCH], AX.X, negate=True)
                        if i == 0:
                            chain(m)
                            m = nc.vector.tensor_scalar(st[:, 0:1], st[:, 0:1], 1e20, None, ALU.min)
                        m.then_inc(s_mb, 1)
                    elif kind == "scale":
                        (u, hh), (i, g) = arg, units[arg[0]]
                        n = HPG * u + hh
                        slot = n % (2 * HPG)
                        st = stat[:, slot, :]
                        dve.wait_ge(s_eb, n + 1)
                        if i == 0:
                            chain(nc.vector.tensor_scalar(st[:, 4:7], st[:, 4:7], 1e-30, None, ALU.max))
                        chain(nc.vector.reciprocal(st[:, 8:11], st[:, 4:7]))
                        nc.vector.tensor_tensor(st[:, 12:15], st[:, 8:11], gate[:, i, HPG * g + hh, :], ALU.mult
                                                ).then_inc(s_f, 1)
                        dve.wait_ge(s_f, n + 1)
                        nc.vector.tensor_scalar(prob[:, slot, 0:cols_of(i)[0]], prob[:, slot, 0:cols_of(i)[0]],
                                                st[:, 13:14], None, ALU.mult).then_inc(s_pv, 1)
                    elif kind == "block":
                        u, b = arg
                        n = base[u] + b
                        w = NCH if key_blocks(u)[b][1] == 2 else P
                        dve.wait_ge(s_th, n + 1)
                        nc.vector.tensor_tensor(pT_lo[0:w, n % (LAG + 1), :], psT[n % 2][0:w].rearrange("p a b -> p (a b)"),
                                                pT_hi[0:w, n % (LAG + 1), :].bitcast(F32), ALU.subtract).then_inc(s_tl, 1)
                    elif kind == "drain":
                        u = arg[0]
                        i, g = units[u]
                        dve.wait_ge(s_oc, u + 1)
                        halves = psO[:, :, :].rearrange("p (m e) t -> p e m t", e=2)
                        dst = aT[:, 2 * g:2 * g + 2, i * P:(i + 1) * P]
                        nc.vector.tensor_tensor(dst[0:HD], halves[0:HD, 0], other[0:HD], ALU.add)
                        nc.vector.tensor_tensor(dst[HD:P], halves[HD:P, 1], other[HD:P], ALU.add).then_inc(s_od, 1)


def split_weight_loads(sp, raw, srcs, s_w, s_hi, s_lo):
    for c, src in enumerate(srcs):
        if c >= 2:
            sp.wait_ge(s_hi, c - 1)
            sp.wait_ge(s_lo, c - 1)
        sp.dma_start(raw[:, c % 2, 0:src.shape[-1]], src).then_inc(s_w[c % 2], 16)


def mix_out(nc, t, x_of, aT, mT, x):
    with ExitStack() as ctx:
        ph = Phase(nc, ctx, "out")
        raw = ph.sb("raw", [P, 2, DM])
        w_hi = ph.sb("w_hi", [P, KC, DM], F32R)
        w_lo = ph.sb("w_lo", [P, KC, DM], F32R)
        gT = ph.sb("gT", [P, KC])
        ones = ph.sb("ones", [P, 1])
        sq = ph.sb("sq", [P, 2, KC, P])
        mixg = ph.sb("mixg", [P, KC, P])
        m_hi = ph.sb("m_hi", [P, 2, KC, P], F32R)
        m_lo = ph.sb("m_lo", [P, 2, KC, P], F32R)
        stat = ph.sb("stat", [P, NT, 6])
        acc = [[ph.ps(f"acc{k}{h}", [P, 512]) for h in range(2)] for k in range(2)]
        psN = [ph.ps(f"psN{k}", [P, 2]) for k in range(2)]
        s_w = [ph.sem("weights_loaded_even"), ph.sem("weights_loaded_odd")]
        s_hi = ph.sem("weight_hi_made")
        s_lo = ph.sem("weight_lo_made")
        s_c = ph.sem("constants_loaded")
        s_one = ph.sem("ones_written")
        s_x = ph.sem("x_loaded")
        s_sq = ph.sem("squares_made")
        s_n = ph.sem("squares_summed")
        s_ms = ph.sem("mean_squares_made")
        s_sd = ph.sem("roots_taken")
        s_mg = ph.sem("gain_applied")
        s_mh = ph.sem("mix_hi_made")
        s_ml = ph.sem("mix_lo_made")
        s_mm = ph.sem("half_multiplied")
        s_y = ph.sem("half_added")
        s_dve = ph.sem("vector_chain")

        def cols(j):
            return slice(j * P, j * P + rows_of(j))

        with nc.Block() as block:

            @block.sync
            def _(sp):
                split_weight_loads(sp, raw, [t["w_out"][0][c * P:(c + 1) * P, :] for c in range(KC)], s_w, s_hi, s_lo)

            @block.gpsimd
            def _(pool):
                nc.gpsimd.memset(ones[:, :], 1.0).then_inc(s_one, 1)
                for k, name in enumerate(("g_attn_out", "pool_scale")):
                    pool.dma_start(gT[:, 4 * k:4 * k + 4], t[name][0].rearrange("(c p) -> p c", p=P),
                                   allow_slow_non_contiguous=True).then_inc(s_c, 16)
                for j in range(NT):
                    pool.dma_start(x[0:rows_of(j), j, :], x_of(j)).then_inc(s_x, 16)

            @block.tensor
            def _(pe):
                pe.wait_ge(s_one, 1)

                def sums(j):
                    r = rows_of(j)
                    pe.wait_ge(s_sq, j + 1)
                    if j >= 2:
                        pe.wait_ge(s_ms, j - 1)
                    for k in range(2):
                        for c in range(4):
                            m = nc.tensor.matmul(psN[j % 2][0:r, k:k + 1], sq[:, j % 2, 4 * k + c, 0:r], ones[:, :],
                                                 start=(c == 0), stop=(c == 3))
                    m.then_inc(s_n, 1)

                sums(0)
                for j in range(NT):
                    r = rows_of(j)
                    pe.wait_ge(s_ml, j + 1)
                    for h in range(2):
                        if j:
                            pe.wait_ge(s_y, 2 * (j - 1) + h + 1)
                        for k in range(2):
                            for c in range(4):
                                cc = 4 * k + c
                                if j == 0 and h == 0:
                                    pe.wait_ge(s_lo, cc + 1)
                                for n_pass, (a, b) in enumerate(((m_hi, w_hi), (m_hi, w_lo), (m_lo, w_hi))):
                                    m = nc.tensor.matmul(acc[k][h][0:r, :], a[:, j % 2, cc, 0:r],
                                                         b[:, cc, 512 * h:512 * h + 512],
                                                         start=(c == 0 and n_pass == 0), stop=(c == 3 and n_pass == 2))
                        m.then_inc(s_mm, 1)
                    if j + 1 < NT:
                        sums(j + 1)

            @block.scalar
            def _(act):
                def squares(j):
                    r = rows_of(j)
                    if j >= 2:
                        act.wait_ge(s_n, j - 1)
                    nc.scalar.activation(sq[:, j % 2, 0:4, 0:r], aT[:, :, cols(j)], ACT.Square)
                    nc.scalar.activation(sq[:, j % 2, 4:8, 0:r], mT[:, :, cols(j)], ACT.Square).then_inc(s_sq, 1)

                def hi(j):
                    r = rows_of(j)
                    act.wait_ge(s_mg, j + 1)
                    if j >= 2:
                        act.wait_ge(s_mm, 2 * (j - 1))
                    nc.scalar.copy(m_hi[:, j % 2, :, 0:r], mixg[:, :, 0:r]).then_inc(s_mh, 1)

                squares(0)
                hi(0)
                for c in range(KC):
                    act.wait_ge(s_w[c % 2], 16 * (c // 2 + 1))
                    nc.scalar.copy(w_hi[:, c, :], raw[:, c % 2, :]).then_inc(s_hi, 1)
                for j in range(NT):
                    r = rows_of(j)
                    if j + 1 < NT:
                        squares(j + 1)
                        hi(j + 1)
                    act.wait_ge(s_ms, j + 1)
                    nc.scalar.activation(stat[0:r, j, 2:4], stat[0:r, j, 0:2], ACT.Sqrt).then_inc(s_sd, 1)

            @block.vector
            def _(dve):
                chain = Chain(dve, s_dve)

                def gains(j):
                    r = rows_of(j)
                    if j:
                        dve.wait_ge(s_ml, j)
                    for k, src in enumerate((aT, mT)):
                        g = gT[:, 4 * k:4 * k + 4].unsqueeze(2).broadcast_to([P, 4, r])
                        m = nc.vector.tensor_tensor(mixg[:, 4 * k:4 * k + 4, 0:r], src[:, :, cols(j)], g, ALU.mult)
                    m.then_inc(s_mg, 1)

                def lo(j):
                    r = rows_of(j)
                    dve.wait_ge(s_mh, j + 1)
                    nc.vector.tensor_tensor(m_lo[:, j % 2, :, 0:r], mixg[:, :, 0:r], m_hi[:, j % 2, :, 0:r].bitcast(F32),
                                            ALU.subtract).then_inc(s_ml, 1)

                dve.wait_ge(s_c, 32)
                gains(0)
                lo(0)
                for c in range(KC):
                    dve.wait_ge(s_hi, c + 1)
                    nc.vector.tensor_tensor(w_lo[:, c, :], raw[:, c % 2, :], w_hi[:, c, :].bitcast(F32),
                                            ALU.subtract).then_inc(s_lo, 1)
                dve.wait_ge(s_x, 16 * NT)
                for j in range(NT):
                    r = rows_of(j)
                    if j + 1 < NT:
                        gains(j + 1)
                        lo(j + 1)
                    dve.wait_ge(s_n, j + 1)
                    nc.vector.tensor_scalar(stat[0:r, j, 0:2], psN[j % 2][0:r, :], 1.0 / AW, EPS, ALU.mult,
                                            ALU.add).then_inc(s_ms, 1)
                    dve.wait_ge(s_sd, j + 1)
                    chain(nc.vector.reciprocal(stat[0:r, j, 4:6], stat[0:r, j, 2:4]))
                    for h in range(2):
                        xh = x[0:r, j, 512 * h:512 * h + 512]
                        dve.wait_ge(s_mm, 2 * j + h + 1)
                        chain(nc.vector.scalar_tensor_tensor(xh, acc[0][h][0:r, :], stat[0:r, j, 4:5], xh, ALU.mult,
                                                             ALU.add))
                        nc.vector.scalar_tensor_tensor(xh, acc[1][h][0:r, :], stat[0:r, j, 5:6], xh, ALU.mult,
                                                       ALU.add).then_inc(s_y, 1)


def cross_attention(nc, t, o, x):
    scale = MD ** -0.5
    n_kb = NMEM // P
    i_s = NT - 1
    R = MH * DT
    with ExitStack() as ctx:
        ph = Phase(nc, ctx, "cross")
        raw = ph.sb("raw", [P, 2, DM])
        wq_hi = ph.sb("wq_hi", [P, KC, AW], F32R)
        wq_lo = ph.sb("wq_lo", [P, KC, AW], F32R)
        wo_hi = ph.sb("wo_hi", [P, MH, DM], F32R)
        wo_lo = ph.sb("wo_lo", [P, MH, DM], F32R)
        ident = ph.sb("ident", [P, P])
        gT = ph.sb("gT", [P, KC])
        xs = ph.sb("xs", [P, DM])
        xg = ph.sb("xg", [P, KC, P])
        xT_hi = ph.sb("xT_hi", [P, KC, P], F32R)
        xT_lo = ph.sb("xT_lo", [P, KC, P], F32R)
        stat = ph.sb("stat", [P, NT, 4])
        sm = ph.sb("sm", [P, 2, 4, MH])
        mem = ph.sb("mem", [P, 2, n_kb, 2 * AW])
        kT_hi = ph.sb("kT_hi", [P, n_kb, MH, P], F32R)
        kT_lo = ph.sb("kT_lo", [P, n_kb, MH, P], F32R)
        v_hi = ph.sb("v_hi", [P, n_kb, AW], F32R)
        v_lo = ph.sb("v_lo", [P, n_kb, AW], F32R)
        qm = ph.sb("qm", [P, AW])
        qT_hi = ph.sb("qT_hi", [P, MH, P], F32R)
        qT_lo = ph.sb("qT_lo", [P, MH, P], F32R)
        prob = ph.sb("prob", [P, MH, NMEM])
        pT_hi = ph.sb("pT_hi", [P, n_kb, MH, P], F32R)
        pT_lo = ph.sb("pT_lo", [P, n_kb, MH, P], F32R)
        oT_hi = ph.sb("oT_hi", [P, MH, P], F32R)
        oT_lo = ph.sb("oT_lo", [P, MH, P], F32R)
        q_z = ph.sb("q_z", [P, DB, MH, R])
        kT_s = ph.sb("kT_s", [P, 2, n_kb, MH, P])
        pT_s = ph.sb("pT_s", [P, 2, n_kb, R])
        own = ph.sb("own", [R, AW])
        o_m = ph.sb("o_m", [R, 2, AW])
        pick = ph.sb("pick", [R, DB, DB * DT])
        psT = [ph.ps(f"psT{k}", [P, 4, P]) for k in range(2)]
        psQ = ph.ps("psQ", [P, 512])
        psS = ph.ps("psS", [P, MH, NMEM])
        psO = ph.ps("psO", [P, 4, P])
        psY = [ph.ps(f"psY{k}", [P, 512]) for k in range(2)]
        s_w = [ph.sem("weights_loaded_even"), ph.sem("weights_loaded_odd")]
        s_hi = ph.sem("weight_hi_made")
        s_lo = ph.sem("weight_lo_made")
        s_c = ph.sem("constants_loaded")
        s_mem = [ph.sem("memory_loaded_even"), ph.sem("memory_loaded_odd")]
        s_mt = ph.sem("memory_transposed")
        s_mh = ph.sem("memory_hi_made")
        s_mlo = ph.sem("memory_lo_made")
        s_sum = ph.sem("squares_summed")
        s_ms = ph.sem("mean_square_made")
        s_sd = ph.sem("root_taken")
        s_xn = ph.sem("x_scaled")
        s_tr = ph.sem("x_transposed")
        s_xg = ph.sem("gain_applied")
        s_th = ph.sem("xT_hi_made")
        s_tl = ph.sem("xT_lo_made")
        s_q = ph.sem("q_multiplied")
        s_qc = ph.sem("q_copied")
        s_qt = ph.sem("q_transposed")
        s_qh = ph.sem("q_hi_made")
        s_ql = ph.sem("q_lo_made")
        s_s = ph.sem("scores_made")
        s_m = ph.sem("maxima_made")
        s_e = ph.sem("exps_made")
        s_p = ph.sem("probs_scaled")
        s_pt = ph.sem("probs_transposed")
        s_ph = ph.sem("pT_hi_made")
        s_pl = ph.sem("pT_lo_made")
        s_o = ph.sem("outputs_made")
        s_oh = ph.sem("oT_hi_made")
        s_ol = ph.sem("oT_lo_made")
        s_y = ph.sem("products_made")
        s_x = ph.sem("x_updated")
        s_z = ph.sem("sample_q_zeroed")
        s_zq = ph.sem("sample_q_placed")
        s_kt = ph.sem("sample_keys_transposed")
        s_kc = ph.sem("sample_keys_copied")
        s_pc = ph.sem("sample_pT_copied")
        s_om = ph.sem("own_heads_kept")
        s_ob = ph.sem("sample_outputs_gathered")
        s_oc = ph.sem("sample_outputs_copied")
        s_ot = ph.sem("sample_outputs_transposed")
        s_dve = ph.sem("vector_chain")
        weights = ([(t["w_mq"][0][c * P:(c + 1) * P, :], wq_hi[:, c, :], wq_lo[:, c, :]) for c in range(KC)]
                   + [(t["w_mo"][0][c * P:(c + 1) * P, :], wo_hi[:, c, :], wo_lo[:, c, :]) for c in range(MH)])
        pm = o["p_mem_kv"][0, 0].rearrange("(k p) u h d -> p k (u h d)", p=P)
        cm = t["cache_mem_kv"][0].rearrange("b (k p) u h d -> b p k (u h d)", p=P)
        n_prompt = NT - 1
        with nc.Block() as block:

            @block.sync
            def _(sp):
                sp.dma_start(mem[:, 0], pm).then_inc(s_mem[0], 16)
                sp.dma_start(mem[:, 1], cm[0]).then_inc(s_mem[1], 16)
                split_weight_loads(sp, raw, [w[0] for w in weights], s_w, s_hi, s_lo)
                for b in range(1, DB):
                    m = b + 1
                    if m == 2:
                        sp.wait_ge(s_mh, 3)
                        sp.wait_ge(s_mlo, 3)
                    else:
                        sp.wait_ge(s_o, n_prompt + b - 1)
                    sp.dma_start(mem[:, m % 2], cm[b]).then_inc(s_mem[m % 2], 16)

            @block.gpsimd
            def _(pool):
                pool.dma_start(gT[:, :], t["g_norm2"][0].rearrange("(c p) -> p c", p=P),
                               allow_slow_non_contiguous=True).then_inc(s_c, 16)
                pool.dma_start(ident[:, :], t["k_ident"]).then_inc(s_c, 16)
                pool.dma_start(own[:, :], t["k_own"]).then_inc(s_c, 16)
                pool.dma_start(pick[:, :, :], t["k_pick"]).then_inc(s_c, 16)
                nc.gpsimd.memset(q_z[:, :, :, :], 0.0).then_inc(s_z, 1)

            @block.tensor
            def _(pe):
                def front(j):
                    r = rows_of(j)
                    pe.wait_ge(s_xn, j + 1)
                    for c in range(KC):
                        m = nc.tensor.transpose(psT[c // 4][:, c % 4, 0:r], xs[0:r, c * P:(c + 1) * P], ident[0:r, 0:r])
                        if c % 4 == 3:
                            m.then_inc(s_tr, 1)
                    pe.wait_ge(s_tl, 2 * (j + 1))
                    if j:
                        pe.wait_ge(s_qc, j)
                    for c in range(KC):
                        if j == 0:
                            pe.wait_ge(s_lo, c + 1)
                        for n_pass, (a, b) in enumerate(((xT_hi, wq_hi), (xT_hi, wq_lo), (xT_lo, wq_hi))):
                            m = nc.tensor.matmul(psQ[0:r, :], a[:, c, 0:r], b[:, c, :], start=(c == 0 and n_pass == 0),
                                                 stop=(c == KC - 1 and n_pass == 2))
                    m.then_inc(s_q, 1)

                def q_transposes(j):
                    r = rows_of(j)
                    pe.wait_ge(s_qc, j + 1)
                    for h in range(MH):
                        m = nc.tensor.transpose(psT[0][:, h, 0:r], qm[0:r, h * MD:(h + 1) * MD], ident[0:r, 0:r])
                    m.then_inc(s_qt, 1)

                def back(j):
                    r = rows_of(j)
                    pe.wait_ge(s_ol, j + 1)
                    if j:
                        pe.wait_ge(s_x, 2 * j)
                    if j == 0:
                        pe.wait_ge(s_lo, len(weights))
                    for half in range(2):
                        for h in range(MH):
                            for n_pass, (a, b) in enumerate(((oT_hi, wo_hi), (oT_hi, wo_lo), (oT_lo, wo_hi))):
                                m = nc.tensor.matmul(psY[half][0:r, :], a[:, h, 0:r], b[:, h, 512 * half:512 * half + 512],
                                                     start=(h == 0 and n_pass == 0), stop=(h == MH - 1 and n_pass == 2))
                        m.then_inc(s_y, 1)

                pe.wait_ge(s_c, 64)
                pe.wait_ge(s_mem[0], 16)
                for kb in range(n_kb):
                    for h in range(MH):
                        m = nc.tensor.transpose(psT[kb][:, h, :], mem[:, 0, kb, h * MD:(h + 1) * MD], ident[:, :])
                    m.then_inc(s_mt, 1)
                pe.wait_ge(s_mlo, 2)
                front(0)
                for j in range(n_prompt):
                    q_transposes(j)
                    pe.wait_ge(s_ql, j + 1)
                    if j:
                        pe.wait_ge(s_e, MH * j)
                    for h in range(MH):
                        for n_pass, (a, b) in enumerate(((qT_hi, kT_hi), (qT_hi, kT_lo), (qT_lo, kT_hi))):
                            m = nc.tensor.matmul(psS[:, h, :].rearrange("p (k t) -> p k t", k=n_kb), a[:, h, :],
                                                 b[:, :, h, :], start=(n_pass == 0), stop=(n_pass == 2))
                    m.then_inc(s_s, 1)
                    front(j + 1)
                    pe.wait_ge(s_p, j + 1)
                    for kb in range(n_kb):
                        for h in range(MH):
                            m = nc.tensor.transpose(psT[kb][:, h, :], prob[:, h, kb * P:(kb + 1) * P], ident[:, :])
                        m.then_inc(s_pt, 1)
                    pe.wait_ge(s_mlo, 3)
                    pe.wait_ge(s_pl, n_kb * (j + 1))
                    if j:
                        pe.wait_ge(s_ol, j)
                    for h in range(MH):
                        for kb in range(n_kb):
                            for n_pass, (a, b) in enumerate(((v_hi, pT_hi), (v_lo, pT_hi), (v_hi, pT_lo))):
                                m = nc.tensor.matmul(psO[:, h, :], a[:, kb, h * MD:(h + 1) * MD], b[:, kb, h, :],
                                                     start=(kb == 0 and n_pass == 0), stop=(kb == n_kb - 1 and n_pass == 2))
                    m.then_inc(s_o, 1)
                    back(j)
                q_transposes(i_s)
                pe.wait_ge(s_zq, 1)

                def sample_keys(b):
                    pe.wait_ge(s_mem[(b + 1) % 2], 16 * ((b + 1) // 2 + 1))
                    if b:
                        pe.wait_ge(s_pc, b - 1) if b > 1 else None
                    for kb in range(n_kb):
                        if b:
                            pe.wait_ge(s_kc, n_kb * (b - 1) + kb + 1)
                        for h in range(MH):
                            m = nc.tensor.transpose(psT[kb][:, h, :], mem[:, (b + 1) % 2, kb, h * MD:(h + 1) * MD],
                                                    ident[:, :])
                        m.then_inc(s_kt, 1)

                sample_keys(0)
                for b in range(DB):
                    pe.wait_ge(s_kc, n_kb * (b + 1))
                    if b:
                        pe.wait_ge(s_e, MH * n_prompt + b)
                    else:
                        pe.wait_ge(s_e, MH * n_prompt)
                    for h in range(MH):
                        m = nc.tensor.matmul(psS[0:R, 0, :].rearrange("p (k t) -> p k t", k=n_kb), q_z[:, b, h, :],
                                             kT_s[:, b % 2, :, h, :], start=(h == 0), stop=(h == MH - 1))
                    m.then_inc(s_s, 1)
                    if b + 1 < DB:
                        sample_keys(b + 1)
                    pe.wait_ge(s_p, n_prompt + b + 1)
                    if b:
                        pe.wait_ge(s_x, 2 * n_prompt)
                    else:
                        pe.wait_ge(s_x, 2 * n_prompt)
                    for kb in range(n_kb):
                        m = nc.tensor.transpose(psY[0][:, kb * R:(kb + 1) * R], prob[0:R, 0, kb * P:(kb + 1) * P],
                                                ident[0:R, 0:R])
                    m.then_inc(s_pt, 1)
                    pe.wait_ge(s_pc, b + 1)
                    if b:
                        pe.wait_ge(s_om, b)
                    else:
                        pe.wait_ge(s_ol, n_prompt)
                    out = psO[0:R, :, :].rearrange("p a b -> p (a b)")
                    for kb in range(n_kb):
                        m = nc.tensor.matmul(out, pT_s[:, b % 2, kb, :], mem[:, (b + 1) % 2, kb, AW:2 * AW],
                                             start=(kb == 0), stop=(kb == n_kb - 1))
                    m.then_inc(s_o, 1)
                    pe.wait_ge(s_om, b + 1)
                    m = nc.tensor.matmul(psQ[0:DB * DT, :], pick[:, b, :], o_m[:, b % 2, :], start=(b == 0),
                                         stop=(b == DB - 1), skip_group_check=True)
                m.then_inc(s_ob, 1)
                pe.wait_ge(s_oc, 1)
                r = DB * DT
                for h in range(MH):
                    m = nc.tensor.transpose(psO[:, h, 0:r], qm[0:r, h * MD:(h + 1) * MD], ident[0:r, 0:r])
                m.then_inc(s_ot, 1)
                back(i_s)

            @block.scalar
            def _(act):
                def norm(j):
                    r = rows_of(j)
                    if j:
                        act.wait_ge(s_tr, 2 * j)
                    nc.scalar.activation(xs[0:r, :], x[0:r, j, :], ACT.Square,
                                         accum_out=stat[0:r, j, 0:1]).then_inc(s_sum, 1)
                    act.wait_ge(s_ms, j + 1)
                    nc.scalar.activation(stat[0:r, j, 2:3], stat[0:r, j, 1:2], ACT.Sqrt).then_inc(s_sd, 1)

                def hi(j):
                    r = rows_of(j)
                    for h in range(2):
                        act.wait_ge(s_xg, 2 * j + h + 1)
                        if j:
                            act.wait_ge(s_q, j)
                        nc.scalar.copy(xT_hi[:, 4 * h:4 * h + 4, 0:r], xg[:, 4 * h:4 * h + 4, 0:r]).then_inc(s_th, 1)

                norm(0)
                for kb in range(n_kb):
                    act.wait_ge(s_mt, kb + 1)
                    nc.scalar.copy(kT_hi[:, kb], psT[kb][:, :, :]).then_inc(s_mh, 1)
                nc.scalar.copy(v_hi[:, :, :], mem[:, 0, :, AW:2 * AW]).then_inc(s_mh, 1)
                hi(0)
                for c, (src, whi, _) in enumerate(weights):
                    act.wait_ge(s_w[c % 2], 16 * (c // 2 + 1))
                    nc.scalar.copy(whi, raw[:, c % 2, 0:src.shape[-1]]).then_inc(s_hi, 1)

                def q_copy(j):
                    r = rows_of(j)
                    act.wait_ge(s_q, j + 1)
                    if j:
                        act.wait_ge(s_qt, j)
                    nc.scalar.copy(qm[0:r, :], psQ[0:r, :]).then_inc(s_qc, 1)

                q_copy(0)
                for j in range(n_prompt):
                    act.wait_ge(s_qt, j + 1)
                    nc.scalar.copy(qT_hi[:, :, :], psT[0][:, :, :]).then_inc(s_qh, 1)
                    norm(j + 1)
                    hi(j + 1)
                    act.wait_ge(s_m, j + 1)
                    for h in range(MH):
                        nc.scalar.activation(prob[:, h, :], psS[:, h, :], ACT.Exp, bias=sm[:, j % 2, 1, h:h + 1],
                                             scale=scale, accum_out=sm[:, j % 2, 2, h:h + 1]).then_inc(s_e, 1)
                    for kb in range(n_kb):
                        act.wait_ge(s_pt, n_kb * j + kb + 1)
                        nc.scalar.copy(pT_hi[:, kb], psT[kb][:, :, :]).then_inc(s_ph, 1)
                    q_copy(j + 1)
                    act.wait_ge(s_o, j + 1)
                    if j:
                        act.wait_ge(s_y, 2 * j)
                    nc.scalar.copy(oT_hi[:, :, :], psO[:, :, :]).then_inc(s_oh, 1)
                for b in range(DB):
                    for kb in range(n_kb):
                        act.wait_ge(s_kt, n_kb * b + kb + 1)
                        nc.scalar.copy(kT_s[:, b % 2, kb], psT[kb][:, :, :]).then_inc(s_kc, 1)
                    act.wait_ge(s_m, n_prompt + b + 1)
                    nc.scalar.activation(prob[0:R, 0, :], psS[0:R, 0, :], ACT.Exp, bias=sm[0:R, b % 2, 1, 0:1],
                                         scale=scale, accum_out=sm[0:R, b % 2, 2, 0:1]).then_inc(s_e, 1)
                    act.wait_ge(s_pt, n_kb * n_prompt + b + 1)
                    nc.scalar.copy(pT_s[:, b % 2].rearrange("p k r -> p (k r)"), psY[0][:, 0:n_kb * R]).then_inc(s_pc, 1)
                act.wait_ge(s_ob, 1)
                r = DB * DT
                nc.scalar.copy(qm[0:r, :], psQ[0:r, :]).then_inc(s_oc, 1)
                act.wait_ge(s_ot, 1)
                nc.scalar.copy(oT_hi[:, :, 0:r], psO[:, :, 0:r]).then_inc(s_oh, 1)

            @block.vector
            def _(dve):
                chain = Chain(dve, s_dve)

                def norm(j):
                    r = rows_of(j)
                    dve.wait_ge(s_sum, j + 1)
                    nc.vector.tensor_scalar(stat[0:r, j, 1:2], stat[0:r, j, 0:1], 1.0 / DM, EPS, ALU.mult,
                                            ALU.add).then_inc(s_ms, 1)
                    dve.wait_ge(s_sd, j + 1)
                    chain(nc.vector.reciprocal(stat[0:r, j, 3:4], stat[0:r, j, 2:3]))
                    nc.vector.tensor_scalar(xs[0:r, :], x[0:r, j, :], stat[0:r, j, 3:4], None, ALU.mult).then_inc(s_xn, 1)

                def gain_and_lo(j):
                    r = rows_of(j)
                    for h in range(2):
                        dve.wait_ge(s_tr, 2 * j + h + 1)
                        g4 = gT[:, 4 * h:4 * h + 4].unsqueeze(2).broadcast_to([P, 4, r])
                        nc.vector.tensor_tensor(xg[:, 4 * h:4 * h + 4, 0:r], psT[h][:, :, 0:r], g4, ALU.mult).then_inc(s_xg, 1)
                    for h in range(2):
                        dve.wait_ge(s_th, 2 * j + h + 1)
                        nc.vector.tensor_tensor(xT_lo[:, 4 * h:4 * h + 4, 0:r], xg[:, 4 * h:4 * h + 4, 0:r],
                                                xT_hi[:, 4 * h:4 * h + 4, 0:r].bitcast(F32), ALU.subtract).then_inc(s_tl, 1)

                def add_y(j):
                    r = rows_of(j)
                    for half in range(2):
                        dve.wait_ge(s_y, 2 * j + half + 1)
                        xh = x[0:r, j, 512 * half:512 * half + 512]
                        nc.vector.tensor_tensor(xh, psY[half][0:r, :], xh, ALU.add).then_inc(s_x, 1)

                norm(0)
                for kb in range(n_kb):
                    dve.wait_ge(s_mh, kb + 1)
                    nc.vector.tensor_tensor(kT_lo[:, kb], psT[kb][:, :, :], kT_hi[:, kb].bitcast(F32),
                                            ALU.subtract).then_inc(s_mlo, 1)
                dve.wait_ge(s_mh, 3)
                nc.vector.tensor_tensor(v_lo[:, :, :], mem[:, 0, :, AW:2 * AW], v_hi[:, :, :].bitcast(F32),
                                        ALU.subtract).then_inc(s_mlo, 1)
                dve.wait_ge(s_c, 64)
                gain_and_lo(0)
                for c, (src, whi, wlo) in enumerate(weights):
                    dve.wait_ge(s_hi, c + 1)
                    nc.vector.tensor_tensor(wlo, raw[:, c % 2, 0:src.shape[-1]], whi.bitcast(F32),
                                            ALU.subtract).then_inc(s_lo, 1)
                for j in range(n_prompt):
                    dve.wait_ge(s_qh, j + 1)
                    nc.vector.tensor_tensor(qT_lo[:, :, :], psT[0][:, :, :], qT_hi[:, :, :].bitcast(F32),
                                            ALU.subtract).then_inc(s_ql, 1)
                    norm(j + 1)
                    gain_and_lo(j + 1)
                    dve.wait_ge(s_s, j + 1)
                    chain(nc.vector.tensor_reduce(sm[:, j % 2, 0, :], psS[:, :, :], AX.X, ALU.max, negate=True))
                    nc.vector.tensor_scalar(sm[:, j % 2, 1, :], sm[:, j % 2, 0, :], scale, None, ALU.mult).then_inc(s_m, 1)
                    dve.wait_ge(s_e, MH * (j + 1))
                    chain(nc.vector.reciprocal(sm[:, j % 2, 3, :], sm[:, j % 2, 2, :]))
                    f = sm[:, j % 2, 3, :].unsqueeze(2).broadcast_to([P, MH, NMEM])
                    nc.vector.tensor_tensor(prob[:, :, :], prob[:, :, :], f, ALU.mult).then_inc(s_p, 1)
                    for kb in range(n_kb):
                        dve.wait_ge(s_ph, n_kb * j + kb + 1)
                        nc.vector.tensor_tensor(pT_lo[:, kb], psT[kb][:, :, :], pT_hi[:, kb].bitcast(F32),
                                                ALU.subtract).then_inc(s_pl, 1)
                    dve.wait_ge(s_oh, j + 1)
                    nc.vector.tensor_tensor(oT_lo[:, :, :], psO[:, :, :], oT_hi[:, :, :].bitcast(F32),
                                            ALU.subtract).then_inc(s_ol, 1)
                    add_y(j)
                dve.wait_ge(s_z, 1)
                dve.wait_ge(s_qt, n_prompt + 1)
                for h in range(MH):
                    m = nc.vector.tensor_copy(q_z[:, :, h, h * DT:(h + 1) * DT],
                                              psT[0][:, h, 0:DB * DT].rearrange("p (b s) -> p b s", b=DB))
                m.then_inc(s_zq, 1)
                for b in range(DB):
                    st = sm[0:R, b % 2]
                    dve.wait_ge(s_s, n_prompt + b + 1)
                    chain(nc.vector.reduce_max(st[:, 0, 0:1], psS[0:R, 0, :], AX.X, negate=True))
                    nc.vector.tensor_scalar(st[:, 1, 0:1], st[:, 0, 0:1], scale, None, ALU.mult).then_inc(s_m, 1)
                    dve.wait_ge(s_e, MH * n_prompt + b + 1)
                    chain(nc.vector.reciprocal(st[:, 3, 0:1], st[:, 2, 0:1]))
                    nc.vector.tensor_scalar(prob[0:R, 0, :], prob[0:R, 0, :], st[:, 3, 0:1], None, ALU.mult).then_inc(s_p, 1)
                    dve.wait_ge(s_o, n_prompt + b + 1)
                    nc.vector.tensor_tensor(o_m[:, b % 2, :], psO[0:R, :, :].rearrange("p a b -> p (a b)"), own[:, :],
                                            ALU.mult).then_inc(s_om, 1)
                r = DB * DT
                dve.wait_ge(s_oh, n_prompt + 1)
                nc.vector.tensor_tensor(oT_lo[:, :, 0:r], psO[:, :, 0:r], oT_hi[:, :, 0:r].bitcast(F32),
                                        ALU.subtract).then_inc(s_ol, 1)
                add_y(i_s)


def mlp(nc, t, o, x, y_of, s_st):
    groups = [(0, 1, 2), (3, 4, 5), (6, 7, 8)]
    n_f = DFF // P
    PF = 2
    with ExitStack() as ctx:
        ph = Phase(nc, ctx, "mlp")
        ident = ph.sb("ident", [P, P])
        gT = ph.sb("gT", [P, KC])
        g_last = ph.sb("g_last", [P, DM])
        xs = ph.sb("xs", [P, DM])
        xg = ph.sb("xg", [P, 4, P])
        xT_hi = ph.sb("xT_hi", [P, 2, KC, 3 * P], F32R)
        xT_lo = ph.sb("xT_lo", [P, 2, KC, 3 * P], F32R)
        stat = ph.sb("stat", [P, 2, NT, 4])
        up_raw = ph.sb("up_raw", [P, 2, KC, PF * P])
        dn_raw = ph.sb("dn_raw", [P, 2, PF, DM])
        up_hi = ph.sb("up_hi", [P, 2, KC, P], F32R)
        up_lo = ph.sb("up_lo", [P, 2, KC, P], F32R)
        dn_hi = ph.sb("dn_hi", [P, 2, DM], F32R)
        dn_lo = ph.sb("dn_lo", [P, 2, DM], F32R)
        h_r = ph.sb("h_r", [P, 3 * P])
        h_2 = ph.sb("h_2", [P, 3 * P])
        h_hi = ph.sb("h_hi", [P, 2, 3 * P], F32R)
        h_lo = ph.sb("h_lo", [P, 2, 3 * P], F32R)
        acc = [[ph.ps(f"acc{k}{h}", [P, 512]) for h in range(2)] for k in range(3)]
        psU = [ph.ps(f"psU{k}", [P, 512]) for k in range(2)]
        s_c = ph.sem("constants_loaded")
        s_r = [ph.sem("raw_loaded_even"), ph.sem("raw_loaded_odd")]
        s_uh = ph.sem("up_hi_made")
        s_ul = ph.sem("up_lo_made")
        s_dh = ph.sem("down_hi_made")
        s_dl = ph.sem("down_lo_made")
        s_sum = ph.sem("squares_summed")
        s_ms = ph.sem("mean_square_made")
        s_sd = ph.sem("root_taken")
        s_xn = ph.sem("x_scaled")
        s_fill = ph.sem("bank_filled")
        s_tr = ph.sem("half_tile_transposed")
        s_xg = ph.sem("gain_applied")
        s_th = ph.sem("xT_hi_made")
        s_tl = ph.sem("xT_lo_made")
        s_up = ph.sem("hidden_multiplied")
        s_re = ph.sem("relu_made")
        s_h2 = ph.sem("square_made")
        s_hh = ph.sem("hidden_hi_made")
        s_hl = ph.sem("hidden_lo_made")
        s_dn = ph.sem("hidden_block_used")
        s_acc = ph.sem("half_added")
        s_y = ph.sem("y_ready")
        s_xf = ph.sem("xs_in_final_use")
        s_dve = ph.sem("vector_chain")

        def width(g):
            return sum(rows_of(i) for i in groups[g])

        def steps():
            n = 0
            for i in groups[0]:
                for h in range(2):
                    yield "x", (0, i, h), n
                    n += 1
            for g in range(len(groups)):
                todo = [(g + 1, i, h) for i in groups[g + 1] for h in range(2)] if g + 1 < len(groups) else []
                for f in range(n_f):
                    yield "f", (g, f), n
                    n += 1
                    if f >= 8 and f % 2 and todo:
                        yield "x", todo.pop(0), n
                        n += 1
                yield "end", (g, 0), n

        plan = list(steps())
        drained = {}
        n_x = n_up = 0
        for kind, arg, n in plan:
            if kind == "x":
                n_x += 1
                drained[n] = (s_xg, n_x)
            elif kind == "f":
                n_up += 1
                drained[n] = (s_re, n_up)

        with nc.Block() as block:

            @block.sync
            def _(sp):
                k = 0
                for g in range(len(groups)):
                    for f in range(0, n_f, PF):
                        if k >= 2:
                            for s in (s_uh, s_ul, s_dh, s_dl):
                                sp.wait_ge(s, PF * (k - 1))
                        sp.dma_start(up_raw[:, k % 2], t["w_up"][0].rearrange("(c p) n -> p c n", p=P)[:, :, f * P:(f + PF) * P]
                                     ).then_inc(s_r[k % 2], 16)
                        sp.dma_start(dn_raw[:, k % 2], t["w_down"][0][f * P:(f + PF) * P, :].rearrange("(a p) n -> p a n", p=P)
                                     ).then_inc(s_r[k % 2], 16)
                        k += 1

            @block.gpsimd
            def _(pool):
                pool.dma_start(gT[:, :], t["g_norm3"][0].rearrange("(c p) -> p c", p=P),
                               allow_slow_non_contiguous=True).then_inc(s_c, 16)
                pool.dma_start(ident[:, :], t["k_ident"]).then_inc(s_c, 16)
                pool.dma_start(g_last[:, :], t["g_final"].rearrange("(a n) -> a n", a=1).broadcast_to([P, DM])
                               ).then_inc(s_c, 16)
                n_h = n_y = 0
                for kind, arg, n in plan:
                    if kind == "f":
                        w = width(arg[0])
                        n_h += 1
                        pool.wait_ge(s_re, n_h)
                        if n_h > 1:
                            pool.wait_ge(s_hl, n_h - 1)
                        nc.gpsimd.tensor_tensor(h_2[:, 0:w], h_r[:, 0:w], h_r[:, 0:w], ALU.mult).then_inc(s_h2, 1)
                for i in range(NT):
                    pool.wait_ge(s_y, i + 1)
                    pool.dma_start(y_of(i), x[0:rows_of(i), i, :]).then_inc(s_st, 16)
                pool.wait_ge(s_st, 16 * NT)

            @block.tensor
            def _(pe):
                pe.wait_ge(s_c, 48)
                n_h = 0

                def down(m):
                    g, f = divmod(m, n_f)
                    pe.wait_ge(s_hl, m + 1)
                    pe.wait_ge(s_dl, m + 1)
                    at = 0
                    for k, i in enumerate(groups[g]):
                        r = rows_of(i)
                        for half in range(2):
                            if f == 0 and g:
                                pe.wait_ge(s_acc, 6 * (g - 1) + 2 * k + half + 1)
                            for n_pass, (a, b) in enumerate(((h_hi, dn_hi), (h_hi, dn_lo), (h_lo, dn_hi))):
                                last = nc.tensor.matmul(acc[k][half][0:r, :], a[:, m % 2, at:at + r],
                                                        b[:, m % 2, 512 * half:512 * half + 512],
                                                        start=(f == 0 and n_pass == 0), stop=(f == n_f - 1 and n_pass == 2))
                        at += r
                    last.then_inc(s_dn, 1)

                n_t = 0
                for kind, arg, n in plan:
                    if kind != "end" and n >= 2:
                        pe.wait_ge(*drained[n - 2])
                    if kind == "x":
                        g, i, h = arg
                        r = rows_of(i)
                        pe.wait_ge(s_xn, i + 1)
                        for c in range(4):
                            m = nc.tensor.transpose(psU[n % 2][:, c * P:c * P + r],
                                                    xs[0:r, (4 * h + c) * P:(4 * h + c + 1) * P], ident[0:r, 0:r])
                        m.then_inc(s_tr, 1)
                        n_t += 1
                    elif kind == "f":
                        g, f = arg
                        w = width(g)
                        if f == 0:
                            pe.wait_ge(s_tl, 6 * (g + 1))
                        pe.wait_ge(s_ul, n_h + 1)
                        for c in range(KC):
                            for n_pass, (a, b) in enumerate(((up_hi, xT_hi), (up_hi, xT_lo), (up_lo, xT_hi))):
                                m = nc.tensor.matmul(psU[n % 2][:, 0:w], a[:, n_h % 2, c, :], b[:, g % 2, c, 0:w],
                                                     start=(c == 0 and n_pass == 0), stop=(c == KC - 1 and n_pass == 2))
                        m.then_inc(s_up, 1)
                        n_h += 1
                        if f:
                            down(n_h - 2)
                    else:
                        down(n_h - 1)

            @block.scalar
            def _(act):
                def norm(which, i, src):
                    r = rows_of(i)
                    nc.scalar.activation(xs[0:r, :], src, ACT.Square, accum_out=stat[0:r, which, i, 0:1]).then_inc(s_sum, 1)

                n_h = n_s = n_t = 0
                splits = 0

                def split(m):
                    k, a = divmod(m, PF)
                    act.wait_ge(s_r[k % 2], 32 * (k // 2 + 1))
                    if m >= 2:
                        act.wait_ge(s_up, m - 1)
                    nc.scalar.copy(up_hi[:, m % 2], up_raw[:, k % 2, :, a * P:(a + 1) * P]).then_inc(s_uh, 1)
                    if m >= 2:
                        act.wait_ge(s_dn, m - 1)
                    nc.scalar.copy(dn_hi[:, m % 2], dn_raw[:, k % 2, a, :]).then_inc(s_dh, 1)

                total = n_f * len(groups)
                split(0)
                for kind, arg, n in plan:
                    if kind == "x":
                        g, i, h = arg
                        if h == 0:
                            if i:
                                act.wait_ge(s_tr, 2 * i)
                            if g >= 2:
                                act.wait_ge(s_y, 3 * (g - 1))
                            norm(0, i, x[0:rows_of(i), i, :])
                            act.wait_ge(s_ms, n_s + 1)
                            nc.scalar.activation(stat[0:rows_of(i), 0, i, 2:3], stat[0:rows_of(i), 0, i, 1:2],
                                                 ACT.Sqrt).then_inc(s_sd, 1)
                            n_s += 1
                        act.wait_ge(s_xg, n_t + 1)
                        k = i - groups[g][0]
                        r = rows_of(i)
                        if g >= 2:
                            act.wait_ge(s_up, n_f * (g - 1))
                        nc.scalar.copy(xT_hi[:, g % 2, 4 * h:4 * h + 4, k * P:k * P + r], xg[:, :, 0:r]).then_inc(s_th, 1)
                        n_t += 1
                    elif kind == "f":
                        w = width(arg[0])
                        if n_h + 1 < total:
                            split(n_h + 1)
                        act.wait_ge(s_up, n_h + 1)
                        if n_h:
                            act.wait_ge(s_h2, n_h)
                        nc.scalar.activation(h_r[:, 0:w], psU[n % 2][:, 0:w], ACT.Relu).then_inc(s_re, 1)
                        act.wait_ge(s_h2, n_h + 1)
                        nc.scalar.copy(h_hi[:, n_h % 2, 0:w], h_2[:, 0:w]).then_inc(s_hh, 1)
                        n_h += 1
                    else:
                        for i in groups[arg[0]]:
                            r = rows_of(i)
                            act.wait_ge(s_acc, 2 * (i + 1))
                            if i % 3:
                                act.wait_ge(s_y, i)
                            norm(1, i, x[0:r, i, :])
                            act.wait_ge(s_ms, n_s + 1)
                            nc.scalar.activation(stat[0:r, 1, i, 2:3], stat[0:r, 1, i, 1:2], ACT.Sqrt).then_inc(s_sd, 1)
                            n_s += 1

            @block.vector
            def _(dve):
                chain = Chain(dve, s_dve)
                n_h = n_s = n_t = 0

                def rms(which, i):
                    r = rows_of(i)
                    st = stat[0:r, which, i]
                    dve.wait_ge(s_sum, n_s + 1)
                    nc.vector.tensor_scalar(st[:, 1:2], st[:, 0:1], 1.0 / DM, EPS, ALU.mult, ALU.add).then_inc(s_ms, 1)
                    dve.wait_ge(s_sd, n_s + 1)
                    chain(nc.vector.reciprocal(st[:, 3:4], st[:, 2:3]))
                    return st[:, 3:4]

                def split(m):
                    k, a = divmod(m, PF)
                    dve.wait_ge(s_uh, m + 1)
                    nc.vector.tensor_tensor(up_lo[:, m % 2], up_raw[:, k % 2, :, a * P:(a + 1) * P],
                                            up_hi[:, m % 2].bitcast(F32), ALU.subtract).then_inc(s_ul, 1)
                    dve.wait_ge(s_dh, m + 1)
                    nc.vector.tensor_tensor(dn_lo[:, m % 2], dn_raw[:, k % 2, a, :], dn_hi[:, m % 2].bitcast(F32),
                                            ALU.subtract).then_inc(s_dl, 1)

                total = n_f * len(groups)
                split(0)
                dve.wait_ge(s_c, 48)
                for kind, arg, n in plan:
                    if kind == "x":
                        g, i, h = arg
                        r = rows_of(i)
                        if h == 0:
                            f = rms(0, i)
                            n_s += 1
                            nc.vector.tensor_scalar(xs[0:r, :], x[0:r, i, :], f, None, ALU.mult).then_inc(s_xn, 1)
                        dve.wait_ge(s_tr, n_t + 1)
                        if n_t:
                            dve.wait_ge(s_tl, n_t)
                        g4 = gT[:, 4 * h:4 * h + 4].unsqueeze(2).broadcast_to([P, 4, r])
                        src = psU[n % 2][:, :].rearrange("p (c t) -> p c t", c=4)[:, :, 0:r]
                        nc.vector.tensor_tensor(xg[:, :, 0:r], src, g4, ALU.mult).then_inc(s_xg, 1)
                        dve.wait_ge(s_th, n_t + 1)
                        k = i - groups[g][0]
                        sl = (slice(None), g % 2, slice(4 * h, 4 * h + 4), slice(k * P, k * P + r))
                        nc.vector.tensor_tensor(xT_lo[sl], xg[:, :, 0:r], xT_hi[sl].bitcast(F32), ALU.subtract).then_inc(s_tl, 1)
                        n_t += 1
                    elif kind == "f":
                        w = width(arg[0])
                        if n_h + 1 < total:
                            split(n_h + 1)
                        dve.wait_ge(s_hh, n_h + 1)
                        nc.vector.tensor_tensor(h_lo[:, n_h % 2, 0:w], h_2[:, 0:w], h_hi[:, n_h % 2, 0:w].bitcast(F32),
                                                ALU.subtract).then_inc(s_hl, 1)
                        n_h += 1
                    else:
                        g = arg[0]
                        for k, i in enumerate(groups[g]):
                            r = rows_of(i)
                            for half in range(2):
                                if k == 0 and half == 0:
                                    dve.wait_ge(s_dn, n_f * (g + 1))
                                xh = x[0:r, i, 512 * half:512 * half + 512]
                                nc.vector.tensor_tensor(xh, acc[k][half][0:r, :], xh, ALU.add).then_inc(s_acc, 1)
                        for k, i in enumerate(groups[g]):
                            r = rows_of(i)
                            f = rms(1, i)
                            n_s += 1
                            nc.vector.scalar_tensor_tensor(x[0:r, i, :], x[0:r, i, :], f, g_last[0:r, :], ALU.mult,
                                                           ALU.mult).then_inc(s_y, 1)


IN_NAMES = ["x_prompt", "x_sample", "cache_cmp_kv", "cache_sel_kv", "cache_win_kv", "state_pool", "cache_mem_kv",
            "page_table", "mem_prompt", "w_in", "pe_cmp", "w_cmp1", "w_cmp2", "w_pool", "g_attn_out", "pool_scale",
            "w_out", "g_norm1", "g_norm2", "g_mem", "w_mq", "w_mkv", "w_mo", "g_norm3", "w_up", "w_down", "g_final"]
OUTS = [("y_prompt", (1, SEQ, DM)), ("y_sample", (DB, DT, DM)),
        ("p_cmp_kv", (1, 1, SEQ, 2, NG, HD)), ("p_sel_kv", (1, 1, SEQ, 2, NG, HD)),
        ("p_win_kv", (1, 1, WIN, 2, NG, HD)), ("p_pool", (1, 1, HIST, PW)), ("p_mem_kv", (1, 1, NMEM, 2, MH, MD)),
        ("s_cmp_kv", (1, DB, DT, 2, NG, HD)), ("s_sel_kv", (1, DB, DT, 2, NG, HD)),
        ("s_win_kv", (1, DB, WIN, 2, NG, HD)), ("s_pool", (1, DB, HIST, PW))]


def constants():
    pos = np.concatenate([np.arange(SEQ), np.tile(PAST + np.arange(DT), DB), np.zeros(P - DB * DT)]).astype(np.float32)
    inv = np.float32(500000.0) ** (-np.arange(HALF, dtype=np.float32) / np.float32(HALF))
    ang = (pos[:, None] * inv[None, :].astype(np.float32)).astype(np.float32)
    cs = np.concatenate([np.cos(ang), np.sin(ang)], axis=1).astype(np.float32)
    first = np.zeros((P, 4, HIST), np.float32)
    for g in range(4):
        wide = 2 << g
        first[:, g, :] = wide / np.minimum(np.arange(HIST) + 1, wide)
    g, h, s = (x.ravel() for x in np.meshgrid(np.arange(NG), np.arange(HPG), np.arange(DT), indexing="ij"))
    smask = np.zeros((NH * DT, S_COLS), np.float32)
    smask[:, PAST:N_SEL] = np.where(np.arange(DT)[None] <= s[:, None], 0, NEG)
    w = np.arange(N_WIN)[None]
    smask[:, S_WIN0:S_CMP0] = np.where((w >= s[:, None]) & (w <= WIN + s[:, None]), 0, NEG)
    smask[:, S_COLS - 1] = NEG
    same = ((g[:, None] == g[None]) & (s[:, None] == s[None])).astype(np.float32)
    block_no = np.tile(np.arange(1, 1 + N_MID, dtype=np.float32), (NH * DT, 1))
    q, k = np.arange(P)[:, None], np.arange(P)[None]
    ends = np.arange(NCH)[None] * STRIDE + CLEN - 1
    pmask = [np.where(k <= q, 0, NEG), np.where(k >= q, 0, NEG)]
    pmask += [np.where((ends <= q + i * P) & (ends < SEQ), 0, NEG) for i in range(NT - 1)]
    own = (np.arange(AW)[None] // MD == np.arange(MH * DT)[:, None] // DT).astype(np.float32)
    pick = np.zeros((MH * DT, DB, DB * DT), np.float32)
    for b in range(DB):
        pick[np.arange(MH * DT), b, b * DT + np.arange(MH * DT) % DT] = 1
    return {"k_own": own, "k_pick": pick, "k_pmask": np.concatenate(pmask, axis=1).astype(np.float32), "k_smask": smask, "k_same": same, "k_block_no": block_no, "k_edge": first, "k_ident": np.eye(P, dtype=np.float32),
            "k_rope": np.ascontiguousarray(cs.reshape(NT, P, ROT).transpose(1, 0, 2))}


def build(nc, t, o):
    with ExitStack() as ctx:
        top = Phase(nc, ctx, "top")
        stored = [nc.alloc_semaphore(f"{tag}_outputs_stored") for tag in ("memory", "poolin", "qkv", "mlp")]
        x_p = t["x_prompt"].rearrange("a (i p) d -> (a i) p d", p=P)
        x_s = t["x_sample"].rearrange("b t d -> (b t) d")
        all_tiles = list(range(NT))

        def x_of(i):
            return x_p[i] if i < NT - 1 else x_s

        with ExitStack() as c2:
            ph = Phase(nc, c2, "memory")
            y = ph.sb("y", [P, NMEM // P, 2 * AW])
            mem = t["mem_prompt"].rearrange("a (i p) d -> (a i) p d", p=P)
            out = o["p_mem_kv"].rearrange("l a (i p) u h d -> (l a i) p (u h d)", p=P)

            def store_mem(eng, sem, i):
                eng.dma_start(out[i], y[:, i, :]).then_inc(sem, 16)
                return 1

            project(nc, "mem", [0, 1], lambda i: mem[i], t["g_mem"][0], t["w_mkv"][0], 2 * AW, y, store_mem, stored[0], t)
        mix_scope = top.ctx.enter_context(ExitStack())
        mixed = Phase(nc, mix_scope, "mixed")
        aT = mixed.sb("aT", [P, 4, TOK], side="right")
        yq_scope = top.ctx.enter_context(ExitStack())
        ys = Phase(nc, yq_scope, "proj")
        yq = ys.sb("yq", [P, NT, C_PI])
        q_rot = ys.sb("q_rot", [P, NT, NH, ROT])
        with ExitStack() as c2:
            def store_kv(eng, sem, i):
                n = 0
                if i == 0:
                    old = t["cache_win_kv"][0].rearrange("b n u g d -> b n (u g d)")
                    new = o["s_win_kv"][0].rearrange("b n u g d -> b n (u g d)")
                    eng.dma_start(new[:, 0:WIN - DT, :], old[:, DT:WIN, :]).then_inc(sem, 16)
                    n += 1
                for name, c in (("cmp", C_KC), ("sel", C_KS), ("win", C_KW)):
                    if i < NT - 1:
                        dst = o[f"p_{name}_kv"][0, 0].rearrange("n u g d -> n (u g d)")
                        at = i * P - (SEQ - dst.shape[0])
                        if at < 0:
                            continue
                        eng.dma_start(dst[at:at + P, :], yq[:, i, c:c + KVW]).then_inc(sem, 16)
                        n += 1
                    elif name != "win":
                        dst = o[f"s_{name}_kv"][0].rearrange("b n u g d -> (b n) (u g d)")
                        eng.dma_start(dst, yq[0:DB * DT, i, c:c + KVW]).then_inc(sem, 16)
                        n += 1
                    else:
                        dst = o["s_win_kv"][0].rearrange("b n u g d -> b n (u g d)")
                        for b in range(DB):
                            eng.dma_start(dst[b, WIN - DT:WIN, :], yq[b * DT:b * DT + DT, i, c:c + KVW]).then_inc(sem, 16)
                        n += DB
                return n

            cs = Phase(nc, c2, "rope").sb("cs", [P, NT, ROT])
            project(nc, "qkv", all_tiles, x_of, t["g_norm1"][0], t["w_in"][0][:, 0:C_PI], C_PI, yq, store_kv,
                    stored[2], t, rope=(q_rot, cs))


        with ExitStack() as c3:
            ph = Phase(nc, c3, "ckv")
            ck_hi = ph.sb("ck_hi", [P, NG, NCH], F32R)
            ck_lo = ph.sb("ck_lo", [P, NG, NCH], F32R)
            cv_p = ph.sb("cv_p", [HD, NG, P], F32R)
            with ExitStack() as c4:
                ph = Phase(nc, c4, "ckv_s")
                ck_s = ph.sb("ck_s", [P, DB, NCH])
                cv_s = ph.sb("cv_s", [HD, DB, P])
                compress(nc, t, o, ck_s, cv_s, ck_hi, ck_lo, cv_p)
                sample_attention(nc, t, o, yq, q_rot, ck_s, cv_s, aT)
            prompt_attention(nc, t, yq, q_rot, ck_hi, ck_lo, cv_p, aT)
        yq_scope.close()
        mT = mixed.sb("mT", [P, 4, TOK], side="right")
        with ExitStack() as c2:
            ph = Phase(nc, c2, "poolin")
            yp = ph.sb("yp", [P, NT, PW])
            sp_out = o["s_pool"][0]

            def store_pool(eng, sem, i):
                if i == NT - 2:
                    eng.dma_start(o["p_pool"][0, 0], yp[P - HIST:P, i, :]).then_inc(sem, 16)
                    return 1
                if i == 0:
                    eng.dma_start(sp_out[:, 0:HIST - DT, :], t["state_pool"][0, :, DT:HIST, :]).then_inc(sem, 16)
                    return 1
                if i == NT - 1:
                    for b in range(DB):
                        eng.dma_start(sp_out[b, HIST - DT:HIST, :], yp[b * DT:b * DT + DT, i, :]).then_inc(sem, 16)
                    return DB
                return 0

            project(nc, "pin", all_tiles, x_of, t["g_norm1"][0], t["w_in"][0][:, C_PI:C_END], PW, yp, store_pool, stored[1], t)
            pool_mix(nc, t, yp, mT)
        x = top.sb("x", [P, NT, DM])
        mix_out(nc, t, x_of, aT, mT, x)
        mix_scope.close()
        cross_attention(nc, t, o, x)
        y_p = o["y_prompt"].rearrange("a (i p) d -> (a i) p d", p=P)
        y_s = o["y_sample"].rearrange("b t d -> (b t) d")
        mlp(nc, t, o, x, lambda i: y_p[i] if i < NT - 1 else y_s, stored[3])


def kernel(**inputs):
    import concourse.bacc as _bacc
    from concourse.bass_utils import run_bass_kernel_spmd as _run

    nc = _bacc.Bacc("TRN2", target_bir_lowering=False, num_devices=1)
    arrays = {f"in_{n}": np.ascontiguousarray(inputs[n]) for n in IN_NAMES}
    arrays.update(constants())
    t = {n: nc.dram_tensor(n, a.shape, mybir.dt.from_np(a.dtype), kind="ExternalInput").ap() for n, a in arrays.items()}
    t = {n.removeprefix("in_"): a for n, a in t.items()}
    o = {n: nc.dram_tensor(f"out_{n}", s, F32, kind="ExternalOutput").ap() for n, s in OUTS}
    build(nc, t, o)
    r = _run(nc, [arrays], core_ids=[0])
    return tuple(r.results[0][f"out_{n}"] for n, _ in OUTS)
```

```python
from contextlib import ExitStack

import numpy as np
import concourse.bass as bass
from concourse import mybir

F32 = mybir.dt.float32
F32R = mybir.dt.float32r
I32 = mybir.dt.int32
ALU = mybir.AluOpType
ACT = mybir.ActivationFunctionType
AX = mybir.AxisListType

P = 128
DM = 1024
SEQ = 1024
DB, DT = 8, 8
PAST = 1024
PAGE = 128
AW = 512
NH, NG, HPG, HD = 8, 2, 4, 64
KVW = 2 * NG * HD
C_Q, C_KC, C_KS, C_KW, C_GL, C_PI, C_END = 0, 512, 768, 1024, 1280, 1304, 1816
SCALE = HD ** -0.5
ROT = HD // 4
HALF = ROT // 2
WIN = 512
STRIDE, CLEN = 16, 32
NCH = SEQ // STRIDE
NCMP = NCH - 1
SELB = 64
NMEM, MH, MD = 256, 4, 128
DFF = 4096
PW = 512
HIST = 15
EPS = 1e-6
NT = SEQ // P + 1
KC = DM // P
NEG = -1e30
TOK = SEQ + DB * DT


def rows_of(i):
    return P if i < NT - 1 else DB * DT


class Phase:

    def __init__(self, nc, ctx, tag):
        self.nc, self.ctx, self.tag, self.sems = nc, ctx, tag, []
        ctx.callback(self.release)

    def sb(self, name, shape, dt=F32, side=None):
        return self.ctx.enter_context(self.nc.sbuf_tensor(f"{self.tag}_{name}", shape, dt, side=side))

    def ps(self, name, shape):
        return self.ctx.enter_context(self.nc.psum_tensor(f"{self.tag}_{name}", shape, F32))

    def sem(self, name):
        s = self.nc.alloc_semaphore(f"{self.tag}_{name}")
        self.sems.append(s)
        return s

    def release(self):
        if self.sems:
            self.nc.clear_and_free_semaphores(self.sems)
            self.nc.all_engine_barrier()


class Chain:

    def __init__(self, eng, sem):
        self.eng, self.sem, self.n = eng, sem, 0

    def __call__(self, ins):
        self.n += 1
        ins.then_inc(self.sem, 1)
        self.eng.wait_ge(self.sem, self.n)


def project(nc, tag, tiles, x_of, gain, weight, width, y, store, s_st, t, ident, rope=None, table=None, wait_stores=True):
    n_grp = -(-width // 512)
    step = -(-width // n_grp // 4) * 4
    groups = [(a, min(a + step, width)) for a in range(0, width, step)]
    RAW = 4
    with ExitStack() as ctx:
        ph = Phase(nc, ctx, tag)
        w_raw = ph.sb("w_raw", [P, RAW, width])
        w_hi = ph.sb("w_hi", [P, KC, width], F32R)
        w_lo = ph.sb("w_lo", [P, KC, width], F32R)
        x_t = ph.sb("x_t", [P, 2, DM])
        junk = ph.sb("junk", [P, DM])
        xT_hi = ph.sb("xT_hi", [P, 2, KC, P], F32R)
        xT_lo = ph.sb("xT_lo", [P, 2, KC, P], F32R)
        gT = ph.sb("gT", [P, KC])
        stat = ph.sb("stat", [P, 4, NT])
        acc = [[ph.ps(f"acc{b}{g}", [P, 512]) for g in range(len(groups))] for b in range(2)]
        psT = [ph.ps(f"psT{h}", [P, 4, P]) for h in range(2)]
        if rope:
            q_rot, cs = rope
            t4 = ph.sb("t4", [P, 4, NH, HALF])
        s_w = [ph.sem(f"weight_slot{k}_loaded") for k in range(RAW)]
        s_g = ph.sem("gain_loaded")
        s_x1 = [ph.sem("first_x_loaded"), ph.sem("second_x_loaded")]
        s_x = [ph.sem("x_loaded_even"), ph.sem("x_loaded_odd")]
        s_id = ph.sem("identity_loaded")
        s_tab = ph.sem("page_table_loaded")
        s_cs = ph.sem("rope_table_loaded")
        s_hi = ph.sem("weight_hi_made")
        s_lo = ph.sem("weight_lo_made")
        s_sum = ph.sem("squares_summed")
        s_ms = ph.sem("mean_square_made")
        s_sd = ph.sem("root_taken")
        s_xn = ph.sem("x_scaled")
        s_tr = ph.sem("x_transposed")
        s_th = ph.sem("xT_hi_made")
        s_tl = ph.sem("xT_lo_made")
        s_mm = ph.sem("group_multiplied")
        s_yv = ph.sem("y_copied_by_vector")
        s_ya = ph.sem("y_copied_by_scalar")
        s_rope = ph.sem("keys_rotated")
        s_dve = ph.sem("vector_chain")
        ng = len(groups)
        n_v, n_a = -(-ng // 2), ng // 2
        n = len(tiles)
        n_stores = []
        with nc.Block() as block:

            @block.sync
            def _(sp):
                for j in range(2):
                    sp.dma_start(x_t[0:rows_of(tiles[j]), j, :], x_of(tiles[j])).then_inc(s_x1[j], 16)
                    if j == 0 and table is not None:
                        sp.dma_start(ident[:, :], t["k_ident"]).then_inc(s_id, 16)
                        sp.dma_start(table[:, :], t["page_table"].rearrange("(a b) n -> a (b n)", a=1)).then_inc(s_tab, 16)
                for c in range(KC):
                    if c >= RAW:
                        sp.wait_ge(s_lo, c - RAW + 1)
                    sp.dma_start(w_raw[:, c % RAW, :], weight[c * P:(c + 1) * P, :]).then_inc(s_w[c % RAW], 16)
                started = 0
                for j, i in enumerate(tiles):
                    sp.wait_ge(s_yv, n_v * (j + 1))
                    if n_a:
                        sp.wait_ge(s_ya, n_a * (j + 1))
                    if rope:
                        sp.wait_ge(s_rope, j + 1)
                    started += store(sp, s_st, i)
                if table is not None:
                    sp.wait_ge(s_tab, 16)
                if wait_stores:
                    sp.wait_ge(s_st, 16 * started)
                n_stores.append(started)

            @block.gpsimd
            def _(pool):
                if rope:
                    pool.dma_start(cs[:, :, :], t["k_rope"]).then_inc(s_cs, 16)
                for j in range(2, n):
                    i = tiles[j]
                    pool.wait_ge(s_tr, 2 * (j - 1))
                    pool.dma_start(x_t[0:rows_of(i), j % 2, :], x_of(i)).then_inc(s_x[j % 2], 16)

            @block.scalar
            def _(act):
                act.dma_start(gT[:, :], gain.rearrange("(c p) -> p c", p=P),
                              allow_slow_non_contiguous=True).then_inc(s_g, 16)

                def square_sum(j):
                    r = rows_of(tiles[j])
                    if j < 2:
                        act.wait_ge(s_x1[j], 16)
                    else:
                        act.wait_ge(s_x[j % 2], 16 * (j // 2))
                    if j:
                        act.wait_ge(s_sum, j)
                    nc.scalar.activation(junk[0:r, :], x_t[0:r, j % 2, :], ACT.Square,
                                         accum_out=stat[0:r, 0, j:j + 1]).then_inc(s_sum, 1)
                    act.wait_ge(s_ms, j + 1)
                    nc.scalar.activation(stat[0:r, 2, j:j + 1], stat[0:r, 1, j:j + 1], ACT.Sqrt).then_inc(s_sd, 1)

                def hi(j):
                    r = rows_of(tiles[j])
                    for h in range(2):
                        act.wait_ge(s_tr, 2 * j + h + 1)
                        if j >= 2:
                            act.wait_ge(s_mm, ng * (j - 1))
                        nc.scalar.copy(xT_hi[:, j % 2, 4 * h:4 * h + 4, 0:r], psT[h][:, :, 0:r]).then_inc(s_th, 1)

                square_sum(0)
                if n > 1:
                    square_sum(1)
                hi(0)
                act.wait_ge(s_g, 16)
                for c in range(KC):
                    act.wait_ge(s_w[c % RAW], 16 * (c // RAW + 1))
                    nc.scalar.mul(w_hi[:, c, :], w_raw[:, c % RAW, :], gT[:, c:c + 1]).then_inc(s_hi, 1)
                for j, i in enumerate(tiles):
                    r = rows_of(i)
                    if j + 1 < n:
                        hi(j + 1)
                    if j + 2 < n:
                        square_sum(j + 2)
                    for g, (a, b) in enumerate(groups):
                        if g % 2 == 1:
                            act.wait_ge(s_mm, ng * j + g + 1)
                            nc.scalar.copy(y[0:r, i, a:b], acc[j % 2][g][0:r, 0:b - a]).then_inc(s_ya, 1)

            @block.vector
            def _(dve):
                chain = Chain(dve, s_dve)

                def scale_x(j):
                    r = rows_of(tiles[j])
                    dve.wait_ge(s_sum, j + 1)
                    nc.vector.tensor_scalar(stat[0:r, 1, j:j + 1], stat[0:r, 0, j:j + 1], 1.0 / DM, EPS,
                                            ALU.mult, ALU.add).then_inc(s_ms, 1)
                    dve.wait_ge(s_sd, j + 1)
                    chain(nc.vector.reciprocal(stat[0:r, 3, j:j + 1], stat[0:r, 2, j:j + 1]))
                    nc.vector.tensor_scalar(x_t[0:r, j % 2, :], x_t[0:r, j % 2, :], stat[0:r, 3, j:j + 1], None,
                                            ALU.mult).then_inc(s_xn, 1)

                def rotate(chain, j, i, r):
                    q = y[0:r, i, C_Q:C_Q + AW].rearrange("p (h d) -> p h d", d=HD)
                    k = y[0:r, i, C_KS:C_KS + 2 * KVW].rearrange("p (b u g d) -> p b u g d", b=2, u=2, g=NG)[:, :, 0]
                    for part in range(2):
                        if part == 0:
                            x1, x2 = q[:, :, 0:HALF], q[:, :, HALF:ROT]
                            o1, o2 = q_rot[0:r, i, :, 0:HALF], q_rot[0:r, i, :, HALF:ROT]
                            shape, tt = [r, NH, HALF], [t4[0:r, m, :, :] for m in range(4)]
                            cos, sin = (cs[0:r, i, m * HALF:(m + 1) * HALF].unsqueeze(1).broadcast_to(shape)
                                        for m in range(2))
                        else:
                            x1, x2 = k[:, :, :, 0:HALF], k[:, :, :, HALF:ROT]
                            o1, o2 = x1, x2
                            shape = [r, 2, NG, HALF]
                            tt = [t4[0:r, m, 0:4, :].rearrange("p (b g) e -> p b g e", b=2) for m in range(4)]
                            cos, sin = (cs[0:r, i, m * HALF:(m + 1) * HALF].unsqueeze(1).unsqueeze(1).broadcast_to(shape)
                                        for m in range(2))
                        nc.vector.tensor_tensor(tt[0], x1, cos, ALU.mult)
                        nc.vector.tensor_tensor(tt[1], x2, sin, ALU.mult)
                        nc.vector.tensor_tensor(tt[2], x2, cos, ALU.mult)
                        chain(nc.vector.tensor_tensor(tt[3], x1, sin, ALU.mult))
                        nc.vector.tensor_tensor(o1, tt[0], tt[1], ALU.subtract)
                        last = nc.vector.tensor_tensor(o2, tt[2], tt[3], ALU.add)
                        if part == 0:
                            chain(last)
                        else:
                            last.then_inc(s_rope, 1)
                    if j + 1 < n:
                        chain.eng.wait_ge(s_rope, j + 1)

                def lo(j):
                    r = rows_of(tiles[j])
                    for h in range(2):
                        dve.wait_ge(s_th, 2 * j + h + 1)
                        nc.vector.tensor_tensor(xT_lo[:, j % 2, 4 * h:4 * h + 4, 0:r], psT[h][:, :, 0:r],
                                                xT_hi[:, j % 2, 4 * h:4 * h + 4, 0:r].bitcast(F32),
                                                ALU.subtract).then_inc(s_tl, 1)

                scale_x(0)
                if n > 1:
                    scale_x(1)
                lo(0)
                dve.wait_ge(s_g, 16)
                for c in range(KC):
                    dve.wait_ge(s_hi, c + 1)
                    nc.vector.scalar_tensor_tensor(w_lo[:, c, :], w_raw[:, c % RAW, :], gT[:, c:c + 1],
                                                   w_hi[:, c, :].bitcast(F32), ALU.mult, ALU.subtract).then_inc(s_lo, 1)
                for j, i in enumerate(tiles):
                    r = rows_of(i)
                    if j + 1 < n:
                        lo(j + 1)
                    if j + 2 < n:
                        scale_x(j + 2)
                    for g, (a, b) in enumerate(groups):
                        if g % 2 == 0:
                            dve.wait_ge(s_mm, ng * j + g + 1)
                            nc.vector.tensor_copy(y[0:r, i, a:b], acc[j % 2][g][0:r, 0:b - a]).then_inc(s_yv, 1)
                    if rope:
                        dve.wait_ge(s_cs, 16)
                        dve.wait_ge(s_yv, n_v * (j + 1))
                        dve.wait_ge(s_ya, n_a * (j + 1))
                        rotate(chain, j, i, r)

            @block.tensor
            def _(pe):
                if table is not None:
                    pe.wait_ge(s_id, 16)

                def transposes(j):
                    r = rows_of(tiles[j])
                    pe.wait_ge(s_xn, j + 1)
                    for c in range(KC):
                        if j and c % 4 == 0:
                            pe.wait_ge(s_tl, 2 * (j - 1) + c // 4 + 1)
                        m = nc.tensor.transpose(psT[c // 4][:, c % 4, 0:r], x_t[0:r, j % 2, c * P:(c + 1) * P],
                                                ident[0:r, 0:r])
                        if c % 4 == 3:
                            m.then_inc(s_tr, 1)

                transposes(0)
                for j, i in enumerate(tiles):
                    r = rows_of(i)
                    pe.wait_ge(s_tl, 2 * (j + 1))
                    if j + 1 < n:
                        transposes(j + 1)
                    if j >= 2:
                        pe.wait_ge(s_yv, n_v * (j - 1))
                        if n_a:
                            pe.wait_ge(s_ya, n_a * (j - 1))
                    if j:
                        order = [(g, c) for g in range(ng) for c in range(KC)]
                    else:
                        order = [(g, c) for c in range(KC) for g in range(ng)]
                    for g, c in order:
                        a, b = groups[g]
                        if j == 0 and g == 0:
                            pe.wait_ge(s_lo, c + 1)
                        for n_pass, (xs, ws) in enumerate(((xT_hi, w_hi), (xT_hi, w_lo), (xT_lo, w_hi))):
                            m = nc.tensor.matmul(acc[j % 2][g][0:r, 0:b - a], xs[:, j % 2, c, 0:r], ws[:, c, a:b],
                                                 start=(c == 0 and n_pass == 0), stop=(c == KC - 1 and n_pass == 2))
                        if c == KC - 1:
                            m.then_inc(s_mm, 1)
    return n_stores[0]


def pool_mix(nc, t, ident, yp, mT, w_raw, s_w):
    seq_len = HIST + DT
    p_len = HIST + SEQ
    length = p_len + DB * seq_len
    with ExitStack() as ctx:
        ph = Phase(nc, ctx, "mix")
        ext = ph.sb("ext", [P, 4, length])
        sums = ph.sb("sums", [P, 2, length])
        diff = ph.sb("diff", [P, 4, TOK])
        state = ph.sb("state", [DB * HIST, PW])
        w = ph.sb("w", [P, 4, P])
        edge = ph.sb("edge", [P, 4, HIST])
        psT = [ph.ps(f"psT{k}", [P, 4, P]) for k in range(2)]
        psM = [ph.ps(f"psM{k}", [P, 512]) for k in range(2)]
        s_c = ph.sem("constants_loaded")
        s_tr = ph.sem("tile_transposed")
        s_ext = ph.sem("ext_written")
        s_d = ph.sem("difference_made")
        s_mm = ph.sem("mixed")
        s_m = ph.sem("mT_written")
        s_dve = ph.sem("vector_chain")
        samples = ext[:, :, p_len:length].rearrange("p g (b s) -> p g b s", b=DB)
        cols = [(0, 512), (512, 1024), (1024, TOK)]
        with nc.Block() as block:

            @block.sync
            def _(sp):
                sp.dma_start(state[:, :], t["state_pool"][0].rearrange("b s c -> (b s) c")).then_inc(s_c, 16)
                sp.dma_start(w[:, :, :], t["w_pool"][0].rearrange("g c d -> c g d")).then_inc(s_c, 16)
                sp.dma_start(edge[:, :, :], t["k_edge"]).then_inc(s_c, 16)
                for c in range(KC):
                    sp.dma_start(w_raw[:, c, :], t["w_out"][0][c * P:(c + 1) * P, :]).then_inc(s_w[c], 16)

            @block.tensor
            def _(pe):
                pe.wait_ge(s_c, 48)
                for k in range(NT + 1):
                    if k >= 2:
                        pe.wait_ge(s_ext, k - 1)
                    r = rows_of(k) if k < NT else DB * HIST
                    for g in range(4):
                        src = yp[0:r, k, g * P:(g + 1) * P] if k < NT else state[:, g * P:(g + 1) * P]
                        m = nc.tensor.transpose(psT[k % 2][:, g, 0:r], src, ident[0:r, 0:r])
                    m.then_inc(s_tr, 1)
                for g in range(4):
                    pe.wait_ge(s_d, g + 1)
                    for k, (a, b) in enumerate(cols):
                        u = 3 * g + k
                        if u >= 2:
                            pe.wait_ge(s_m, u - 1)
                        nc.tensor.matmul(psM[u % 2][:, 0:b - a], w[:, g, :], diff[:, g, a:b],
                                         start=True, stop=True).then_inc(s_mm, 1)

            @block.scalar
            def _(act):
                for k in range(NT + 1):
                    act.wait_ge(s_tr, k + 1)
                    if k < NT - 1:
                        dst, src = ext[:, :, HIST + k * P:HIST + (k + 1) * P], psT[k % 2][:, :, :]
                        nc.scalar.copy(dst, src).then_inc(s_ext, 1)
                        continue
                    n = DT if k == NT - 1 else HIST
                    for g in range(4):
                        dst = samples[:, g, :, HIST:seq_len] if k == NT - 1 else samples[:, g, :, 0:HIST]
                        m = nc.scalar.copy(dst, psT[k % 2][:, g, 0:DB * n].rearrange("p (b s) -> p b s", b=DB))
                    m.then_inc(s_ext, 1)
                for u in range(12):
                    g, (a, b) = u // 3, cols[u % 3]
                    act.wait_ge(s_mm, u + 1)
                    nc.scalar.copy(mT[:, g, a:b], psM[u % 2][:, 0:b - a]).then_inc(s_m, 1)

            @block.vector
            def _(dve):
                chain = Chain(dve, s_dve)
                chain(nc.vector.memset(ext[:, :, 0:HIST], 0.0))
                dve.wait_ge(s_ext, NT + 1)
                dve.wait_ge(s_c, 48)
                for g in range(4):
                    wide = 2 << g
                    cur, m, at = ext[:, g, :], 1, 1
                    while m < wide:
                        new = sums[:, at % 2, :]
                        chain(nc.vector.tensor_tensor(new[:, 2 * m - 1:length], cur[:, 2 * m - 1:length],
                                                      cur[:, m - 1:length - m], ALU.add))
                        cur, m, at = new, 2 * m, at + 1
                    chain(nc.vector.tensor_tensor(cur[:, HIST:2 * HIST], cur[:, HIST:2 * HIST], edge[:, g, :], ALU.mult))
                    nc.vector.scalar_tensor_tensor(diff[:, g, 0:SEQ], cur[:, HIST:p_len], 1.0 / wide,
                                                   ext[:, g, HIST:p_len], ALU.mult, ALU.subtract)
                    tail = cur[:, p_len:length].rearrange("p (b s) -> p b s", b=DB)[:, :, HIST:seq_len]
                    nc.vector.scalar_tensor_tensor(diff[:, g, SEQ:TOK].rearrange("p (b s) -> p b s", b=DB), tail,
                                                   1.0 / wide, samples[:, g, :, HIST:seq_len], ALU.mult,
                                                   ALU.subtract).then_inc(s_d, 1)
                    dve.wait_ge(s_d, g + 1)


def compress(nc, t, ident, table, o, ck_s, cv_s, ck_hi, ck_lo, cv_p, s_stored, n_stored):
    n_seq = DB + 1
    pairs = PAGE // 2
    n_j = STRIDE // 2
    RAW = 3
    with ExitStack() as ctx:
        ph = Phase(nc, ctx, "cmp")
        raw = ph.sb("raw", [P, RAW, 4, 2, 2 * NG, HD])
        paired = ph.sb("paired", [P, 2, 4, 2 * NG, 2, HD])
        rT = ph.sb("rT", [P, 2, 2 * NG, 4 * P])
        w1 = ph.sb("w1", [P, 2, n_j, 2, HD])
        w2 = ph.sb("w2", [HD, 2, 2 * HD])
        pe_t = ph.sb("pe_t", [P, 2, 2 * n_j])
        pe_b = ph.sb("pe_b", [HD, 2])
        late = ph.sb("late", [HD, 2, NG, NCMP])
        z = ph.sb("z", [HD, 2, n_seq, NG, NCH])
        z3 = ph.sb("z3", [HD, 2, n_seq, NG, NCH])
        psT = [ph.ps(f"psT{k}", [P, 4, P]) for k in range(2)]
        psU = [ph.ps(f"psU{k}", [P, 2, NG, NCH]) for k in range(2)]
        psE = ph.ps("psE", [HD, 2])
        psV = [ph.ps(f"psV{k}", [HD, 4, 2 * HD]) for k in range(2)]
        psP = ph.ps("psP", [P, 2, 2, HD])
        s_c = ph.sem("weights_loaded")
        s_raw = [ph.sem(f"even_pages_slot{k}_loaded") for k in range(RAW)]
        s_raw_odd = [ph.sem(f"odd_pages_slot{k}_loaded") for k in range(RAW)]
        s_pair = ph.sem("columns_paired")
        s_tr = ph.sem("tile_transposed")
        s_rT = ph.sem("tile_copied")
        s_pe = ph.sem("pe_term_made")
        s_peb = ph.sem("pe_term_copied")
        s_pl = ph.sem("pe_loaded")
        s_u = ph.sem("windows_multiplied")
        s_late = ph.sem("late_half_moved")
        s_z = ph.sem("hidden_made")
        s_sq = ph.sem("hidden_squared")
        s_cu = ph.sem("cubic_made")
        s_ex = ph.sem("exp_made")
        s_ge = ph.sem("gelu_made")
        s_out = ph.sem("outputs_multiplied")
        s_fin = ph.sem("hi_parts_copied")
        s_dve = ph.sem("vector_chain")
        cache = t["cache_cmp_kv"][0].rearrange("n (p r) u g d -> n p (r u g d)", r=2)
        own = o["p_cmp_kv"][0, 0].rearrange("(k p r) u g d -> p k (r u g d)", p=P, r=2)
        with nc.Block() as block:

            def load_pages(eng, first, queue_sem):
                for q in range(DB):
                    if q >= RAW:
                        eng.wait_ge(s_pair, 4 * (q - RAW + 1))
                    for n in range(first, PAST // PAGE, 2):
                        page = eng.value_load(table[0:1, q * DB + n:q * DB + n + 1], min_val=0,
                                              max_val=cache.shape[0] - 1)
                        dst = raw[pairs * (n % 2):pairs * (n % 2) + pairs, q % RAW, n // 2].rearrange("p r c d -> p (r c d)")
                        eng.dma_start(dst, cache[bass.DynSlice(page, 1)].rearrange("a p f -> (a p) f")
                                      ).then_inc(queue_sem[q % RAW], 16)

            @block.sync
            def _(sp):
                load_pages(sp, 0, s_raw)
                sp.wait_ge(s_pair, 4 * (DB - RAW + 1))
                sp.wait_ge(s_stored, 16 * n_stored)
                sp.dma_start(raw[:, DB % RAW].rearrange("p k r c d -> p k (r c d)"), own).then_inc(s_raw[DB % RAW], 16)

            @block.gpsimd
            def _(pool):
                load_pages(pool, 1, s_raw_odd)

            @block.tensor
            def _(pe):
                def transposes(q):
                    for k in range(4):
                        pe.wait_ge(s_pair, 4 * q + k + 1)
                        u = 4 * q + k
                        if u >= 2:
                            pe.wait_ge(s_rT, u - 1)
                        for cg in range(2 * NG):
                            m = nc.tensor.transpose(psT[u % 2][:, cg, :], paired[:, q % 2, k, cg].rearrange("p r d -> p (r d)"),
                                                    ident[:, :])
                        m.then_inc(s_tr, 1)

                transposes(0)
                pe.wait_ge(s_c, 16 * 8)
                for q in range(n_seq):
                    if q + 1 < n_seq:
                        transposes(q + 1)
                    if q == 1:
                        pe.wait_ge(s_pl, 32)
                        for c in range(2):
                            for k in range(2 * n_j):
                                m = nc.tensor.matmul(psE[:, c:c + 1], w1[:, c, k % n_j, k // n_j, :], pe_t[:, c, k:k + 1],
                                                     start=(k == 0), stop=(k == 2 * n_j - 1))
                        m.then_inc(s_pe, 1)
                    pe.wait_ge(s_rT, 4 * (q + 1))
                    if q >= 2:
                        pe.wait_ge(s_z, q - 1)
                    for c in range(2):
                        for j in range(n_j):
                            mov = rT[:, q % 2, NG * c:NG * c + NG, :].rearrange("p g (n j) -> p j g n", j=n_j)[:, j]
                            m = nc.tensor.matmul(psU[q % 2][:, c, :, :], w1[:, c, j, :, :].rearrange("p r h -> p (r h)"),
                                                 mov, start=(j == 0), stop=(j == n_j - 1))
                    m.then_inc(s_u, 1)
                pe.wait_ge(s_ge, n_seq)
                for g in range(NG):
                    nc.tensor.matmul(psT[0][g * HD:(g + 1) * HD, :, :].rearrange("p a b -> p (a b)"), w2[:, 0, 0:HD],
                                     z3[:, 0, 0:DB, g, :], start=True, stop=True)
                for b in range(DB):
                    for g in range(NG):
                        nc.tensor.matmul(psV[b // 4][:, b % 4, g * HD:(g + 1) * HD], z3[:, 1, b, g, :], w2[:, 1, 0:HD],
                                         start=True, stop=True)
                for g in range(NG):
                    nc.tensor.matmul(psP[:, 0, g, :], w2[:, 0, :], z3[:, 0, DB, g, :], start=True, stop=True)
                for g in range(NG):
                    m = nc.tensor.matmul(psP[0:HD, 1, g, :], z3[:, 1, DB, g, :], w2[:, 1, 0:HD], start=True, stop=True)
                m.then_inc(s_out, 1)

            @block.scalar
            def _(act):
                for c in range(2):
                    for r in range(2):
                        src = t["w_cmp1"][0, c].rearrange("(r j p) h -> r p j h", r=2, p=P)[r]
                        act.dma_start(w1[:, c, :, r, :], src).then_inc(s_c, 16)
                    for k in range(2):
                        act.dma_start(w2[:, c, k * HD:(k + 1) * HD], t["w_cmp2"][0, c]).then_inc(s_c, 16)
                for c in range(2):
                    act.dma_start(pe_t[:, c, :], t["pe_cmp"][0, c].rearrange("l d -> (l d)").rearrange("(j p) -> p j", p=P),
                                  allow_slow_non_contiguous=True).then_inc(s_pl, 16)

                def late_half(act, q):
                    act.wait_ge(s_u, q + 1)
                    if q:
                        act.wait_ge(s_z, q)
                    for c in range(2):
                        m = nc.scalar.copy(late[:, c, :, :], psU[q % 2][HD:P, c, :, 1:NCH])
                    m.then_inc(s_late, 1)

                for q in range(n_seq + 3):
                    if q < n_seq:
                        for k in range(4):
                            u = 4 * q + k
                            act.wait_ge(s_tr, u + 1)
                            if q >= 2:
                                act.wait_ge(s_u, q - 1)
                            nc.scalar.copy(rT[:, q % 2, :, k * P:(k + 1) * P], psT[u % 2][:, :, :]).then_inc(s_rT, 1)
                    if 0 <= q - 1 < n_seq:
                        late_half(act, q - 1)
                    if 0 <= q - 2 < n_seq:
                        act.wait_ge(s_z, q - 1)
                        nc.scalar.activation(z3[:, :, q - 2], z[:, :, q - 2], ACT.Square).then_inc(s_sq, 1)
                    if 0 <= q - 3 < n_seq:
                        act.wait_ge(s_cu, q - 2)
                        nc.scalar.activation(z3[:, :, q - 3], z3[:, :, q - 3], ACT.Exp,
                                             scale=-2.0 * 0.7978845608028654).then_inc(s_ex, 1)
                act.wait_ge(s_out, 1)
                nc.scalar.copy(ck_hi[:, :, :], psP[:, 0, :, :])
                nc.scalar.copy(cv_p[0:NCMP, :, 0:HD], psP[0:NCMP, 1, :, :])
                nc.scalar.copy(cv_s[:, 0:4, :], psV[0][:, :, :])
                nc.scalar.copy(cv_s[:, 4:8, :], psV[1][:, :, :]).then_inc(s_fin, 1)

            @block.vector
            def _(dve):
                chain = Chain(dve, s_dve)
                nc.vector.memset(z[:, :, :, :, NCMP:NCH], 0.0)

                def pair(q):
                    n = DB // 2
                    dve.wait_ge(s_raw[q % RAW], 16 * (n * (q // RAW + 1) if q < DB else n * (q // RAW) + 1))
                    if q < DB:
                        dve.wait_ge(s_raw_odd[q % RAW], 16 * n * (q // RAW + 1))
                    if q >= 2:
                        dve.wait_ge(s_tr, 4 * (q - 1))
                    for k in range(4):
                        nc.vector.tensor_copy(paired[:, q % 2, k], raw[:, q % RAW, k].rearrange("p r c d -> p c r d")
                                              ).then_inc(s_pair, 1)

                pair(0)
                for q in range(n_seq + 3):
                    if q + 1 < n_seq:
                        pair(q + 1)
                    if q == 1:
                        dve.wait_ge(s_pe, 1)
                        nc.vector.tensor_copy(pe_b[:, :], psE[:, :]).then_inc(s_peb, 1)
                        dve.wait_ge(s_peb, 1)
                    if 0 <= q - 1 < n_seq:
                        dve.wait_ge(s_late, q)
                        for c in range(2):
                            m = nc.vector.scalar_tensor_tensor(z[:, c, q - 1, :, 0:NCMP], psU[(q - 1) % 2][0:HD, c, :, 0:NCMP],
                                                               pe_b[:, c:c + 1], late[:, c, :, :], ALU.add, ALU.add)
                        m.then_inc(s_z, 1)
                    if 0 <= q - 2 < n_seq:
                        w = z3[:, :, q - 2]
                        dve.wait_ge(s_sq, q - 1)
                        chain(nc.vector.tensor_scalar(w, w, 0.044715, 1.0, ALU.mult, ALU.add))
                        nc.vector.tensor_tensor(w, w, z[:, :, q - 2], ALU.mult).then_inc(s_cu, 1)
                    if 0 <= q - 3 < n_seq:
                        w = z3[:, :, q - 3]
                        dve.wait_ge(s_ex, q - 2)
                        chain(nc.vector.tensor_scalar(w, w, 1.0, None, ALU.add))
                        chain(nc.vector.reciprocal(w, w))
                        nc.vector.tensor_tensor(w, w, z[:, :, q - 3], ALU.mult).then_inc(s_ge, 1)
                dve.wait_ge(s_fin, 1)
                nc.vector.tensor_copy(ck_s[:, :, :], psT[0][:, :, :].rearrange("p a b -> p (a b)").rearrange("p (b n) -> p b n", b=DB))
                nc.vector.tensor_tensor(ck_lo[:, :, :], psP[:, 0, :, :], ck_hi[:, :, :].bitcast(F32), ALU.subtract)
                chain(nc.vector.tensor_tensor(cv_p[0:NCMP, :, HD:P], psP[0:NCMP, 1, :, :],
                                              cv_p[0:NCMP, :, 0:HD].bitcast(F32), ALU.subtract))


N_SEL = PAST + DT
N_WIN = WIN + DT
S_WIN0 = N_SEL
S_CMP0 = N_SEL + N_WIN
S_COLS = S_CMP0 + NCH
N_MID = PAST // SELB - 2


def sample_attention(nc, t, ident, table, o, yq, q_rot, ck_s, cv_s, aT):
    R = NH * DT
    KV = 3
    with ExitStack() as ctx:
        ph = Phase(nc, ctx, "smp")
        same = ph.sb("same", [R, R])
        mask = ph.sb("mask", [R, S_COLS])
        block_no = ph.sb("block_no", [R, N_MID])
        gate_tok = ph.sb("gate_tok", [R, 3 * NH])
        gate = ph.sb("gate", [R, DB, 3])
        q_pair = ph.sb("q_pair", [R, 2, HPG, NG, HD])
        q_bd = ph.sb("q_bd", [P, 2, DB, R])
        sel = ph.sb("sel", [P, KV, PAST // P, KVW])
        win = ph.sb("win", [P, KV, WIN // P, KVW])
        new = ph.sb("new", [DT, KV, 2, KVW])
        kT = ph.sb("kT", [P, 2, N_SEL + N_WIN])
        sc = ph.sb("sc", [R, 2, S_COLS])
        stat = ph.sb("stat", [R, 2, 16])
        mid = ph.sb("mid", [R, 2, NCH])
        imp = ph.sb("imp", [R, 2, 4, N_MID])
        pT = ph.sb("pT", [P, 2, 15, R])
        a_rows = ph.sb("a_rows", [R, DB, HD])
        scratch = nc.dram_tensor("gate_scratch", (R, 3 * NH), F32, kind="Internal").ap()
        psS = ph.ps("psS", [R, 4, 512])
        psT = [ph.ps(f"psT{k}", [P, 512]) for k in range(2)]
        psO = ph.ps("psO", [R, P])
        psI = ph.ps("psI", [P, 512])
        s_c = ph.sem("constants_loaded")
        s_kv = [ph.sem(f"even_pages_slot{k}_loaded") for k in range(KV)]
        s_kv_odd = [ph.sem(f"odd_pages_slot{k}_loaded") for k in range(KV)]
        s_ge = ph.sem("gate_exp")
        s_gt = ph.sem("gate_made")
        s_gw = ph.sem("gate_stored")
        s_gr = ph.sem("gate_read")
        s_qp = ph.sem("q_paired")
        s_qt = ph.sem("q_transposed")
        s_qz = ph.sem("q_zeroed")
        s_qb = ph.sem("q_blocks_written")
        s_kt = ph.sem("keys_transposed")
        s_kc = ph.sem("keys_copied")
        s_s = ph.sem("scores_made")
        s_sm = ph.sem("scores_masked")
        s_mc = ph.sem("cmp_max")
        s_ec = ph.sem("cmp_exp")
        s_pc = ph.sem("cmp_probs")
        s_i = ph.sem("importance_summed")
        s_ic = ph.sem("importance_copied")
        s_m = ph.sem("maxima")
        s_e = ph.sem("exps")
        s_p = ph.sem("probs_scaled")
        s_pt = ph.sem("probs_transposed")
        s_pq = ph.sem("pT_copied")
        s_o = ph.sem("output_multiplied")
        s_a = ph.sem("output_copied")
        s_at = ph.sem("outputs_transposed")
        s_af = ph.sem("aT_written")
        s_dve = ph.sem("vector_chain")
        i_s = NT - 1
        cache = t["cache_sel_kv"][0].rearrange("n p u g d -> n p (u g d)")
        cwin = t["cache_win_kv"][0].rearrange("b (k p) u g d -> b p k (u g d)", p=P)
        new_sel = o["s_sel_kv"][0].rearrange("b n u g d -> b n (u g d)")
        new_win = o["s_win_kv"][0].rearrange("b n u g d -> b n (u g d)")
        blocks = ([(k * P, P, lambda b, k=k: sel[:, b % KV, k, P:KVW]) for k in range(8)]
                  + [(PAST, DT, lambda b: new[:, b % KV, 0, P:KVW]), (S_WIN0 + WIN, DT, lambda b: new[:, b % KV, 1, P:KVW])]
                  + [(S_WIN0 + k * P, P, lambda b, k=k: win[:, b % KV, k, P:KVW]) for k in range(4)]
                  + [(S_CMP0, HD, lambda b: cv_s[:, b, :])])
        key_src = ([(k * P, P, lambda b, k=k: sel[:, b % KV, k, 0:P]) for k in range(8)]
                   + [(PAST, DT, lambda b: new[:, b % KV, 0, 0:P])]
                   + [(S_WIN0 + k * P, P, lambda b, k=k: win[:, b % KV, k, 0:P]) for k in range(4)]
                   + [(S_WIN0 + WIN, DT, lambda b: new[:, b % KV, 1, 0:P])])
        key_sets = [key_src[0:4], key_src[4:8], key_src[8:12], key_src[12:14]]
        n_odd = PAST // PAGE // 2
        n_even = n_odd + 3
        with nc.Block() as block:

            def load_pages(eng, first, b, queue_sem):
                if b >= KV:
                    eng.wait_ge(s_o, b - KV + 1)
                for n in range(first, PAST // PAGE, 2):
                    page = eng.value_load(table[0:1, b * DB + n:b * DB + n + 1], min_val=0,
                                          max_val=cache.shape[0] - 1)
                    eng.dma_start(sel[:, b % KV, n, :], cache[bass.DynSlice(page, 1)].rearrange("a p f -> (a p) f")
                                  ).then_inc(queue_sem[b % KV], 16)

            @block.sync
            def _(sp):
                for b in range(DB):
                    load_pages(sp, 0, b, s_kv)
                    sp.dma_start(win[:, b % KV], cwin[b]).then_inc(s_kv[b % KV], 16)
                    sp.dma_start(new[:, b % KV, 0, :], new_sel[b]).then_inc(s_kv[b % KV], 16)
                    sp.dma_start(new[:, b % KV, 1, :], new_win[b, WIN - DT:WIN]).then_inc(s_kv[b % KV], 16)

            @block.gpsimd
            def _(pool):
                q = yq[0:R, i_s, C_Q:C_Q + AW].rearrange("p (g h d) -> p h g d", g=NG, h=HPG)
                nc.gpsimd.tensor_copy(q_pair[:, 0], q).then_inc(s_qp, 1)
                nc.gpsimd.tensor_copy(q_pair[:, 1], q).then_inc(s_qp, 1)
                pool.wait_ge(s_qp, 2)
                nc.gpsimd.tensor_copy(q_pair[:, 1, :, :, 0:ROT],
                                      q_rot[0:R, i_s].rearrange("p (g h) e -> p h g e", g=NG)).then_inc(s_qp, 1)
                load_pages(pool, 1, 0, s_kv_odd)
                load_pages(pool, 1, 1, s_kv_odd)
                pool.wait_ge(s_gt, 1)
                pool.dma_start(scratch, gate_tok[:, :]).then_inc(s_gw, 16)
                pool.wait_ge(s_gw, 16)
                for h in range(NH):
                    pool.dma_start(gate[h * DT:(h + 1) * DT, :, :],
                                   scratch.rearrange("(b t) (h j) -> h t b j", b=DB, h=NH)[h],
                                   allow_slow_non_contiguous=True).then_inc(s_gr, 16)
                for b in range(2, DB):
                    load_pages(pool, 1, b, s_kv_odd)

            @block.tensor
            def _(pe):
                pe.wait_ge(s_qp, 3)
                for v in range(2):
                    for h in range(HPG):
                        m = nc.tensor.transpose(psT[v][:, h * R:(h + 1) * R],
                                                q_pair[:, v, h].rearrange("p g d -> p (g d)"), ident[0:R, 0:R])
                    m.then_inc(s_qt, 1)
                pe.wait_ge(s_qb, 4)

                def keys(b):
                    pe.wait_ge(s_kv[b % KV], 16 * n_even * (b // KV + 1))
                    pe.wait_ge(s_kv_odd[b % KV], 16 * n_odd * (b // KV + 1))
                    for k, members in enumerate(key_sets):
                        u = 4 * b + k
                        if u >= 2:
                            pe.wait_ge(s_kc, u - 1)
                        if b >= 2 and k < 2:
                            pe.wait_ge(s_pq, 2 * (b - 1))
                        for m_i, (c0, n, src) in enumerate(members):
                            m = nc.tensor.transpose(psT[k % 2][:, m_i * P:m_i * P + n], src(b), ident[0:n, 0:n])
                        m.then_inc(s_kt, 1)

                def scores(b):
                    pe.wait_ge(s_kc, 4 * (b + 1))
                    if b:
                        pe.wait_ge(s_sm, b)
                    c = 0
                    while c < S_COLS:
                        end = min(S_COLS, (c // 512 + 1) * 512, *[x for x in (S_WIN0, S_CMP0) if x > c] or [S_COLS])
                        if c >= S_CMP0:
                            q, k = q_bd[:, 0, b, :], ck_s[:, b, c - S_CMP0:end - S_CMP0]
                        else:
                            q, k = q_bd[:, 1, b, :], kT[:, b % 2, c:end]
                        m = nc.tensor.matmul(psS[:, c // 512, c % 512:c % 512 + end - c], q, k, start=True, stop=True)
                        c = end
                    m.then_inc(s_s, 1)

                def importance(b):
                    pe.wait_ge(s_pc, b + 1)
                    if b:
                        pe.wait_ge(s_ic, b)
                    nc.tensor.matmul(psI[0:R, 0:NCH], same[:, :], sc[:, b % 2, S_CMP0:S_COLS],
                                     start=True, stop=True).then_inc(s_i, 1)

                def prob_transposes(b):
                    pe.wait_ge(s_p, b + 1)
                    for v in range(2):
                        for m_i, (c0, n, _) in enumerate(blocks[8 * v:8 * v + 8]):
                            m = nc.tensor.transpose(psT[v][0:n, m_i * R:(m_i + 1) * R], sc[:, b % 2, c0:c0 + n],
                                                    ident[0:R, 0:R])
                        m.then_inc(s_pt, 1)

                def values(b):
                    if b:
                        pe.wait_ge(s_a, 2 * b)
                    for m_i, (c0, n, val) in enumerate(blocks):
                        if m_i % 8 == 0:
                            pe.wait_ge(s_pq, 2 * b + m_i // 8 + 1)
                        m = nc.tensor.matmul(psO[:, :], pT[0:n, b % 2, m_i, :], val(b), start=(m_i == 0),
                                             stop=(m_i == len(blocks) - 1))
                    m.then_inc(s_o, 1)

                keys(0)
                scores(0)
                keys(1)
                pe.wait_ge(s_c, 48)
                importance(0)
                for b in range(DB):
                    if b + 1 < DB:
                        scores(b + 1)
                    prob_transposes(b)
                    if b + 1 < DB:
                        importance(b + 1)
                    if b + 2 < DB:
                        keys(b + 2)
                    values(b)
                pe.wait_ge(s_a, 2 * DB)
                for b in range(DB):
                    m = nc.tensor.transpose(psI[0:HD, b * R:(b + 1) * R], a_rows[:, b, :], ident[0:R, 0:R])
                m.then_inc(s_at, 1)

            @block.scalar
            def _(act):
                act.dma_start(mask[:, :], t["k_smask"]).then_inc(s_c, 16)
                act.dma_start(same[:, :], t["k_same"]).then_inc(s_c, 16)
                act.dma_start(block_no[:, :], t["k_block_no"]).then_inc(s_c, 16)
                nc.scalar.activation(gate_tok[:, :], yq[0:R, i_s, C_GL:C_PI], ACT.Exp, scale=-1.0).then_inc(s_ge, 1)

                def copy_keys(b):
                    for k, members in enumerate(key_sets):
                        act.wait_ge(s_kt, 4 * b + k + 1)
                        c0 = members[0][0]
                        n = sum(x[1] for x in members)
                        if b >= 2 and k == 0:
                            act.wait_ge(s_s, b - 1)
                        if k < 2:
                            m = nc.scalar.copy(kT[:, b % 2, c0:c0 + n], psT[k % 2][:, 0:n])
                        elif k == 2:
                            nc.scalar.copy(kT[:, b % 2, c0:c0 + DT], psT[0][:, 0:DT])
                            m = nc.scalar.copy(kT[:, b % 2, S_WIN0:S_WIN0 + 3 * P], psT[0][:, P:4 * P])
                        else:
                            m = nc.scalar.copy(kT[:, b % 2, c0:c0 + n], psT[1][:, 0:n])
                        m.then_inc(s_kc, 1)

                def cmp_exp(b):
                    st = stat[:, b % 2]
                    act.wait_ge(s_mc, b + 1)
                    nc.scalar.activation(sc[:, b % 2, S_CMP0:S_COLS], sc[:, b % 2, S_CMP0:S_COLS], ACT.Exp,
                                         bias=st[:, 3:4], scale=SCALE, accum_out=st[:, 4:5]).then_inc(s_ec, 1)

                copy_keys(0)
                copy_keys(1)
                cmp_exp(0)
                for b in range(DB):
                    st = stat[:, b % 2]
                    act.wait_ge(s_m, b + 1)
                    for v, (c0, c1) in enumerate(((0, N_SEL), (S_WIN0, S_CMP0))):
                        nc.scalar.activation(sc[:, b % 2, c0:c1], sc[:, b % 2, c0:c1], ACT.Exp, bias=st[:, 8 + v:9 + v],
                                             scale=SCALE, accum_out=st[:, 10 + v:11 + v]).then_inc(s_e, 1)
                    if b + 1 < DB:
                        cmp_exp(b + 1)
                    act.wait_ge(s_pt, 2 * b + 1)
                    if b >= 2:
                        act.wait_ge(s_o, b - 1)
                    nc.scalar.copy(pT[:, b % 2, 0:8, :], psT[0][:, :].rearrange("p (m r) -> p m r", r=R)).then_inc(s_pq, 1)
                    act.wait_ge(s_pt, 2 * b + 2)
                    nc.scalar.copy(pT[0:DT, b % 2, 8:10, :], psT[1][0:DT, 0:2 * R].rearrange("p (m r) -> p m r", r=R))
                    nc.scalar.copy(pT[:, b % 2, 10:14, :], psT[1][:, 2 * R:6 * R].rearrange("p (m r) -> p m r", r=R))
                    nc.scalar.copy(pT[0:HD, b % 2, 14, :], psT[1][0:HD, 6 * R:7 * R]).then_inc(s_pq, 1)
                    if b + 2 < DB:
                        copy_keys(b + 2)
                act.wait_ge(s_at, 1)
                src = psI[0:HD, :].rearrange("d (b m e s) -> d b m e s", b=DB, m=4, e=2)
                dst = aT[:, :, SEQ:TOK].rearrange("d m (b s) -> d b m s", b=DB)
                nc.scalar.copy(dst[0:HD], src[:, :, :, 0])
                nc.scalar.copy(dst[HD:P], src[:, :, :, 1]).then_inc(s_af, 1)
                act.wait_ge(s_af, 1)

            @block.vector
            def _(dve):
                chain = Chain(dve, s_dve)
                nc.vector.memset(q_bd[:, :, :, :], 0.0).then_inc(s_qz, 1)
                dve.wait_ge(s_ge, 1)
                chain(nc.vector.tensor_scalar(gate_tok[:, :], gate_tok[:, :], 1.0, None, ALU.add))
                nc.vector.reciprocal(gate_tok[:, :], gate_tok[:, :]).then_inc(s_gt, 1)
                dve.wait_ge(s_qz, 1)
                for v in range(2):
                    dve.wait_ge(s_qt, v + 1)
                    src = psT[v][:, 0:HPG * R].rearrange("p (h b s) -> p b h s", h=HPG, b=DB)
                    for g in range(NG):
                        dst = q_bd[g * HD:(g + 1) * HD, v, :, g * 32:(g + 1) * 32].rearrange("p b (h s) -> p b h s", h=HPG)
                        nc.vector.tensor_copy(dst, src[g * HD:(g + 1) * HD]).then_inc(s_qb, 1)
                dve.wait_ge(s_c, 48)

                def cmp_max(b):
                    st, S = stat[:, b % 2], sc[:, b % 2]
                    dve.wait_ge(s_s, b + 1)
                    if b >= 2:
                        dve.wait_ge(s_pt, 2 * (b - 1))
                    flat = psS[:, :, :].rearrange("p a b -> p (a b)")
                    nc.vector.tensor_tensor(S, flat[:, 0:S_COLS], mask[:, :], ALU.add).then_inc(s_sm, 1)
                    dve.wait_ge(s_sm, b + 1)
                    chain(nc.vector.reduce_max(st[:, 2:3], S[:, S_CMP0:S_COLS], AX.X, negate=True))
                    nc.vector.tensor_scalar(st[:, 3:4], st[:, 2:3], SCALE, None, ALU.mult).then_inc(s_mc, 1)

                def cmp_probs(b):
                    st, S = stat[:, b % 2], sc[:, b % 2]
                    dve.wait_ge(s_ec, b + 1)
                    chain(nc.vector.reciprocal(st[:, 5:6], st[:, 4:5]))
                    nc.vector.tensor_scalar(S[:, S_CMP0:S_COLS], S[:, S_CMP0:S_COLS], st[:, 5:6], None,
                                            ALU.mult).then_inc(s_pc, 1)

                def selection(b):
                    st, S = stat[:, b % 2], sc[:, b % 2]
                    nc.vector.reduce_max(st[:, 13:14], S[:, S_WIN0:S_CMP0], AX.X, negate=True)
                    dve.wait_ge(s_i, b + 1)
                    w = mid[:, b % 2]
                    nc.vector.tensor_copy(w, psI[0:R, 0:NCH]).then_inc(s_ic, 1)
                    dve.wait_ge(s_ic, b + 1)
                    quad = w.rearrange("p (j e) -> p j e", e=4)
                    whole, halves, total, drop = (imp[:, b % 2, x] for x in range(4))
                    nc.vector.reduce_sum(whole, quad[:, 1:1 + N_MID, 0:3], AX.X)
                    chain(nc.vector.tensor_tensor(halves, quad[:, 1:1 + N_MID, 3], quad[:, 0:N_MID, 3], ALU.add))
                    chain(nc.vector.scalar_tensor_tensor(total, halves, SELB / 4 / CLEN, whole, ALU.mult, ALU.add))
                    chain(nc.vector.tensor_reduce(st[:, 6:7], total, AX.X, ALU.min))
                    chain(nc.vector.scalar_tensor_tensor(drop, total, st[:, 6:7], block_no[:, :], ALU.is_equal, ALU.mult))
                    chain(nc.vector.reduce_max(st[:, 7:8], drop, AX.X))
                    chain(nc.vector.tensor_scalar(drop, block_no[:, :], st[:, 7:8], NEG, ALU.is_equal, ALU.mult))
                    body = S[:, SELB:SELB * (1 + N_MID)].rearrange("p (j e) -> p j e", e=SELB)
                    chain(nc.vector.tensor_tensor(body, body, drop.unsqueeze(2).broadcast_to([R, N_MID, SELB]), ALU.add))
                    chain(nc.vector.reduce_max(st[:, 12:13], S[:, 0:N_SEL], AX.X, negate=True))
                    nc.vector.tensor_scalar(st[:, 8:10], st[:, 12:14], SCALE, None, ALU.mult).then_inc(s_m, 1)

                def scale_probs(b):
                    st, S = stat[:, b % 2], sc[:, b % 2]
                    dve.wait_ge(s_e, 2 * (b + 1))
                    if b == 0:
                        dve.wait_ge(s_gr, 16 * NH)
                    chain(nc.vector.reciprocal(st[:, 14:16], st[:, 10:12]))
                    chain(nc.vector.tensor_tensor(st[:, 14:16], st[:, 14:16], gate[:, b, 1:3], ALU.mult))
                    nc.vector.tensor_scalar(S[:, 0:N_SEL], S[:, 0:N_SEL], st[:, 14:15], None, ALU.mult)
                    nc.vector.tensor_scalar(S[:, S_CMP0:S_COLS], S[:, S_CMP0:S_COLS], gate[:, b, 0:1], None, ALU.mult)
                    nc.vector.tensor_scalar(S[:, S_WIN0:S_CMP0], S[:, S_WIN0:S_CMP0], st[:, 15:16], None,
                                            ALU.mult).then_inc(s_p, 1)

                def keep_outputs(b):
                    dve.wait_ge(s_o, b + 1)
                    for g in range(NG):
                        nc.vector.tensor_copy(a_rows[g * 32:(g + 1) * 32, b, :],
                                              psO[g * 32:(g + 1) * 32, g * HD:(g + 1) * HD]).then_inc(s_a, 1)

                cmp_max(0)
                cmp_probs(0)
                for b in range(DB):
                    selection(b)
                    if b:
                        keep_outputs(b - 1)
                    scale_probs(b)
                    if b + 1 < DB:
                        cmp_max(b + 1)
                        cmp_probs(b + 1)
                keep_outputs(DB - 1)


WB = WIN // P + 1
P_WIN0 = SEQ
P_CMP0 = SEQ + WB * P
P_COLS = P_CMP0 + NCH


def prompt_attention(nc, t, ident, yq, q_rot, ck_hi, ck_lo, cv_p, aT):
    LAG = 2
    n_tiles = NT - 1
    units = [(i, g) for i in range(n_tiles) for g in range(NG)]

    def key_blocks(u):
        i, _ = units[u]
        first = max(0, i - WB + 1)
        return ([(kb * P, 0, kb) for kb in range(i + 1)]
                + [(P_WIN0 + (kb - first) * P, 1, kb) for kb in range(first, i + 1)] + [(P_CMP0, 2, 0)])

    base = [0]
    for u in range(len(units)):
        base.append(base[-1] + len(key_blocks(u)))

    def steps():
        for s in range(3):
            yield "prep", (0, s)
        for u in range(len(units) + 1):
            blocks = list(range(len(key_blocks(u - 1)))) if u else []
            prep = []
            if u < len(units):
                i, g = units[u]
                prep = [(i, 3), (i, 4)] if g == 0 else [(i + 1, s) for s in range(3) if i + 1 < n_tiles]
            shares = [blocks[k * len(blocks) // 16:(k + 1) * len(blocks) // 16] for k in range(16)]
            for hh in range(HPG):
                live = u < len(units)
                if live:
                    yield "sel scores", (u, hh)
                if hh == 0 and u >= 2:
                    yield "drain", (u - 2, 0)
                kinds = (("sel max", "win scores"), ("sel exp", "win max"), ("win exp",), ("scale",))
                for k in range(4):
                    for b in shares[4 * hh + k]:
                        yield "block", (u - 1, b)
                    for kind in kinds[k] if live else ():
                        yield kind, (u, hh)
                    if prep and k == 1:
                        yield "prep", prep.pop(0)
        yield "drain", (len(units) - 1, 0)

    def cols_of(i):
        return (i + 1) * P, (min(i, WB - 1) + 1) * P

    with ExitStack() as ctx:
        ph = Phase(nc, ctx, "att")
        identR = ph.sb("identR", [P, P], F32R)
        n_mask = 2 * P + n_tiles * NCH
        masksR = ph.sb("masksR", [P, n_mask], F32R)
        causal, oldest = masksR[:, 0:P], masksR[:, P:2 * P]
        gate = ph.sb("gate", [P, n_tiles, NH, 3])
        q_dup = ph.sb("q_dup", [P, 2, NH, 2, HD])
        k_dup = ph.sb("k_dup", [P, 2, NG, 2, HD])
        qS = ph.sb("qS", [P, 2, NH, P], F32R)
        k_hi = ph.sb("k_hi", [P, 2, NG, SEQ], F32R)
        k_lo = ph.sb("k_lo", [P, 2, NG, SEQ], F32R)
        v_st = ph.sb("v_st", [P, 2, n_tiles, NG, P], F32R)
        prob = ph.sb("prob", [P, 2 * HPG, P_COLS])
        stat = ph.sb("stat", [P, 2 * HPG, 16])
        pT_hi = ph.sb("pT_hi", [P, LAG + 1, 4 * P], F32R)
        pT_lo = ph.sb("pT_lo", [P, LAG + 1, 4 * P], F32R)
        other = ph.sb("other", [P, 2, P])
        psA = ph.ps("psA", [P, 2, 512])
        psB = ph.ps("psB", [P, 2, 512])
        psT = [ph.ps(f"psT{k}", [P, 4, P]) for k in range(3)]
        psO = ph.ps("psO", [P, 4, P])
        flatA = psA[:, :, :].rearrange("p a b -> p (a b)")
        flatB = psB[:, :, :].rearrange("p a b -> p (a b)")

        def places(i, n):
            a = (512 * (n % 2), 2) if (i + 1) * P <= 512 else (0, 1)
            nwin = cols_of(i)[1]
            b = (512 * (n % 2), 512 * (n % 2) + nwin, 2) if nwin + NCH <= 512 else (0, WB * P, 1)
            return *a, *b
        s_c = ph.sem("constants_loaded")
        s_mr = ph.sem("masks_rounded")
        s_ge = ph.sem("gate_exp")
        s_g = ph.sem("gate_made")
        s_qd = ph.sem("queries_doubled")
        s_kd = ph.sem("keys_doubled")
        s_qt = ph.sem("prep_transposed")
        s_qh = ph.sem("prep_hi_made")
        s_ql = ph.sem("prep_lo_made")
        s_vh = ph.sem("value_hi_made")
        s_sa = ph.sem("sel_scores_made")
        s_sb = ph.sem("win_cmp_scores_made")
        s_ma = ph.sem("sel_max_made")
        s_mb = ph.sem("win_cmp_max_made")
        s_ea = ph.sem("sel_exp_made")
        s_eb = ph.sem("win_cmp_exp_made")
        s_f = ph.sem("factors_made")
        s_pv = ph.sem("probs_scaled_by_vector")
        s_pp = ph.sem("probs_scaled_by_pool")
        s_pt = ph.sem("probs_transposed")
        s_th = ph.sem("pT_hi_made")
        s_tl = ph.sem("pT_lo_made")
        s_o = ph.sem("unit_output_made")
        s_oc = ph.sem("other_halves_copied")
        s_od = ph.sem("output_drained")
        s_dve = ph.sem("vector_chain")

        def prep_no(arg):
            return 5 * arg[0] + arg[1]

        bank, drained = {}, []
        for kind, arg in steps():
            if kind in ("block", "prep"):
                bank[kind, arg] = psT[len(drained) % len(psT)]
                drained.append((s_tl, base[arg[0]] + arg[1] + 1) if kind == "block" else (s_ql, prep_no(arg) + 1))

        with nc.Block() as block:

            @block.sync
            def _(sp):
                sp.dma_start(prob[:, 0, 0:n_mask], t["k_pmask"]).then_inc(s_c, 16)

            @block.gpsimd
            def _(pool):
                def double_keys(i):
                    if i:
                        pool.wait_ge(s_qt, 5 * (i - 1) + 1)
                    k = yq[:, i, C_KS:C_KS + 2 * KVW].rearrange("p (b u g d) -> p b u g d", b=2, u=2, g=NG)[:, :, 0]
                    for b in range(2):
                        m = nc.gpsimd.tensor_copy(k_dup[:, b], k[:, b].unsqueeze(2).broadcast_to([P, NG, 2, HD]))
                    m.then_inc(s_kd, 1)

                def double_queries(i):
                    if i:
                        pool.wait_ge(s_qt, 5 * i)
                    q = yq[:, i, C_Q:C_Q + AW].rearrange("p (h d) -> p h d", d=HD).unsqueeze(2)
                    r = q_rot[:, i].unsqueeze(2).broadcast_to([P, NH, 2, ROT])
                    nc.gpsimd.tensor_copy(q_dup[:, 0], q.broadcast_to([P, NH, 2, HD]))
                    nc.gpsimd.tensor_copy(q_dup[:, 1, :, :, ROT:HD], q[:, :, :, ROT:HD].broadcast_to([P, NH, 2, HD - ROT]))
                    nc.gpsimd.tensor_copy(q_dup[:, 1, :, :, 0:ROT], r).then_inc(s_qd, 1)

                double_keys(0)
                double_queries(0)
                for kind, arg in steps():
                    if kind == "prep" and arg[1] == 1 and arg[0] + 1 < n_tiles:
                        double_keys(arg[0] + 1)
                    if kind == "prep" and arg[1] == 4 and arg[0] + 1 < n_tiles:
                        double_queries(arg[0] + 1)
                    if kind == "scale":
                        (u, hh), (i, g) = arg, units[arg[0]]
                        n = HPG * u + hh
                        slot = n % (2 * HPG)
                        pool.wait_ge(s_f, n + 1)
                        if hh < HPG - 1:
                            nc.gpsimd.tensor_scalar(prob[:, slot, 0:cols_of(i)[0]], prob[:, slot, 0:cols_of(i)[0]],
                                                    stat[:, slot, 13:14], 1.0, ALU.mult, ALU.mult)
                        c1 = P_WIN0 + cols_of(i)[1]
                        nc.gpsimd.tensor_scalar(prob[:, slot, P_WIN0:c1], prob[:, slot, P_WIN0:c1],
                                                stat[:, slot, 14:15], 1.0, ALU.mult, ALU.mult)
                        nc.gpsimd.tensor_scalar(prob[:, slot, P_CMP0:P_COLS], prob[:, slot, P_CMP0:P_COLS],
                                                stat[:, slot, 12:13], 1.0, ALU.mult, ALU.mult).then_inc(s_pp, 1)

            @block.tensor
            def _(pe):
                def product(u, arg):
                    i, g = units[u]
                    c0, branch, kb = key_blocks(u)[arg]
                    n = base[u] + arg
                    last = arg == len(key_blocks(u)) - 1
                    rows = NCMP if branch == 2 else P
                    val = cv_p[0:NCMP, g, :] if branch == 2 else v_st[:, branch, kb, g, :]
                    pe.wait_ge(s_th, n + 1)
                    if arg == 0 and u:
                        pe.wait_ge(s_od, u)
                    out = psO[:, :, :].rearrange("p a b -> p (a b)")
                    nc.tensor.matmul(out, val, pT_hi[0:rows, n % (LAG + 1), :], start=(arg == 0), stop=False)
                    pe.wait_ge(s_tl, n + 1)
                    m = nc.tensor.matmul(out, val, pT_lo[0:rows, n % (LAG + 1), :], start=False, stop=last)
                    if last:
                        m.then_inc(s_o, 1)

                pe.wait_ge(s_c, 16)
                pe.wait_ge(s_mr, 2)
                fill = 0
                for kind, arg in steps():
                    if kind in ("block", "prep"):
                        if fill >= len(psT):
                            pe.wait_ge(*drained[fill - len(psT)])
                        fill += 1
                    if kind == "prep":
                        i, s = arg
                        pe.wait_ge(s_kd if s == 0 else s_qd, i + 1)
                        for x in range(4):
                            src = k_dup[:, x // 2, x % 2] if s == 0 else q_dup[:, (s - 1) % 2, 4 * ((s - 1) // 2) + x]
                            m = nc.tensor.transpose(bank[kind, arg][:, x, :], src.rearrange("p a b -> p (a b)"), ident[:, :])
                        m.then_inc(s_qt, 1)
                    elif kind == "sel scores":
                        (u, hh), (i, g) = arg, units[arg[0]]
                        n = HPG * u + hh
                        h = HPG * g + hh
                        nsel, _ = cols_of(i)
                        pe.wait_ge(s_ql, 5 * i + (3 if g == 0 else 5))
                        a0, room, *_ = places(i, n)
                        if n >= room:
                            pe.wait_ge(s_ea, n - room + 1)
                        q = qS[:, 1, h, :]
                        for c in range(0, nsel, 512):
                            e = min(c + 512, nsel)
                            nc.tensor.matmul(flatA[:, a0 + c:a0 + e], q, k_hi[:, 0, g, c:e], start=True, stop=False)
                            m = nc.tensor.matmul(flatA[:, a0 + c:a0 + e], q, k_lo[:, 0, g, c:e], start=False, stop=(e < nsel))
                        m = nc.tensor.matmul(flatA[:, a0 + nsel - P:a0 + nsel], identR[:, :], causal, start=False, stop=True)
                        m.then_inc(s_sa, 1)
                    elif kind == "win scores":
                        (u, hh), (i, g) = arg, units[arg[0]]
                        n = HPG * u + hh
                        h = HPG * g + hh
                        _, nwin = cols_of(i)
                        q = qS[:, 1, h, :]
                        _, _, b0, b1, room = places(i, n)
                        if n >= room:
                            pe.wait_ge(s_eb, n - room + 1)
                        k0 = (i + 1) * P - nwin
                        for c in range(0, nwin, 512):
                            e = min(c + 512, nwin)
                            nc.tensor.matmul(flatB[:, b0 + c:b0 + e], q, k_hi[:, 1, g, k0 + c:k0 + e], start=True, stop=False)
                            nc.tensor.matmul(flatB[:, b0 + c:b0 + e], q, k_lo[:, 1, g, k0 + c:k0 + e], start=False, stop=False)
                            if c == 0 and nwin == WB * P:
                                nc.tensor.matmul(flatB[:, b0:b0 + P], identR[:, :], oldest, start=False, stop=True)
                        nc.tensor.matmul(flatB[:, b0 + nwin - P:b0 + nwin], identR[:, :], causal, start=False, stop=True)
                        out = flatB[:, b1:b1 + NCH]
                        qc = qS[:, 0, h, :]
                        nc.tensor.matmul(out, qc, ck_hi[:, g, :], start=True, stop=False)
                        nc.tensor.matmul(out, qc, ck_lo[:, g, :], start=False, stop=False)
                        nc.tensor.matmul(out, identR[:, :], masksR[:, 2 * P + i * NCH:2 * P + (i + 1) * NCH],
                                         start=False, stop=True).then_inc(s_sb, 1)
                    elif kind == "block":
                        u, b = arg
                        n = base[u] + b
                        c0, branch, _ = key_blocks(u)[b]
                        w = NCH if branch == 2 else P
                        if b == 0:
                            pe.wait_ge(s_pv, u + 1)
                            pe.wait_ge(s_pp, HPG * (u + 1))
                        for hh in range(HPG):
                            m = nc.tensor.transpose(bank[kind, arg][0:w, hh, :], prob[:, HPG * (u % 2) + hh, c0:c0 + w],
                                                    ident[:, :])
                        m.then_inc(s_pt, 1)
                        if b >= LAG:
                            product(u, b - LAG)
                    elif kind == "drain":
                        n_b = len(key_blocks(arg[0]))
                        for b in range(max(0, n_b - LAG), n_b):
                            product(arg[0], b)

            @block.scalar
            def _(act):
                act.wait_ge(s_c, 16)
                nc.scalar.copy(identR[:, :], ident[:, :]).then_inc(s_mr, 1)
                nc.scalar.copy(masksR[:, :], prob[:, 0, 0:n_mask]).then_inc(s_mr, 1)
                act.wait_ge(s_mr, 2)
                nc.scalar.activation(gate[:, :, :, :].rearrange("p i h j -> p i (h j)"), yq[:, 0:n_tiles, C_GL:C_PI],
                                     ACT.Exp, scale=-1.0).then_inc(s_ge, 1)
                for kind, arg in steps():
                    if kind == "prep":
                        i, s = arg
                        p = prep_no(arg)
                        act.wait_ge(s_qt, p + 1)
                        if s == 0:
                            dst = k_hi[:, :, :, i * P:(i + 1) * P]
                            nc.scalar.copy(dst, bank[kind, arg][:, :, :].rearrange("p (b g) t -> p b g t", b=2)).then_inc(s_qh, 1)
                            v = yq[:, i, C_KS:C_KS + 2 * KVW].rearrange("p (b u g d) -> p b u g d", b=2, u=2, g=NG)[:, :, 1]
                            nc.scalar.copy(v_st[:, :, i, :, 0:HD], v).then_inc(s_vh, 1)
                        else:
                            dst = qS[:, (s - 1) % 2, 4 * ((s - 1) // 2):4 * ((s - 1) // 2) + 4, :]
                            nc.scalar.mul(dst, bank[kind, arg][:, :, :], SCALE).then_inc(s_qh, 1)
                    elif kind == "sel exp":
                        (u, hh), (i, g) = arg, units[arg[0]]
                        n = HPG * u + hh
                        slot = n % (2 * HPG)
                        nsel, _ = cols_of(i)
                        a0 = places(i, n)[0]
                        act.wait_ge(s_ma, n + 1)
                        nc.scalar.activation(prob[:, slot, 0:nsel], flatA[:, a0:a0 + nsel], ACT.Exp, bias=stat[:, slot, 1:2],
                                             accum_out=stat[:, slot, 5:6]).then_inc(s_ea, 1)
                    elif kind == "win exp":
                        (u, hh), (i, g) = arg, units[arg[0]]
                        n = HPG * u + hh
                        slot = n % (2 * HPG)
                        _, nwin = cols_of(i)
                        _, _, b0, b1, _ = places(i, n)
                        act.wait_ge(s_mb, n + 1)
                        nc.scalar.activation(prob[:, slot, P_WIN0:P_WIN0 + nwin], flatB[:, b0:b0 + nwin], ACT.Exp,
                                             bias=stat[:, slot, 2:3], accum_out=stat[:, slot, 6:7])
                        nc.scalar.activation(prob[:, slot, P_CMP0:P_COLS], flatB[:, b1:b1 + NCH], ACT.Exp,
                                             bias=stat[:, slot, 0:1], accum_out=stat[:, slot, 4:5]).then_inc(s_eb, 1)
                    elif kind == "block":
                        u, b = arg
                        n = base[u] + b
                        w = NCH if key_blocks(u)[b][1] == 2 else P
                        act.wait_ge(s_pt, n + 1)
                        nc.scalar.copy(pT_hi[0:w, n % (LAG + 1), :], bank[kind, arg][0:w].rearrange("p a b -> p (a b)")).then_inc(s_th, 1)
                    elif kind == "drain":
                        u = arg[0]
                        act.wait_ge(s_o, u + 1)
                        if u:
                            act.wait_ge(s_od, u)
                        halves = psO[:, :, :].rearrange("p (m e) t -> p e m t", e=2)
                        nc.scalar.copy(other[0:HD], halves[HD:P, 0])
                        nc.scalar.copy(other[HD:P], halves[0:HD, 1]).then_inc(s_oc, 1)

            @block.vector
            def _(dve):
                chain = Chain(dve, s_dve)
                flat_gate = gate[:, :, :, :].rearrange("p i h j -> p (i h j)")
                dve.wait_ge(s_ge, 1)
                chain(nc.vector.tensor_scalar(flat_gate, flat_gate, 1.0, None, ALU.add))
                nc.vector.reciprocal(flat_gate, flat_gate).then_inc(s_g, 1)
                dve.wait_ge(s_g, 1)
                for kind, arg in steps():
                    if kind == "prep":
                        i, s = arg
                        p = prep_no(arg)
                        dve.wait_ge(s_qh, p + 1)
                        if s == 0:
                            dve.wait_ge(s_vh, i + 1)
                            v = yq[:, i, C_KS:C_KS + 2 * KVW].rearrange("p (b u g d) -> p b u g d", b=2, u=2, g=NG)[:, :, 1]
                            nc.vector.tensor_tensor(v_st[:, :, i, :, HD:P], v, v_st[:, :, i, :, 0:HD].bitcast(F32),
                                                    ALU.subtract)
                            nc.vector.tensor_tensor(k_lo[:, :, :, i * P:(i + 1) * P],
                                                    bank[kind, arg][:, :, :].rearrange("p (b g) t -> p b g t", b=2),
                                                    k_hi[:, :, :, i * P:(i + 1) * P].bitcast(F32),
                                                    ALU.subtract).then_inc(s_ql, 1)
                        else:
                            q = qS[HD:P, (s - 1) % 2, 4 * ((s - 1) // 2):4 * ((s - 1) // 2) + 4, :]
                            nc.vector.scalar_tensor_tensor(q, bank[kind, arg][HD:P, :, :], SCALE, q.bitcast(F32), ALU.mult,
                                                           ALU.subtract).then_inc(s_ql, 1)
                    elif kind == "sel max":
                        (u, hh), (i, g) = arg, units[arg[0]]
                        n = HPG * u + hh
                        st = stat[:, n % (2 * HPG), :]
                        nsel, _ = cols_of(i)
                        a0 = places(i, n)[0]
                        dve.wait_ge(s_sa, n + 1)
                        nc.vector.reduce_max(st[:, 1:2], flatA[:, a0:a0 + nsel], AX.X, negate=True).then_inc(s_ma, 1)
                    elif kind == "win max":
                        (u, hh), (i, g) = arg, units[arg[0]]
                        n = HPG * u + hh
                        st = stat[:, n % (2 * HPG), :]
                        _, nwin = cols_of(i)
                        _, _, b0, b1, _ = places(i, n)
                        dve.wait_ge(s_sb, n + 1)
                        m = nc.vector.reduce_max(st[:, 2:3], flatB[:, b0:b0 + nwin], AX.X, negate=True)
                        m = nc.vector.reduce_max(st[:, 0:1], flatB[:, b1:b1 + NCH], AX.X, negate=True)
                        if i == 0:
                            chain(m)
                            m = nc.vector.tensor_scalar(st[:, 0:1], st[:, 0:1], 1e20, None, ALU.min)
                        m.then_inc(s_mb, 1)
                    elif kind == "scale":
                        (u, hh), (i, g) = arg, units[arg[0]]
                        n = HPG * u + hh
                        slot = n % (2 * HPG)
                        st = stat[:, slot, :]
                        dve.wait_ge(s_eb, n + 1)
                        if i == 0:
                            chain(nc.vector.tensor_scalar(st[:, 4:7], st[:, 4:7], 1e-30, None, ALU.max))
                        chain(nc.vector.reciprocal(st[:, 8:11], st[:, 4:7]))
                        nc.vector.tensor_tensor(st[:, 12:15], st[:, 8:11], gate[:, i, HPG * g + hh, :], ALU.mult
                                                ).then_inc(s_f, 1)
                        dve.wait_ge(s_f, n + 1)
                        if hh == HPG - 1:
                            nc.vector.tensor_scalar(prob[:, slot, 0:cols_of(i)[0]], prob[:, slot, 0:cols_of(i)[0]],
                                                    st[:, 13:14], None, ALU.mult).then_inc(s_pv, 1)
                    elif kind == "block":
                        u, b = arg
                        n = base[u] + b
                        w = NCH if key_blocks(u)[b][1] == 2 else P
                        dve.wait_ge(s_th, n + 1)
                        nc.vector.tensor_tensor(pT_lo[0:w, n % (LAG + 1), :], bank[kind, arg][0:w].rearrange("p a b -> p (a b)"),
                                                pT_hi[0:w, n % (LAG + 1), :].bitcast(F32), ALU.subtract).then_inc(s_tl, 1)
                    elif kind == "drain":
                        u = arg[0]
                        i, g = units[u]
                        dve.wait_ge(s_oc, u + 1)
                        halves = psO[:, :, :].rearrange("p (m e) t -> p e m t", e=2)
                        dst = aT[:, 2 * g:2 * g + 2, i * P:(i + 1) * P]
                        nc.vector.tensor_tensor(dst[0:HD], halves[0:HD, 0], other[0:HD], ALU.add)
                        nc.vector.tensor_tensor(dst[HD:P], halves[HD:P, 1], other[HD:P], ALU.add).then_inc(s_od, 1)


def split_weight_loads(sp, raw, srcs, s_w, s_hi, s_lo):
    for c, src in enumerate(srcs):
        if c >= 2:
            sp.wait_ge(s_hi, c - 1)
            sp.wait_ge(s_lo, c - 1)
        sp.dma_start(raw[:, c % 2, 0:src.shape[-1]], src).then_inc(s_w[c % 2], 16)


def mix_out(nc, t, x_of, aT, mT, x, raw, s_w):
    with ExitStack() as ctx:
        ph = Phase(nc, ctx, "out")
        w_hi = ph.sb("w_hi", [P, KC, DM], F32R)
        w_lo = ph.sb("w_lo", [P, KC, DM], F32R)
        gT = ph.sb("gT", [P, KC])
        ones = ph.sb("ones", [P, 1])
        sq = ph.sb("sq", [P, 2, KC, P])
        mixg = ph.sb("mixg", [P, KC, P])
        m_hi = ph.sb("m_hi", [P, 2, KC, P], F32R)
        m_lo = ph.sb("m_lo", [P, 2, KC, P], F32R)
        stat = ph.sb("stat", [P, NT, 6])
        acc = [[ph.ps(f"acc{k}{h}", [P, 512]) for h in range(2)] for k in range(2)]
        psN = [ph.ps(f"psN{k}", [P, 2]) for k in range(2)]
        s_hi = ph.sem("weight_hi_made")
        s_lo = ph.sem("weight_lo_made")
        s_c = ph.sem("constants_loaded")
        s_one = ph.sem("ones_written")
        s_x = ph.sem("x_loaded")
        s_sq = ph.sem("squares_made")
        s_n = ph.sem("squares_summed")
        s_ms = ph.sem("mean_squares_made")
        s_sd = ph.sem("roots_taken")
        s_mg = ph.sem("gain_applied")
        s_mh = ph.sem("mix_hi_made")
        s_ml = ph.sem("mix_lo_made")
        s_mm = ph.sem("half_multiplied")
        s_y = ph.sem("half_added")
        s_dve = ph.sem("vector_chain")

        def cols(j):
            return slice(j * P, j * P + rows_of(j))

        with nc.Block() as block:

            @block.gpsimd
            def _(pool):
                nc.gpsimd.memset(ones[:, :], 1.0).then_inc(s_one, 1)
                for k, name in enumerate(("g_attn_out", "pool_scale")):
                    pool.dma_start(gT[:, 4 * k:4 * k + 4], t[name][0].rearrange("(c p) -> p c", p=P),
                                   allow_slow_non_contiguous=True).then_inc(s_c, 16)
                for j in range(NT):
                    pool.dma_start(x[0:rows_of(j), j, :], x_of(j)).then_inc(s_x, 16)

            @block.tensor
            def _(pe):
                pe.wait_ge(s_one, 1)

                def sums(j):
                    r = rows_of(j)
                    pe.wait_ge(s_sq, j + 1)
                    if j >= 2:
                        pe.wait_ge(s_ms, j - 1)
                    for k in range(2):
                        for c in range(4):
                            m = nc.tensor.matmul(psN[j % 2][0:r, k:k + 1], sq[:, j % 2, 4 * k + c, 0:r], ones[:, :],
                                                 start=(c == 0), stop=(c == 3))
                    m.then_inc(s_n, 1)

                sums(0)
                for j in range(NT):
                    r = rows_of(j)
                    pe.wait_ge(s_ml, j + 1)
                    if j:
                        order = [(h, c) for h in range(2) for c in range(KC)]
                    else:
                        order = [(h, c) for c in range(KC) for h in range(2)]
                    for h, c in order:
                        if j and c == 0:
                            pe.wait_ge(s_y, 2 * (j - 1) + h + 1)
                        if j == 0 and h == 0:
                            pe.wait_ge(s_lo, c + 1)
                        for n_pass, (a, b) in enumerate(((m_hi, w_hi), (m_hi, w_lo), (m_lo, w_hi))):
                            m = nc.tensor.matmul(acc[c // 4][h][0:r, :], a[:, j % 2, c, 0:r], b[:, c, 512 * h:512 * h + 512],
                                                 start=(c % 4 == 0 and n_pass == 0), stop=(c % 4 == 3 and n_pass == 2))
                        if c == KC - 1:
                            m.then_inc(s_mm, 1)
                    if j + 1 < NT:
                        sums(j + 1)

            @block.scalar
            def _(act):
                def squares(j):
                    r = rows_of(j)
                    if j >= 2:
                        act.wait_ge(s_n, j - 1)
                    nc.scalar.activation(sq[:, j % 2, 0:4, 0:r], aT[:, :, cols(j)], ACT.Square)
                    nc.scalar.activation(sq[:, j % 2, 4:8, 0:r], mT[:, :, cols(j)], ACT.Square).then_inc(s_sq, 1)

                def hi(j):
                    r = rows_of(j)
                    act.wait_ge(s_mg, j + 1)
                    if j >= 2:
                        act.wait_ge(s_mm, 2 * (j - 1))
                    nc.scalar.copy(m_hi[:, j % 2, :, 0:r], mixg[:, :, 0:r]).then_inc(s_mh, 1)

                squares(0)
                hi(0)
                for c in range(KC):
                    act.wait_ge(s_w[c], 16)
                    nc.scalar.copy(w_hi[:, c, :], raw[:, c, :]).then_inc(s_hi, 1)
                for j in range(NT):
                    r = rows_of(j)
                    if j + 1 < NT:
                        squares(j + 1)
                        hi(j + 1)
                    act.wait_ge(s_ms, j + 1)
                    nc.scalar.activation(stat[0:r, j, 2:4], stat[0:r, j, 0:2], ACT.Sqrt).then_inc(s_sd, 1)

            @block.vector
            def _(dve):
                chain = Chain(dve, s_dve)

                def gains(j):
                    r = rows_of(j)
                    if j:
                        dve.wait_ge(s_ml, j)
                    for k, src in enumerate((aT, mT)):
                        g = gT[:, 4 * k:4 * k + 4].unsqueeze(2).broadcast_to([P, 4, r])
                        m = nc.vector.tensor_tensor(mixg[:, 4 * k:4 * k + 4, 0:r], src[:, :, cols(j)], g, ALU.mult)
                    m.then_inc(s_mg, 1)

                def lo(j):
                    r = rows_of(j)
                    dve.wait_ge(s_mh, j + 1)
                    nc.vector.tensor_tensor(m_lo[:, j % 2, :, 0:r], mixg[:, :, 0:r], m_hi[:, j % 2, :, 0:r].bitcast(F32),
                                            ALU.subtract).then_inc(s_ml, 1)

                dve.wait_ge(s_c, 32)
                gains(0)
                lo(0)
                for c in range(KC):
                    dve.wait_ge(s_hi, c + 1)
                    nc.vector.tensor_tensor(w_lo[:, c, :], raw[:, c, :], w_hi[:, c, :].bitcast(F32),
                                            ALU.subtract).then_inc(s_lo, 1)
                dve.wait_ge(s_x, 16 * NT)
                for j in range(NT):
                    r = rows_of(j)
                    if j + 1 < NT:
                        gains(j + 1)
                        lo(j + 1)
                    dve.wait_ge(s_n, j + 1)
                    nc.vector.tensor_scalar(stat[0:r, j, 0:2], psN[j % 2][0:r, :], 1.0 / AW, EPS, ALU.mult,
                                            ALU.add).then_inc(s_ms, 1)
                    dve.wait_ge(s_sd, j + 1)
                    chain(nc.vector.reciprocal(stat[0:r, j, 4:6], stat[0:r, j, 2:4]))
                    for h in range(2):
                        xh = x[0:r, j, 512 * h:512 * h + 512]
                        dve.wait_ge(s_mm, 2 * j + h + 1)
                        chain(nc.vector.scalar_tensor_tensor(xh, acc[0][h][0:r, :], stat[0:r, j, 4:5], xh, ALU.mult,
                                                             ALU.add))
                        nc.vector.scalar_tensor_tensor(xh, acc[1][h][0:r, :], stat[0:r, j, 5:6], xh, ALU.mult,
                                                       ALU.add).then_inc(s_y, 1)


def cross_attention(nc, t, ident, o, x):
    scale = MD ** -0.5
    n_kb = NMEM // P
    i_s = NT - 1
    R = MH * DT
    MEM = 3
    with ExitStack() as ctx:
        ph = Phase(nc, ctx, "cross")
        raw = ph.sb("raw", [P, 2, DM])
        wq_hi = ph.sb("wq_hi", [P, KC, AW], F32R)
        wq_lo = ph.sb("wq_lo", [P, KC, AW], F32R)
        wo_hi = ph.sb("wo_hi", [P, MH, DM], F32R)
        wo_lo = ph.sb("wo_lo", [P, MH, DM], F32R)
        g_2 = ph.sb("g_2", [P, DM])
        xs = ph.sb("xs", [P, DM])
        xT_hi = ph.sb("xT_hi", [P, KC, P], F32R)
        xT_lo = ph.sb("xT_lo", [P, KC, P], F32R)
        stat = ph.sb("stat", [P, NT, 4])
        sm = ph.sb("sm", [P, 2, 4, MH])
        mem = ph.sb("mem", [P, MEM, n_kb, 2 * AW])
        kT_hi = ph.sb("kT_hi", [P, n_kb, MH, P], F32R)
        kT_lo = ph.sb("kT_lo", [P, n_kb, MH, P], F32R)
        v_hi = ph.sb("v_hi", [P, n_kb, AW], F32R)
        v_lo = ph.sb("v_lo", [P, n_kb, AW], F32R)
        qm = ph.sb("qm", [P, AW])
        qT_hi = ph.sb("qT_hi", [P, MH, P], F32R)
        qT_lo = ph.sb("qT_lo", [P, MH, P], F32R)
        prob = ph.sb("prob", [P, MH, NMEM])
        pT_hi = ph.sb("pT_hi", [P, n_kb, MH, P], F32R)
        pT_lo = ph.sb("pT_lo", [P, n_kb, MH, P], F32R)
        oT_hi = ph.sb("oT_hi", [P, MH, P], F32R)
        oT_lo = ph.sb("oT_lo", [P, MH, P], F32R)
        q_z = ph.sb("q_z", [P, DB, MH, R])
        kT_s = ph.sb("kT_s", [P, 2, n_kb, MH, P])
        pT_s = ph.sb("pT_s", [P, 2, n_kb, R])
        own = ph.sb("own", [R, AW])
        o_m = ph.sb("o_m", [R, 2, AW])
        pick = ph.sb("pick", [R, DB, DB * DT])
        psT = [ph.ps(f"psT{k}", [P, 4, P]) for k in range(2)]
        psQ = ph.ps("psQ", [P, 512])
        psS = ph.ps("psS", [P, MH, NMEM])
        psO = ph.ps("psO", [P, 4, P])
        psY = [ph.ps(f"psY{k}", [P, 512]) for k in range(2)]
        s_w = [ph.sem("weights_loaded_even"), ph.sem("weights_loaded_odd")]
        s_hi = ph.sem("weight_hi_made")
        s_lo = ph.sem("weight_lo_made")
        s_c = ph.sem("constants_loaded")
        s_g = ph.sem("gain_loaded")
        s_mem = [ph.sem(f"memory_slot{k}_loaded") for k in range(MEM)]
        s_mt = ph.sem("memory_transposed")
        s_mh = ph.sem("memory_hi_made")
        s_mlo = ph.sem("memory_lo_made")
        s_sum = ph.sem("squares_summed")
        s_ms = ph.sem("mean_square_made")
        s_sd = ph.sem("root_taken")
        s_xn = ph.sem("x_scaled")
        s_tr = ph.sem("x_transposed")
        s_th = ph.sem("xT_hi_made")
        s_tl = ph.sem("xT_lo_made")
        s_q = ph.sem("q_multiplied")
        s_qc = ph.sem("q_copied")
        s_qt = ph.sem("q_transposed")
        s_qh = ph.sem("q_hi_made")
        s_ql = ph.sem("q_lo_made")
        s_s = ph.sem("scores_made")
        s_m = ph.sem("maxima_made")
        s_e = ph.sem("exps_made")
        s_p = ph.sem("probs_scaled")
        s_pt = ph.sem("probs_transposed")
        s_ph = ph.sem("pT_hi_made")
        s_pl = ph.sem("pT_lo_made")
        s_o = ph.sem("outputs_made")
        s_oh = ph.sem("oT_hi_made")
        s_ol = ph.sem("oT_lo_made")
        s_y = ph.sem("products_made")
        s_x = ph.sem("x_updated")
        s_z = ph.sem("sample_q_zeroed")
        s_zq = ph.sem("sample_q_placed")
        s_kt = ph.sem("sample_keys_transposed")
        s_kc = ph.sem("sample_keys_copied")
        s_pc = ph.sem("sample_pT_copied")
        s_om = ph.sem("own_heads_kept")
        s_ob = ph.sem("sample_outputs_gathered")
        s_oc = ph.sem("sample_outputs_copied")
        s_ot = ph.sem("sample_outputs_transposed")
        s_dve = ph.sem("vector_chain")
        weights = ([(t["w_mq"][0][c * P:(c + 1) * P, :], wq_hi[:, c, :], wq_lo[:, c, :]) for c in range(KC)]
                   + [(t["w_mo"][0][c * P:(c + 1) * P, :], wo_hi[:, c, :], wo_lo[:, c, :]) for c in range(MH)])
        pm = o["p_mem_kv"][0, 0].rearrange("(k p) u h d -> p k (u h d)", p=P)
        cm = t["cache_mem_kv"][0].rearrange("b (k p) u h d -> b p k (u h d)", p=P)
        n_prompt = NT - 1
        with nc.Block() as block:

            @block.sync
            def _(sp):
                sp.dma_start(g_2[:, :], t["g_norm2"].broadcast_to([P, DM])).then_inc(s_g, 16)
                sp.dma_start(mem[:, 0], pm).then_inc(s_mem[0], 16)
                split_weight_loads(sp, raw, [w[0] for w in weights], s_w, s_hi, s_lo)
                for m in range(1, DB + 1):
                    if m == MEM:
                        sp.wait_ge(s_mh, 3)
                        sp.wait_ge(s_mlo, 3)
                    elif m > MEM:
                        sp.wait_ge(s_o, n_prompt + m - MEM)
                    sp.dma_start(mem[:, m % MEM], cm[m - 1]).then_inc(s_mem[m % MEM], 16)

            @block.gpsimd
            def _(pool):
                pool.dma_start(own[:, :], t["k_own"]).then_inc(s_c, 16)
                pool.dma_start(pick[:, :, :], t["k_pick"]).then_inc(s_c, 16)
                nc.gpsimd.memset(q_z[:, :, :, :], 0.0).then_inc(s_z, 1)

            @block.tensor
            def _(pe):
                def x_transposes(j):
                    r = rows_of(j)
                    pe.wait_ge(s_xn, j + 1)
                    for c in range(KC):
                        m = nc.tensor.transpose(psT[c // 4][:, c % 4, 0:r], xs[0:r, c * P:(c + 1) * P], ident[0:r, 0:r])
                        if c % 4 == 3:
                            m.then_inc(s_tr, 1)

                def q_products(j):
                    r = rows_of(j)
                    pe.wait_ge(s_tl, 2 * (j + 1))
                    if j:
                        pe.wait_ge(s_ql, j)
                    for c in range(KC):
                        if j == 0:
                            pe.wait_ge(s_lo, c + 1)
                        for n_pass, (a, b) in enumerate(((xT_hi, wq_hi), (xT_hi, wq_lo), (xT_lo, wq_hi))):
                            m = nc.tensor.matmul(psQ[0:r, :], a[:, c, 0:r], b[:, c, :], start=(c == 0 and n_pass == 0),
                                                 stop=(c == KC - 1 and n_pass == 2))
                    m.then_inc(s_q, 1)

                def q_transposes(j):
                    r = rows_of(j)
                    pe.wait_ge(s_qc, j + 1)
                    for h in range(MH):
                        m = nc.tensor.transpose(psQ[:, h * P:h * P + r], qm[0:r, h * MD:(h + 1) * MD], ident[0:r, 0:r])
                    m.then_inc(s_qt, 1)

                def scores(j):
                    pe.wait_ge(s_ql, j + 1)
                    if j:
                        pe.wait_ge(s_e, MH * j)
                    for h in range(MH):
                        for n_pass, (a, b) in enumerate(((qT_hi, kT_hi), (qT_hi, kT_lo), (qT_lo, kT_hi))):
                            m = nc.tensor.matmul(psS[:, h, :].rearrange("p (k t) -> p k t", k=n_kb), a[:, h, :],
                                                 b[:, :, h, :], start=(n_pass == 0), stop=(n_pass == 2))
                    m.then_inc(s_s, 1)

                def prob_transposes(j):
                    pe.wait_ge(s_p, j + 1)
                    pe.wait_ge(s_tl, 2 * (j + 2))
                    for kb in range(n_kb):
                        for h in range(MH):
                            m = nc.tensor.transpose(psT[kb][:, h, :], prob[:, h, kb * P:(kb + 1) * P], ident[:, :])
                        m.then_inc(s_pt, 1)

                def values(j):
                    pe.wait_ge(s_mlo, 3)
                    pe.wait_ge(s_pl, n_kb * (j + 1))
                    if j:
                        pe.wait_ge(s_ol, j)
                    for h in range(MH):
                        for kb in range(n_kb):
                            for n_pass, (a, b) in enumerate(((v_hi, pT_hi), (v_lo, pT_hi), (v_hi, pT_lo))):
                                m = nc.tensor.matmul(psO[:, h, :], a[:, kb, h * MD:(h + 1) * MD], b[:, kb, h, :],
                                                     start=(kb == 0 and n_pass == 0), stop=(kb == n_kb - 1 and n_pass == 2))
                    m.then_inc(s_o, 1)

                def back(j):
                    r = rows_of(j)
                    pe.wait_ge(s_ol, j + 1)
                    if j:
                        pe.wait_ge(s_x, 2 * j)
                    if j == 0:
                        pe.wait_ge(s_lo, len(weights))
                    for half in range(2):
                        for h in range(MH):
                            for n_pass, (a, b) in enumerate(((oT_hi, wo_hi), (oT_hi, wo_lo), (oT_lo, wo_hi))):
                                m = nc.tensor.matmul(psY[half][0:r, :], a[:, h, 0:r], b[:, h, 512 * half:512 * half + 512],
                                                     start=(h == 0 and n_pass == 0), stop=(h == MH - 1 and n_pass == 2))
                        m.then_inc(s_y, 1)

                pe.wait_ge(s_mem[0], 16)
                for kb in range(n_kb):
                    for h in range(MH):
                        m = nc.tensor.transpose(psT[kb][:, h, :], mem[:, 0, kb, h * MD:(h + 1) * MD], ident[:, :])
                    m.then_inc(s_mt, 1)
                pe.wait_ge(s_mlo, 2)
                x_transposes(0)
                q_products(0)
                q_transposes(0)
                x_transposes(1)
                for j in range(n_prompt):
                    scores(j)
                    if j:
                        back(j - 1)
                    prob_transposes(j)
                    q_products(j + 1)
                    values(j)
                    q_transposes(j + 1)
                    if j + 2 < NT:
                        x_transposes(j + 2)

                def sample_keys(b):
                    pe.wait_ge(s_mem[(b + 1) % MEM], 16 * ((b + 1) // MEM + 1))
                    for kb in range(n_kb):
                        if b:
                            pe.wait_ge(s_kc, n_kb * (b - 1) + kb + 1)
                        for h in range(MH):
                            m = nc.tensor.transpose(psT[kb][:, h, :], mem[:, (b + 1) % MEM, kb, h * MD:(h + 1) * MD],
                                                    ident[:, :])
                        m.then_inc(s_kt, 1)

                def sample_scores(b):
                    pe.wait_ge(s_kc, n_kb * (b + 1))
                    if b == 0:
                        pe.wait_ge(s_e, MH * n_prompt)
                    elif b >= 2:
                        pe.wait_ge(s_e, MH * n_prompt + b - 1)
                    for h in range(MH):
                        m = nc.tensor.matmul(psS[0:R, 2 * (b % 2), :].rearrange("p (k t) -> p k t", k=n_kb), q_z[:, b, h, :],
                                             kT_s[:, b % 2, :, h, :], start=(h == 0), stop=(h == MH - 1))
                    m.then_inc(s_s, 1)

                def sample_prob_transposes(b):
                    pe.wait_ge(s_p, n_prompt + b + 1)
                    if b:
                        pe.wait_ge(s_pc, b)
                    else:
                        pe.wait_ge(s_x, 2 * n_prompt)
                    for kb in range(n_kb):
                        m = nc.tensor.transpose(psY[0][:, kb * R:(kb + 1) * R], prob[0:R, b % 2, kb * P:(kb + 1) * P],
                                                ident[0:R, 0:R])
                    m.then_inc(s_pt, 1)

                def sample_values(b):
                    pe.wait_ge(s_pc, b + 1)
                    if b:
                        pe.wait_ge(s_om, b)
                    else:
                        pe.wait_ge(s_ol, n_prompt)
                    out = psO[0:R, :, :].rearrange("p a b -> p (a b)")
                    for kb in range(n_kb):
                        m = nc.tensor.matmul(out, pT_s[:, b % 2, kb, :], mem[:, (b + 1) % MEM, kb, AW:2 * AW],
                                             start=(kb == 0), stop=(kb == n_kb - 1))
                    m.then_inc(s_o, 1)

                def gather(b):
                    pe.wait_ge(s_om, b + 1)
                    m = nc.tensor.matmul(psQ[0:DB * DT, :], pick[:, b, :], o_m[:, b % 2, :], start=(b == 0),
                                         stop=(b == DB - 1), skip_group_check=True)
                    if b == DB - 1:
                        m.then_inc(s_ob, 1)

                sample_keys(0)
                back(n_prompt - 1)
                sample_keys(1)
                pe.wait_ge(s_zq, 1)
                pe.wait_ge(s_c, 32)
                sample_scores(0)
                for b in range(DB):
                    if b + 1 < DB:
                        sample_scores(b + 1)
                    sample_prob_transposes(b)
                    if b + 2 < DB:
                        sample_keys(b + 2)
                    sample_values(b)
                    if b:
                        gather(b - 1)
                gather(DB - 1)
                pe.wait_ge(s_oc, 1)
                r = DB * DT
                for h in range(MH):
                    m = nc.tensor.transpose(psO[:, h, 0:r], qm[0:r, h * MD:(h + 1) * MD], ident[0:r, 0:r])
                m.then_inc(s_ot, 1)
                back(i_s)

            @block.scalar
            def _(act):
                def norm(j):
                    r = rows_of(j)
                    if j:
                        act.wait_ge(s_tr, 2 * j)
                    nc.scalar.activation(xs[0:r, :], x[0:r, j, :], ACT.Square,
                                         accum_out=stat[0:r, j, 0:1]).then_inc(s_sum, 1)
                    act.wait_ge(s_ms, j + 1)
                    nc.scalar.activation(stat[0:r, j, 2:3], stat[0:r, j, 1:2], ACT.Sqrt).then_inc(s_sd, 1)

                def x_hi(j):
                    r = rows_of(j)
                    for h in range(2):
                        act.wait_ge(s_tr, 2 * j + h + 1)
                        if j:
                            act.wait_ge(s_q, j)
                        nc.scalar.copy(xT_hi[:, 4 * h:4 * h + 4, 0:r], psT[h][:, :, 0:r]).then_inc(s_th, 1)

                def q_copy(j):
                    r = rows_of(j)
                    act.wait_ge(s_q, j + 1)
                    if j:
                        act.wait_ge(s_qt, j)
                    nc.scalar.copy(qm[0:r, :], psQ[0:r, :]).then_inc(s_qc, 1)

                def q_hi(j):
                    act.wait_ge(s_qt, j + 1)
                    nc.scalar.copy(qT_hi[:, :, :], psQ[:, :].rearrange("p (h t) -> p h t", h=MH)).then_inc(s_qh, 1)

                norm(0)
                for kb in range(n_kb):
                    act.wait_ge(s_mt, kb + 1)
                    nc.scalar.copy(kT_hi[:, kb], psT[kb][:, :, :]).then_inc(s_mh, 1)
                nc.scalar.copy(v_hi[:, :, :], mem[:, 0, :, AW:2 * AW]).then_inc(s_mh, 1)
                x_hi(0)
                norm(1)

                def weight_hi(c):
                    src, whi, _ = weights[c]
                    act.wait_ge(s_w[c % 2], 16 * (c // 2 + 1))
                    nc.scalar.copy(whi, raw[:, c % 2, 0:src.shape[-1]]).then_inc(s_hi, 1)

                for c in range(KC):
                    weight_hi(c)
                q_copy(0)
                q_hi(0)
                x_hi(1)
                for j in range(n_prompt):
                    act.wait_ge(s_m, j + 1)
                    for h in range(MH):
                        nc.scalar.activation(prob[:, h, :], psS[:, h, :], ACT.Exp, bias=sm[:, j % 2, 1, h:h + 1],
                                             scale=scale, accum_out=sm[:, j % 2, 2, h:h + 1]).then_inc(s_e, 1)
                    if j + 2 < NT:
                        norm(j + 2)
                    if j == 0:
                        for c in range(KC, len(weights)):
                            weight_hi(c)
                    for kb in range(n_kb):
                        act.wait_ge(s_pt, n_kb * j + kb + 1)
                        nc.scalar.copy(pT_hi[:, kb], psT[kb][:, :, :]).then_inc(s_ph, 1)
                    q_copy(j + 1)
                    act.wait_ge(s_o, j + 1)
                    if j:
                        act.wait_ge(s_y, 2 * j)
                    nc.scalar.copy(oT_hi[:, :, :], psO[:, :, :]).then_inc(s_oh, 1)
                    if j + 1 < n_prompt:
                        q_hi(j + 1)
                    if j + 2 < NT:
                        x_hi(j + 2)

                def keys_copy(b):
                    for kb in range(n_kb):
                        act.wait_ge(s_kt, n_kb * b + kb + 1)
                        nc.scalar.copy(kT_s[:, b % 2, kb], psT[kb][:, :, :]).then_inc(s_kc, 1)

                def sample_exp(b):
                    act.wait_ge(s_m, n_prompt + b + 1)
                    nc.scalar.activation(prob[0:R, b % 2, :], psS[0:R, 2 * (b % 2), :], ACT.Exp, bias=sm[0:R, b % 2, 1, 0:1],
                                         scale=scale, accum_out=sm[0:R, b % 2, 2, 0:1]).then_inc(s_e, 1)

                keys_copy(0)
                keys_copy(1)
                sample_exp(0)
                for b in range(DB):
                    if b + 1 < DB:
                        sample_exp(b + 1)
                    act.wait_ge(s_pt, n_kb * n_prompt + b + 1)
                    nc.scalar.copy(pT_s[:, b % 2].rearrange("p k r -> p (k r)"), psY[0][:, 0:n_kb * R]).then_inc(s_pc, 1)
                    if b + 2 < DB:
                        keys_copy(b + 2)
                act.wait_ge(s_ob, 1)
                r = DB * DT
                nc.scalar.copy(qm[0:r, :], psQ[0:r, :]).then_inc(s_oc, 1)
                act.wait_ge(s_ot, 1)
                nc.scalar.copy(oT_hi[:, :, 0:r], psO[:, :, 0:r]).then_inc(s_oh, 1)

            @block.vector
            def _(dve):
                chain = Chain(dve, s_dve)

                def norm(j):
                    r = rows_of(j)
                    dve.wait_ge(s_sum, j + 1)
                    nc.vector.tensor_scalar(stat[0:r, j, 1:2], stat[0:r, j, 0:1], 1.0 / DM, EPS, ALU.mult,
                                            ALU.add).then_inc(s_ms, 1)
                    dve.wait_ge(s_sd, j + 1)
                    chain(nc.vector.reciprocal(stat[0:r, j, 3:4], stat[0:r, j, 2:3]))
                    nc.vector.scalar_tensor_tensor(xs[0:r, :], x[0:r, j, :], stat[0:r, j, 3:4], g_2[0:r, :], ALU.mult,
                                                   ALU.mult).then_inc(s_xn, 1)

                def x_lo(j):
                    r = rows_of(j)
                    for h in range(2):
                        dve.wait_ge(s_th, 2 * j + h + 1)
                        nc.vector.tensor_tensor(xT_lo[:, 4 * h:4 * h + 4, 0:r], psT[h][:, :, 0:r],
                                                xT_hi[:, 4 * h:4 * h + 4, 0:r].bitcast(F32), ALU.subtract).then_inc(s_tl, 1)

                def q_lo(j):
                    dve.wait_ge(s_qh, j + 1)
                    nc.vector.tensor_tensor(qT_lo[:, :, :], psQ[:, :].rearrange("p (h t) -> p h t", h=MH),
                                            qT_hi[:, :, :].bitcast(F32), ALU.subtract).then_inc(s_ql, 1)

                def add_y(j):
                    r = rows_of(j)
                    for half in range(2):
                        dve.wait_ge(s_y, 2 * j + half + 1)
                        xh = x[0:r, j, 512 * half:512 * half + 512]
                        nc.vector.tensor_tensor(xh, psY[half][0:r, :], xh, ALU.add).then_inc(s_x, 1)

                dve.wait_ge(s_g, 16)
                norm(0)
                for kb in range(n_kb):
                    dve.wait_ge(s_mh, kb + 1)
                    nc.vector.tensor_tensor(kT_lo[:, kb], psT[kb][:, :, :], kT_hi[:, kb].bitcast(F32),
                                            ALU.subtract).then_inc(s_mlo, 1)
                dve.wait_ge(s_mh, 3)
                nc.vector.tensor_tensor(v_lo[:, :, :], mem[:, 0, :, AW:2 * AW], v_hi[:, :, :].bitcast(F32),
                                        ALU.subtract).then_inc(s_mlo, 1)
                x_lo(0)
                norm(1)

                def weight_lo(c):
                    src, whi, wlo = weights[c]
                    dve.wait_ge(s_hi, c + 1)
                    nc.vector.tensor_tensor(wlo, raw[:, c % 2, 0:src.shape[-1]], whi.bitcast(F32),
                                            ALU.subtract).then_inc(s_lo, 1)

                for c in range(KC):
                    weight_lo(c)
                q_lo(0)
                x_lo(1)
                for j in range(n_prompt):
                    dve.wait_ge(s_s, j + 1)
                    chain(nc.vector.tensor_reduce(sm[:, j % 2, 0, :], psS[:, :, :], AX.X, ALU.max, negate=True))
                    nc.vector.tensor_scalar(sm[:, j % 2, 1, :], sm[:, j % 2, 0, :], scale, None, ALU.mult).then_inc(s_m, 1)
                    dve.wait_ge(s_e, MH * (j + 1))
                    chain(nc.vector.reciprocal(sm[:, j % 2, 3, :], sm[:, j % 2, 2, :]))
                    f = sm[:, j % 2, 3, :].unsqueeze(2).broadcast_to([P, MH, NMEM])
                    nc.vector.tensor_tensor(prob[:, :, :], prob[:, :, :], f, ALU.mult).then_inc(s_p, 1)
                    if j + 2 < NT:
                        norm(j + 2)
                    if j == 0:
                        for c in range(KC, len(weights)):
                            weight_lo(c)
                    for kb in range(n_kb):
                        dve.wait_ge(s_ph, n_kb * j + kb + 1)
                        nc.vector.tensor_tensor(pT_lo[:, kb], psT[kb][:, :, :], pT_hi[:, kb].bitcast(F32),
                                                ALU.subtract).then_inc(s_pl, 1)
                    if j:
                        add_y(j - 1)
                    dve.wait_ge(s_oh, j + 1)
                    nc.vector.tensor_tensor(oT_lo[:, :, :], psO[:, :, :], oT_hi[:, :, :].bitcast(F32),
                                            ALU.subtract).then_inc(s_ol, 1)
                    if j + 1 < n_prompt:
                        q_lo(j + 1)
                    if j + 2 < NT:
                        x_lo(j + 2)
                dve.wait_ge(s_z, 1)
                dve.wait_ge(s_c, 32)
                dve.wait_ge(s_qt, n_prompt + 1)
                for h in range(MH):
                    m = nc.vector.tensor_copy(q_z[:, :, h, h * DT:(h + 1) * DT],
                                              psQ[:, h * P:h * P + DB * DT].rearrange("p (b s) -> p b s", b=DB))
                m.then_inc(s_zq, 1)
                add_y(n_prompt - 1)

                def sample_max(b):
                    st = sm[0:R, b % 2]
                    dve.wait_ge(s_s, n_prompt + b + 1)
                    chain(nc.vector.reduce_max(st[:, 0, 0:1], psS[0:R, 2 * (b % 2), :], AX.X, negate=True))
                    nc.vector.tensor_scalar(st[:, 1, 0:1], st[:, 0, 0:1], scale, None, ALU.mult).then_inc(s_m, 1)

                def sample_scale(b):
                    st = sm[0:R, b % 2]
                    dve.wait_ge(s_e, MH * n_prompt + b + 1)
                    chain(nc.vector.reciprocal(st[:, 3, 0:1], st[:, 2, 0:1]))
                    nc.vector.tensor_scalar(prob[0:R, b % 2, :], prob[0:R, b % 2, :], st[:, 3, 0:1], None,
                                            ALU.mult).then_inc(s_p, 1)

                def own_heads(b):
                    dve.wait_ge(s_o, n_prompt + b + 1)
                    nc.vector.tensor_tensor(o_m[:, b % 2, :], psO[0:R, :, :].rearrange("p a b -> p (a b)"), own[:, :],
                                            ALU.mult).then_inc(s_om, 1)

                sample_max(0)
                for b in range(DB):
                    sample_scale(b)
                    if b + 1 < DB:
                        sample_max(b + 1)
                    if b:
                        own_heads(b - 1)
                own_heads(DB - 1)
                r = DB * DT
                dve.wait_ge(s_oh, n_prompt + 1)
                nc.vector.tensor_tensor(oT_lo[:, :, 0:r], psO[:, :, 0:r], oT_hi[:, :, 0:r].bitcast(F32),
                                        ALU.subtract).then_inc(s_ol, 1)
                add_y(i_s)


def mlp(nc, t, ident, x, y_of, s_st):
    groups = [(0, 1, 2), (3, 4, 5), (6, 7, 8)]
    n_f = DFF // P
    PF = 2
    with ExitStack() as ctx:
        ph = Phase(nc, ctx, "mlp")
        g_3 = ph.sb("g_3", [P, DM])
        g_last = ph.sb("g_last", [P, DM])
        xs = ph.sb("xs", [P, 2, DM])
        junk = ph.sb("junk", [P, DM])
        xT_hi = ph.sb("xT_hi", [P, 2, KC, 3 * P], F32R)
        xT_lo = ph.sb("xT_lo", [P, 2, KC, 3 * P], F32R)
        stat = ph.sb("stat", [P, 2, NT, 4])
        up_raw = ph.sb("up_raw", [P, 2, KC, PF * P])
        dn_raw = ph.sb("dn_raw", [P, 2, PF, DM])
        up_hi = ph.sb("up_hi", [P, 2, KC, P], F32R)
        up_lo = ph.sb("up_lo", [P, 2, KC, P], F32R)
        dn_hi = ph.sb("dn_hi", [P, 2, DM], F32R)
        dn_lo = ph.sb("dn_lo", [P, 2, DM], F32R)
        h_r = ph.sb("h_r", [P, 3 * P])
        h_2 = ph.sb("h_2", [P, 3 * P])
        h_hi = ph.sb("h_hi", [P, 2, 3 * P], F32R)
        h_lo = ph.sb("h_lo", [P, 2, 3 * P], F32R)
        acc = [[ph.ps(f"acc{k}{h}", [P, 512]) for h in range(2)] for k in range(3)]
        psU = [ph.ps(f"psU{k}", [P, 512]) for k in range(2)]
        s_g = ph.sem("gain_loaded")
        s_gl = ph.sem("final_gain_loaded")
        s_r = [ph.sem("raw_loaded_even"), ph.sem("raw_loaded_odd")]
        s_uh = ph.sem("up_hi_made")
        s_ul = ph.sem("up_lo_made")
        s_dh = ph.sem("down_hi_made")
        s_dl = ph.sem("down_lo_made")
        s_sum = ph.sem("squares_summed")
        s_ms = ph.sem("mean_square_made")
        s_sd = ph.sem("root_taken")
        s_xn = ph.sem("x_scaled")
        s_tr = ph.sem("half_tile_transposed")
        s_th = ph.sem("xT_hi_made")
        s_tl = ph.sem("xT_lo_made")
        s_up = ph.sem("hidden_multiplied")
        s_re = ph.sem("relu_made")
        s_h2 = ph.sem("relu_squared")
        s_hh = ph.sem("hidden_hi_made")
        s_hl = ph.sem("hidden_lo_made")
        s_dn = ph.sem("hidden_block_used")
        s_acc = ph.sem("half_added")
        s_y = ph.sem("y_ready")
        s_dve = ph.sem("vector_chain")

        def width(g):
            return sum(rows_of(i) for i in groups[g])

        def tile_steps(g):
            yield "norm", groups[g][0]
            for i in groups[g]:
                if i + 1 in groups[g]:
                    yield "norm", i + 1
                for h in range(2):
                    yield "x", (g, i, h)

        def steps():
            n = 0
            for kind, arg in tile_steps(0):
                yield kind, arg, n
                n += kind == "x"
            for g in range(len(groups)):
                todo = [("final", i) for i in groups[g - 1]] if g else []
                todo += list(tile_steps(g + 1)) if g + 1 < len(groups) else []
                last = g == len(groups) - 1
                f0, f1 = (4, n_f - 4) if last else (16, n_f)
                f = 0
                while f < n_f:
                    if f == f0:
                        yield "loop", (g, g * n_f + f0, g * n_f + f1), n
                        f, n = f1, n + f1 - f0
                        continue
                    yield "f", (g, g * n_f + f - f % 4, f % 4), n
                    f, n = f + 1, n + 1
                    if f >= 2 and todo:
                        kind, arg = todo.pop(0)
                        yield kind, arg, n
                        n += kind == "x"
                yield "end", (g, 0), n
            for i in groups[-1]:
                yield "final", i, n

        plan = list(steps())
        drained = {}
        n_x = n_up = 0
        for kind, arg, n in plan:
            if kind == "x":
                n_x += 1
                drained[n] = (s_tl, n_x)
            elif kind == "f":
                n_up += 1
                drained[n] = (s_re, n_up)
            elif kind == "loop":
                for m in range(arg[1], arg[2]):
                    n_up += 1
                    drained[n + m - arg[1]] = (s_re, n_up)

        def reached(i, u, m):
            return not isinstance(i, int) or i + u >= m

        def is_last(i, u):
            return isinstance(i, int) and i + u == n_f * len(groups) - 1

        with nc.Block() as block:

            @block.sync
            def _(sp):
                sp.dma_start(g_3[:, :], t["g_norm3"].broadcast_to([P, DM])).then_inc(s_g, 16)
                def load(g, f, k):
                    if g or not isinstance(f, int):
                        for s in (s_uh, s_ul, s_dh, s_dl):
                            sp.wait_ge(s, f + (g * n_f + PF * (k - 1)))
                    at = bass.DynSlice(f * P + PF * P * k, PF * P)
                    sp.dma_start(up_raw[:, k], t["w_up"][0].rearrange("(c p) n -> p c n", p=P)[:, :, at]
                                 ).then_inc(s_r[k], 16)
                    sp.dma_start(dn_raw[:, k], t["w_down"][0][at, :].rearrange("(a p) n -> p a n", p=P)
                                 ).then_inc(s_r[k], 16)

                for g in range(len(groups)):
                    for k in range(2):
                        load(g, 0, k)
                    with sp.Fori(4, n_f - 3, 4) as f:
                        for k in range(2):
                            load(g, f, k)

            @block.gpsimd
            def _(pool):
                pool.wait_ge(s_up, 1)
                pool.dma_start(g_last[:, :], t["g_final"].rearrange("(a n) -> a n", a=1).broadcast_to([P, DM])
                               ).then_inc(s_gl, 16)
                for i in range(NT):
                    pool.wait_ge(s_y, i + 1)
                    pool.dma_start(y_of(i), x[0:rows_of(i), i, :]).then_inc(s_st, 16)
                pool.wait_ge(s_st, 16 * NT)

            @block.tensor
            def _(pe):
                def up(g, i, u, n):
                    w = width(g)
                    pe.wait_ge(s_ul, i + (u + 1))
                    for c in range(KC):
                        for n_pass, (a, b) in enumerate(((up_hi, xT_hi), (up_hi, xT_lo), (up_lo, xT_hi))):
                            m = nc.tensor.matmul(psU[n % 2][:, 0:w], a[:, u % 2, c, :], b[:, g % 2, c, 0:w],
                                                 start=(c == 0 and n_pass == 0), stop=(c == KC - 1 and n_pass == 2))
                    m.then_inc(s_up, 1)

                def down(g, i, u, first=False, end=False):
                    pe.wait_ge(s_hl, i + (u + 1))
                    pe.wait_ge(s_dl, i + (u + 1))
                    at = 0
                    for k, tile in enumerate(groups[g]):
                        r = rows_of(tile)
                        for half in range(2):
                            if first and g:
                                pe.wait_ge(s_acc, 6 * (g - 1) + 2 * k + half + 1)
                            for n_pass, (a, b) in enumerate(((h_hi, dn_hi), (h_hi, dn_lo), (h_lo, dn_hi))):
                                last = nc.tensor.matmul(acc[k][half][0:r, :], a[:, u % 2, at:at + r],
                                                        b[:, u % 2, 512 * half:512 * half + 512],
                                                        start=(first and n_pass == 0), stop=(end and n_pass == 2))
                        at += r
                    last.then_inc(s_dn, 1)

                n_t = 0
                for kind, arg, n in plan:
                    if kind in ("x", "f") and n >= 2:
                        pe.wait_ge(*drained[n - 2])
                    if kind == "x":
                        g, i, h = arg
                        r = rows_of(i)
                        pe.wait_ge(s_xn, i + 1)
                        for c in range(4):
                            m = nc.tensor.transpose(psU[n % 2][:, c * P:c * P + r],
                                                    xs[0:r, i % 2, (4 * h + c) * P:(4 * h + c + 1) * P], ident[0:r, 0:r])
                        m.then_inc(s_tr, 1)
                        n_t += 1
                    elif kind == "f":
                        g, i, u = arg
                        if i + u == g * n_f:
                            pe.wait_ge(s_tl, 6 * (g + 1))
                        up(g, i, u, n)
                        if i + u > g * n_f:
                            down(g, i, u - 1, first=i + u == g * n_f + 1)
                    elif kind == "loop":
                        g, m0, m1 = arg
                        with pe.Fori(m0, m1, 4) as i:
                            for u in range(4):
                                pe.wait_ge(s_re, i + (u - 1))
                                up(g, i, u, n + u)
                                down(g, i, u - 1)
                    elif kind == "end":
                        down(arg[0], n_f * arg[0], n_f - 1, end=True)

            @block.scalar
            def _(act):
                n_s = n_t = 0

                def norm(which, i):
                    r = rows_of(i)
                    if n_s:
                        act.wait_ge(s_sum, n_s)
                    nc.scalar.activation(junk[0:r, :], x[0:r, i, :], ACT.Square,
                                         accum_out=stat[0:r, which, i, 0:1]).then_inc(s_sum, 1)
                    act.wait_ge(s_ms, n_s + 1)
                    nc.scalar.activation(stat[0:r, which, i, 2:3], stat[0:r, which, i, 1:2], ACT.Sqrt).then_inc(s_sd, 1)

                def up_part(i, u):
                    k, a = u % 4 // PF, u % PF
                    act.wait_ge(s_r[k], i * 8 + 32 * (u // 4 + 1))
                    if reached(i, u, 2):
                        act.wait_ge(s_up, i + (u - 1))
                    nc.scalar.copy(up_hi[:, u % 2], up_raw[:, k, :, a * P:(a + 1) * P]).then_inc(s_uh, 1)

                def down_part(i, u):
                    k, a = u % 4 // PF, u % PF
                    if reached(i, u, 2):
                        act.wait_ge(s_dn, i + (u - 1))
                    nc.scalar.copy(dn_hi[:, u % 2], dn_raw[:, k, a, :]).then_inc(s_dh, 1)

                def hidden(g, i, u, n):
                    w = width(g)
                    if not reached(i, u, 1):
                        up_part(0, 0)
                        down_part(0, 0)
                    if not is_last(i, u):
                        up_part(i, u + 1)
                    act.wait_ge(s_up, i + (u + 1))
                    if reached(i, u, 1):
                        act.wait_ge(s_h2, i + u)
                        act.wait_ge(s_hh, i + u)
                    nc.scalar.activation(h_r[:, 0:w], psU[n % 2][:, 0:w], ACT.Relu).then_inc(s_re, 1)
                    act.wait_ge(s_re, i + (u + 1))
                    if reached(i, u, 2):
                        act.wait_ge(s_dn, i + (u - 1))
                    nc.scalar.activation(h_hi[:, u % 2, 0:w], h_r[:, 0:w], ACT.Square).then_inc(s_hh, 1)
                    if not is_last(i, u):
                        down_part(i, u + 1)

                for kind, arg, n in plan:
                    if kind == "norm":
                        norm(0, arg)
                        n_s += 1
                    elif kind == "x":
                        g, i, h = arg
                        act.wait_ge(s_tr, n_t + 1)
                        k = i - groups[g][0]
                        r = rows_of(i)
                        if g >= 2:
                            act.wait_ge(s_up, n_f * (g - 1))
                        src = psU[n % 2][:, :].rearrange("p (c t) -> p c t", c=4)[:, :, 0:r]
                        nc.scalar.copy(xT_hi[:, g % 2, 4 * h:4 * h + 4, k * P:k * P + r], src).then_inc(s_th, 1)
                        n_t += 1
                    elif kind == "f":
                        hidden(*arg, n)
                    elif kind == "loop":
                        g, m0, m1 = arg
                        with act.Fori(m0, m1, 4) as i:
                            for u in range(4):
                                hidden(g, i, u, n + u)
                    elif kind == "final":
                        act.wait_ge(s_acc, 2 * (arg + 1))
                        norm(1, arg)
                        n_s += 1

            @block.vector
            def _(dve):
                chain = Chain(dve, s_dve)
                n_s = n_t = 0

                def rms(which, i):
                    r = rows_of(i)
                    st = stat[0:r, which, i]
                    dve.wait_ge(s_sum, n_s + 1)
                    nc.vector.tensor_scalar(st[:, 1:2], st[:, 0:1], 1.0 / DM, EPS, ALU.mult, ALU.add).then_inc(s_ms, 1)
                    dve.wait_ge(s_sd, n_s + 1)
                    chain(nc.vector.reciprocal(st[:, 3:4], st[:, 2:3]))
                    return st[:, 3:4]

                def up_part(i, u):
                    k, a = u % 4 // PF, u % PF
                    dve.wait_ge(s_uh, i + (u + 1))
                    nc.vector.tensor_tensor(up_lo[:, u % 2], up_raw[:, k, :, a * P:(a + 1) * P],
                                            up_hi[:, u % 2].bitcast(F32), ALU.subtract).then_inc(s_ul, 1)

                def down_part(i, u):
                    k, a = u % 4 // PF, u % PF
                    dve.wait_ge(s_dh, i + (u + 1))
                    nc.vector.tensor_tensor(dn_lo[:, u % 2], dn_raw[:, k, a, :], dn_hi[:, u % 2].bitcast(F32),
                                            ALU.subtract).then_inc(s_dl, 1)

                def hidden(g, i, u):
                    w = width(g)
                    if not reached(i, u, 1):
                        up_part(0, 0)
                        down_part(0, 0)
                    if not is_last(i, u):
                        up_part(i, u + 1)
                    dve.wait_ge(s_re, i + (u + 1))
                    if reached(i, u, 1):
                        dve.wait_ge(s_hl, i + u)
                    nc.vector.tensor_tensor(h_2[:, 0:w], h_r[:, 0:w], h_r[:, 0:w], ALU.mult).then_inc(s_h2, 1)
                    dve.wait_ge(s_h2, i + (u + 1))
                    dve.wait_ge(s_hh, i + (u + 1))
                    nc.vector.tensor_tensor(h_lo[:, u % 2, 0:w], h_2[:, 0:w], h_hi[:, u % 2, 0:w].bitcast(F32),
                                            ALU.subtract).then_inc(s_hl, 1)
                    if not is_last(i, u):
                        down_part(i, u + 1)

                dve.wait_ge(s_g, 16)
                for kind, arg, n in plan:
                    if kind == "norm":
                        i = arg
                        r = rows_of(i)
                        f = rms(0, i)
                        n_s += 1
                        if i >= 2:
                            dve.wait_ge(s_tr, 2 * (i - 1))
                        nc.vector.scalar_tensor_tensor(xs[0:r, i % 2, :], x[0:r, i, :], f, g_3[0:r, :], ALU.mult,
                                                       ALU.mult).then_inc(s_xn, 1)
                    elif kind == "x":
                        g, i, h = arg
                        r = rows_of(i)
                        dve.wait_ge(s_th, n_t + 1)
                        src = psU[n % 2][:, :].rearrange("p (c t) -> p c t", c=4)[:, :, 0:r]
                        k = i - groups[g][0]
                        sl = (slice(None), g % 2, slice(4 * h, 4 * h + 4), slice(k * P, k * P + r))
                        nc.vector.tensor_tensor(xT_lo[sl], src, xT_hi[sl].bitcast(F32), ALU.subtract).then_inc(s_tl, 1)
                        n_t += 1
                    elif kind == "f":
                        hidden(*arg)
                    elif kind == "loop":
                        g, m0, m1 = arg
                        with dve.Fori(m0, m1, 4) as i:
                            for u in range(4):
                                hidden(g, i, u)
                    elif kind == "end":
                        g = arg[0]
                        for k, i in enumerate(groups[g]):
                            r = rows_of(i)
                            for half in range(2):
                                if k == 0 and half == 0:
                                    dve.wait_ge(s_dn, n_f * (g + 1))
                                xh = x[0:r, i, 512 * half:512 * half + 512]
                                nc.vector.tensor_tensor(xh, acc[k][half][0:r, :], xh, ALU.add).then_inc(s_acc, 1)
                    else:
                        i = arg
                        r = rows_of(i)
                        dve.wait_ge(s_gl, 16)
                        f = rms(1, i)
                        n_s += 1
                        nc.vector.scalar_tensor_tensor(x[0:r, i, :], x[0:r, i, :], f, g_last[0:r, :], ALU.mult,
                                                       ALU.mult).then_inc(s_y, 1)


IN_NAMES = ["x_prompt", "x_sample", "cache_cmp_kv", "cache_sel_kv", "cache_win_kv", "state_pool", "cache_mem_kv",
            "page_table", "mem_prompt", "w_in", "pe_cmp", "w_cmp1", "w_cmp2", "w_pool", "g_attn_out", "pool_scale",
            "w_out", "g_norm1", "g_norm2", "g_mem", "w_mq", "w_mkv", "w_mo", "g_norm3", "w_up", "w_down", "g_final"]
OUTS = [("y_prompt", (1, SEQ, DM)), ("y_sample", (DB, DT, DM)),
        ("p_cmp_kv", (1, 1, SEQ, 2, NG, HD)), ("p_sel_kv", (1, 1, SEQ, 2, NG, HD)),
        ("p_win_kv", (1, 1, WIN, 2, NG, HD)), ("p_pool", (1, 1, HIST, PW)), ("p_mem_kv", (1, 1, NMEM, 2, MH, MD)),
        ("s_cmp_kv", (1, DB, DT, 2, NG, HD)), ("s_sel_kv", (1, DB, DT, 2, NG, HD)),
        ("s_win_kv", (1, DB, WIN, 2, NG, HD)), ("s_pool", (1, DB, HIST, PW))]


def constants():
    pos = np.concatenate([np.arange(SEQ), np.tile(PAST + np.arange(DT), DB), np.zeros(P - DB * DT)]).astype(np.float32)
    inv = np.float32(500000.0) ** (-np.arange(HALF, dtype=np.float32) / np.float32(HALF))
    ang = (pos[:, None] * inv[None, :].astype(np.float32)).astype(np.float32)
    cs = np.concatenate([np.cos(ang), np.sin(ang)], axis=1).astype(np.float32)
    first = np.zeros((P, 4, HIST), np.float32)
    for g in range(4):
        wide = 2 << g
        first[:, g, :] = wide / np.minimum(np.arange(HIST) + 1, wide)
    g, h, s = (x.ravel() for x in np.meshgrid(np.arange(NG), np.arange(HPG), np.arange(DT), indexing="ij"))
    smask = np.zeros((NH * DT, S_COLS), np.float32)
    smask[:, PAST:N_SEL] = np.where(np.arange(DT)[None] <= s[:, None], 0, NEG)
    w = np.arange(N_WIN)[None]
    smask[:, S_WIN0:S_CMP0] = np.where((w >= s[:, None]) & (w <= WIN + s[:, None]), 0, NEG)
    smask[:, S_COLS - 1] = NEG
    same = ((g[:, None] == g[None]) & (s[:, None] == s[None])).astype(np.float32)
    block_no = np.tile(np.arange(1, 1 + N_MID, dtype=np.float32), (NH * DT, 1))
    q, k = np.arange(P)[:, None], np.arange(P)[None]
    ends = np.arange(NCH)[None] * STRIDE + CLEN - 1
    pmask = [np.where(k <= q, 0, NEG), np.where(k >= q, 0, NEG)]
    pmask += [np.where((ends <= q + i * P) & (ends < SEQ), 0, NEG) for i in range(NT - 1)]
    own = (np.arange(AW)[None] // MD == np.arange(MH * DT)[:, None] // DT).astype(np.float32)
    pick = np.zeros((MH * DT, DB, DB * DT), np.float32)
    for b in range(DB):
        pick[np.arange(MH * DT), b, b * DT + np.arange(MH * DT) % DT] = 1
    return {"k_own": own, "k_pick": pick, "k_pmask": np.concatenate(pmask, axis=1).astype(np.float32),
            "k_smask": smask, "k_same": same, "k_block_no": block_no, "k_edge": first,
            "k_ident": np.eye(P, dtype=np.float32),
            "k_rope": np.ascontiguousarray(cs.reshape(NT, P, ROT).transpose(1, 0, 2))}


def build(nc, t, o):
    with ExitStack() as ctx:
        top = Phase(nc, ctx, "top")
        stored = [nc.alloc_semaphore(f"{tag}_outputs_stored") for tag in ("memory", "poolin", "qkv", "mlp")]
        x_p = t["x_prompt"].rearrange("a (i p) d -> (a i) p d", p=P)
        x_s = t["x_sample"].rearrange("b t d -> (b t) d")
        ident = top.sb("ident", [P, P])
        table = top.sb("table", [1, DB * DB], I32)
        all_tiles = [0, NT - 1] + list(range(1, NT - 1))

        def x_of(i):
            return x_p[i] if i < NT - 1 else x_s

        with ExitStack() as c2:
            ph = Phase(nc, c2, "memory")
            y = ph.sb("y", [P, NMEM // P, 2 * AW])
            mem = t["mem_prompt"].rearrange("a (i p) d -> (a i) p d", p=P)
            out = o["p_mem_kv"].rearrange("l a (i p) u h d -> (l a i) p (u h d)", p=P)

            def store_mem(eng, sem, i):
                eng.dma_start(out[i], y[:, i, :]).then_inc(sem, 16)
                return 1

            project(nc, "mem", [0, 1], lambda i: mem[i], t["g_mem"][0], t["w_mkv"][0], 2 * AW, y, store_mem, stored[0], t, ident,
                    table=table)
        mix_scope = top.ctx.enter_context(ExitStack())
        mixed = Phase(nc, mix_scope, "mixed")
        aT = mixed.sb("aT", [P, 4, TOK], side="right")
        yq_scope = top.ctx.enter_context(ExitStack())
        ys = Phase(nc, yq_scope, "proj")
        yq = ys.sb("yq", [P, NT, C_PI])
        q_rot = ys.sb("q_rot", [P, NT, NH, ROT])
        with ExitStack() as c2:
            def store_kv(eng, sem, i):
                n = 0
                if i == 0:
                    old = t["cache_win_kv"][0].rearrange("b n u g d -> b n (u g d)")
                    new = o["s_win_kv"][0].rearrange("b n u g d -> b n (u g d)")
                    eng.dma_start(new[:, 0:WIN - DT, :], old[:, DT:WIN, :]).then_inc(sem, 16)
                    n += 1
                for name, c in (("cmp", C_KC), ("sel", C_KS), ("win", C_KW)):
                    if i < NT - 1:
                        dst = o[f"p_{name}_kv"][0, 0].rearrange("n u g d -> n (u g d)")
                        at = i * P - (SEQ - dst.shape[0])
                        if at < 0:
                            continue
                        eng.dma_start(dst[at:at + P, :], yq[:, i, c:c + KVW]).then_inc(sem, 16)
                        n += 1
                    elif name != "win":
                        dst = o[f"s_{name}_kv"][0].rearrange("b n u g d -> (b n) (u g d)")
                        eng.dma_start(dst, yq[0:DB * DT, i, c:c + KVW]).then_inc(sem, 16)
                        n += 1
                    else:
                        dst = o["s_win_kv"][0].rearrange("b n u g d -> b n (u g d)")
                        for b in range(DB):
                            eng.dma_start(dst[b, WIN - DT:WIN, :], yq[b * DT:b * DT + DT, i, c:c + KVW]).then_inc(sem, 16)
                        n += DB
                return n

            cs = Phase(nc, c2, "rope").sb("cs", [P, NT, ROT])
            n_kv_stores = project(nc, "qkv", all_tiles, x_of, t["g_norm1"][0], t["w_in"][0][:, 0:C_PI], C_PI, yq, store_kv,
                    stored[2], t, ident, rope=(q_rot, cs),
                                  wait_stores=False)


        with ExitStack() as c3:
            ph = Phase(nc, c3, "ckv")
            ck_hi = ph.sb("ck_hi", [P, NG, NCH], F32R)
            ck_lo = ph.sb("ck_lo", [P, NG, NCH], F32R)
            cv_p = ph.sb("cv_p", [HD, NG, P], F32R)
            with ExitStack() as c4:
                ph = Phase(nc, c4, "ckv_s")
                ck_s = ph.sb("ck_s", [P, DB, NCH])
                cv_s = ph.sb("cv_s", [HD, DB, P])
                compress(nc, t, ident, table, o, ck_s, cv_s, ck_hi, ck_lo, cv_p, stored[2], n_kv_stores)
                sample_attention(nc, t, ident, table, o, yq, q_rot, ck_s, cv_s, aT)
            prompt_attention(nc, t, ident, yq, q_rot, ck_hi, ck_lo, cv_p, aT)
        yq_scope.close()
        mT = mixed.sb("mT", [P, 4, TOK], side="right")
        w_out_raw = mixed.sb("w_out_raw", [P, KC, DM], side="right")
        s_w_out = [mixed.sem(f"w_out_slice{c}_loaded") for c in range(KC)]
        with ExitStack() as c2:
            ph = Phase(nc, c2, "poolin")
            yp = ph.sb("yp", [P, NT, PW])
            sp_out = o["s_pool"][0]

            def store_pool(eng, sem, i):
                if i == NT - 2:
                    eng.dma_start(o["p_pool"][0, 0], yp[P - HIST:P, i, :]).then_inc(sem, 16)
                    return 1
                if i == 0:
                    eng.dma_start(sp_out[:, 0:HIST - DT, :], t["state_pool"][0, :, DT:HIST, :]).then_inc(sem, 16)
                    return 1
                if i == NT - 1:
                    for b in range(DB):
                        eng.dma_start(sp_out[b, HIST - DT:HIST, :], yp[b * DT:b * DT + DT, i, :]).then_inc(sem, 16)
                    return DB
                return 0

            project(nc, "pin", all_tiles, x_of, t["g_norm1"][0], t["w_in"][0][:, C_PI:C_END], PW, yp, store_pool, stored[1],
                    t, ident)
            pool_mix(nc, t, ident, yp, mT, w_out_raw, s_w_out)
        x = top.sb("x", [P, NT, DM])
        mix_out(nc, t, x_of, aT, mT, x, w_out_raw, s_w_out)
        mix_scope.close()
        cross_attention(nc, t, ident, o, x)
        y_p = o["y_prompt"].rearrange("a (i p) d -> (a i) p d", p=P)
        y_s = o["y_sample"].rearrange("b t d -> (b t) d")
        mlp(nc, t, ident, x, lambda i: y_p[i] if i < NT - 1 else y_s, stored[3])


def kernel(**inputs):
    import concourse.bacc as _bacc
    from concourse.bass_utils import run_bass_kernel_spmd as _run

    nc = _bacc.Bacc("TRN2", target_bir_lowering=False, num_devices=1)
    arrays = {f"in_{n}": np.ascontiguousarray(inputs[n]) for n in IN_NAMES}
    arrays.update(constants())
    t = {n: nc.dram_tensor(n, a.shape, mybir.dt.from_np(a.dtype), kind="ExternalInput").ap() for n, a in arrays.items()}
    t = {n.removeprefix("in_"): a for n, a in t.items()}
    o = {n: nc.dram_tensor(f"out_{n}", s, F32, kind="ExternalOutput").ap() for n, s in OUTS}
    build(nc, t, o)
    r = _run(nc, [arrays], core_ids=[0])
    return tuple(r.results[0][f"out_{n}"] for n, _ in OUTS)
```
